# Optimizing a Trainium2 kernel written in Bass

```python
import jax, jax.numpy as jnp
from jax import lax
import numpy as np

D_MODEL = 1024
BATCH = 1
SEQ = 1024
DEPTH = 1
DEC_BATCH = 8
DEC_SEQ = 4
PAST_LEN = 8192
PAGE_SIZE = 128

CONV_WIDTH = D_MODEL // 2
CONV_GROUPS = 4
CONV_K = 3
DN_HEADS = 4
DN_HEAD_DIM = D_MODEL // 8
DN_WIDTH = DN_HEADS * DN_HEAD_DIM
DN_CONV_K = 4
DN_CHUNK = 64
PEER_HEADS = 8
PEER_NKEYS = 128
PEER_TOPK = 16
PEER_QDIM = 128
PEER_HALF = PEER_QDIM // 2
PEER_EXPERTS = PEER_NKEYS * PEER_NKEYS
PEER_BLOCK = 256
EPS = 1e-6

SPLIT_SIZES = (CONV_WIDTH, CONV_WIDTH, CONV_WIDTH, 3 * DN_WIDTH, DN_WIDTH, DN_HEADS, DN_HEADS, 2 * D_MODEL)
IN_WIDTH = 3 * CONV_WIDTH + 4 * DN_WIDTH + 2 * DN_HEADS + 2 * D_MODEL

kernel_name = "hybrid_conv_deltanet_peer_step"

def rmsnorm(x, g):
    xf = x.astype(jnp.float32)
    y = xf * lax.rsqrt(jnp.mean(xf * xf, axis=-1, keepdims=True) + EPS) * g.astype(jnp.float32)
    return y.astype(x.dtype)

def l2norm(x):
    return x * lax.rsqrt(jnp.sum(x * x, axis=-1, keepdims=True) + EPS)

def causal_conv(x, buf, w):
    T = x.shape[1]
    K = w.shape[0]
    xp = jnp.concatenate([buf.astype(x.dtype), x], axis=1)
    y = w[0] * xp[:, 0:T]
    for j in range(1, K):
        y = y + w[j] * xp[:, j:j + T]
    return y, xp[:, -(K - 1):]

def gated_delta_chunked(q, k, v, g, beta, s0):
    Bsz, T, H, dk = q.shape
    dv = v.shape[-1]
    C = DN_CHUNK
    n_chunks = -(-T // C)
    pad = n_chunks * C - T

    def prep(a):
        a = jnp.pad(a, [(0, 0), (0, pad)] + [(0, 0)] * (a.ndim - 2))
        a = a.reshape((Bsz, n_chunks, C) + a.shape[2:])
        return jnp.moveaxis(a, 3, 1)

    q, k, v, g, beta = prep(q), prep(k), prep(v), prep(g), prep(beta)
    G = jnp.cumsum(g, axis=-1)
    idx = jnp.arange(C)
    strict = idx[:, None] > idx[None, :]
    causal = idx[:, None] >= idx[None, :]
    diff = G[..., :, None] - G[..., None, :]
    decay = jnp.exp(jnp.where(causal, diff, -jnp.inf))
    kk = jnp.einsum('bhncd,bhnsd->bhncs', k, k)
    m = jnp.where(strict, kk * decay * beta[..., :, None], 0.0)
    a_mat = m + jnp.eye(C, dtype=m.dtype)
    rhs = jnp.concatenate([v * beta[..., None], k * (beta * jnp.exp(G))[..., None]], axis=-1)
    sol = lax.linalg.triangular_solve(a_mat, rhs, left_side=True, lower=True, unit_diagonal=True)
    u, w = sol[..., :dv], sol[..., dv:]
    qk = jnp.einsum('bhncd,bhnsd->bhncs', q, k) * decay
    q_dec = q * jnp.exp(G)[..., None]
    k_dec = k * jnp.exp(G[..., -1:] - G)[..., None]
    g_last = jnp.exp(G[..., -1])

    def step(S, xs):
        u_c, w_c, qk_c, qd_c, kd_c, gl_c = xs
        v_new = u_c - jnp.einsum('bhcd,bhde->bhce', w_c, S)
        o = jnp.einsum('bhcd,bhde->bhce', qd_c, S) + jnp.einsum('bhcs,bhse->bhce', qk_c, v_new)
        S = S * gl_c[..., None, None] + jnp.einsum('bhcd,bhce->bhde', kd_c, v_new)
        return S, o

    xs = tuple(jnp.moveaxis(a, 2, 0) for a in (u, w, qk, q_dec, k_dec, g_last))
    S, o = lax.scan(step, s0, xs)
    o = jnp.transpose(o, (1, 0, 3, 2, 4)).reshape(Bsz, n_chunks * C, H, dv)[:, :T]
    return o, S

def peer(xn, w_query, sub_keys, expert_u, expert_v):
    shape = xn.shape
    xf = xn.reshape(-1, D_MODEL)
    n = xf.shape[0]
    nb = -(-n // PEER_BLOCK)
    xf = jnp.pad(xf, ((0, nb * PEER_BLOCK - n), (0, 0))).reshape(nb, PEER_BLOCK, D_MODEL)

    def block(xb):
        q = (xb @ w_query).reshape(PEER_BLOCK, PEER_HEADS, 2, PEER_HALF)
        s = jnp.einsum('bhpd,phnd->bhpn', q, sub_keys).astype(jnp.float32)
        top_s, top_i = lax.top_k(s, PEER_TOPK)
        cand = top_s[:, :, 0, :, None] + top_s[:, :, 1, None, :]
        best_s, best_j = lax.top_k(cand.reshape(PEER_BLOCK, PEER_HEADS, PEER_TOPK * PEER_TOPK), PEER_TOPK)
        e1 = jnp.take_along_axis(top_i[:, :, 0, :], best_j // PEER_TOPK, axis=-1)
        e2 = jnp.take_along_axis(top_i[:, :, 1, :], best_j % PEER_TOPK, axis=-1)
        eid = e1 * PEER_NKEYS + e2
        gate = jax.nn.softmax(best_s, axis=-1)
        u_sel = expert_u[eid]
        act = jax.nn.gelu(jnp.einsum('bd,bhkd->bhk', xb, u_sel).astype(jnp.float32), approximate=False)
        v_sel = expert_v[eid]
        return jnp.einsum('bhk,bhkd->bd', (gate * act).astype(xb.dtype), v_sel)

    out = lax.map(block, xf)
    return out.reshape(-1, D_MODEL)[:n].reshape(shape)

def decoder_layer(x, buf_a, buf_qkv, s0, g_norm_mix, w_in, w_conv_a, w_conv_qkv, a_log, dt_bias,
                  g_dn_norm, w_out_a, w_out_dn, w_o, g_norm_ffn, w_query, sub_keys, expert_u, expert_v):
    Bsz, T, _ = x.shape
    xn = rmsnorm(x, g_norm_mix)
    proj = xn @ w_in
    offs = [int(o) for o in np.cumsum(SPLIT_SIZES)[:-1]]
    b_c, c_c, h_c, qkv, z, a_raw, b_raw, gates = jnp.split(proj, offs, axis=-1)

    conv_out, new_buf_a = causal_conv(c_c * h_c, buf_a, w_conv_a)
    y_a = (b_c * conv_out) @ w_out_a

    qkv_c, new_buf_qkv = causal_conv(qkv, buf_qkv, w_conv_qkv)
    qkv_c = jax.nn.silu(qkv_c).astype(jnp.float32)
    q, k, v = jnp.split(qkv_c, 3, axis=-1)
    q = l2norm(q.reshape(Bsz, T, DN_HEADS, DN_HEAD_DIM)) * (DN_HEAD_DIM ** -0.5)
    k = l2norm(k.reshape(Bsz, T, DN_HEADS, DN_HEAD_DIM))
    v = v.reshape(Bsz, T, DN_HEADS, DN_HEAD_DIM)
    g = -jnp.exp(a_log.astype(jnp.float32)) * jax.nn.softplus(a_raw.astype(jnp.float32) + dt_bias.astype(jnp.float32))
    beta = jax.nn.sigmoid(b_raw.astype(jnp.float32))
    o, s_new = gated_delta_chunked(q, k, v, g, beta, s0.astype(jnp.float32))
    zf = z.astype(jnp.float32).reshape(Bsz, T, DN_HEADS, DN_HEAD_DIM)
    o = o * lax.rsqrt(jnp.mean(o * o, axis=-1, keepdims=True) + EPS) * g_dn_norm.astype(jnp.float32) * jax.nn.silu(zf)
    y_b = o.reshape(Bsz, T, DN_WIDTH).astype(x.dtype) @ w_out_dn

    gate_a, gate_b = jnp.split(jax.nn.sigmoid(gates), 2, axis=-1)
    h = x + (gate_a * y_a + gate_b * y_b) @ w_o

    h = h + peer(rmsnorm(h, g_norm_ffn), w_query, sub_keys, expert_u, expert_v)
    return h, new_buf_a, new_buf_qkv, s_new.astype(x.dtype)

def trunk(x, bufs_a, bufs_qkv, states, weights, g_norm_final):
    new_a, new_qkv, new_s = [], [], []
    for l in range(DEPTH):
        x, a, c, s = decoder_layer(x, bufs_a[l], bufs_qkv[l], states[l], *[w[l] for w in weights])
        new_a.append(a)
        new_qkv.append(c)
        new_s.append(s)
    return rmsnorm(x, g_norm_final), jnp.stack(new_a), jnp.stack(new_qkv), jnp.stack(new_s)

def setup_inputs(seed: int = 0) -> dict:
    key = jax.random.key(seed)
    ks = jax.random.split(key, 24)
    f32 = jnp.float32
    nrm = lambda k, shp, s: jax.random.normal(k, shp, f32) * s
    return {
        "x_prompt": nrm(ks[0], (BATCH, SEQ, D_MODEL), 1.0),
        "x_sample": nrm(ks[1], (DEC_BATCH, DEC_SEQ, D_MODEL), 1.0),
        "state_conv_a": nrm(ks[2], (DEPTH, DEC_BATCH, CONV_K - 1, CONV_WIDTH), 1.0),
        "state_conv_qkv": nrm(ks[3], (DEPTH, DEC_BATCH, DN_CONV_K - 1, 3 * DN_WIDTH), 1.0),
        "state_delta": nrm(ks[4], (DEPTH, DEC_BATCH, DN_HEADS, DN_HEAD_DIM, DN_HEAD_DIM), 0.3),
        "g_norm_mix": 1.0 + nrm(ks[5], (DEPTH, D_MODEL), 0.02),
        "w_in": nrm(ks[6], (DEPTH, D_MODEL, IN_WIDTH), D_MODEL ** -0.5),
        "w_conv_a": nrm(ks[7], (DEPTH, CONV_K, CONV_WIDTH), CONV_K ** -0.5),
        "w_conv_qkv": nrm(ks[8], (DEPTH, DN_CONV_K, 3 * DN_WIDTH), DN_CONV_K ** -0.5),
        "a_log": jnp.log(jax.random.uniform(ks[9], (DEPTH, DN_HEADS), f32, 1.0, 16.0)),
        "dt_bias": nrm(ks[10], (DEPTH, DN_HEADS), 0.1),
        "g_dn_norm": 1.0 + nrm(ks[11], (DEPTH, DN_HEAD_DIM), 0.02),
        "w_out_a": nrm(ks[12], (DEPTH, CONV_WIDTH, D_MODEL), CONV_WIDTH ** -0.5),
        "w_out_dn": nrm(ks[13], (DEPTH, DN_WIDTH, D_MODEL), DN_WIDTH ** -0.5),
        "w_o": nrm(ks[14], (DEPTH, D_MODEL, D_MODEL), D_MODEL ** -0.5),
        "g_norm_ffn": 1.0 + nrm(ks[15], (DEPTH, D_MODEL), 0.02),
        "w_query": nrm(ks[16], (DEPTH, D_MODEL, PEER_HEADS * PEER_QDIM), D_MODEL ** -0.5),
        "sub_keys": nrm(ks[17], (DEPTH, 2, PEER_HEADS, PEER_NKEYS, PEER_HALF), PEER_HALF ** -0.5),
        "expert_u": nrm(ks[18], (DEPTH, PEER_EXPERTS, D_MODEL), D_MODEL ** -0.5),
        "expert_v": nrm(ks[19], (DEPTH, PEER_EXPERTS, D_MODEL), 0.5),
        "g_norm_final": 1.0 + nrm(ks[20], (D_MODEL,), 0.02),
    }

def reference(x_prompt, x_sample, state_conv_a, state_conv_qkv, state_delta, g_norm_mix, w_in,
              w_conv_a, w_conv_qkv, a_log, dt_bias, g_dn_norm, w_out_a, w_out_dn, w_o, g_norm_ffn,
              w_query, sub_keys, expert_u, expert_v, g_norm_final):
    weights = (g_norm_mix, w_in, w_conv_a, w_conv_qkv, a_log, dt_bias, g_dn_norm, w_out_a, w_out_dn,
               w_o, g_norm_ffn, w_query, sub_keys, expert_u, expert_v)
    bp = x_prompt.shape[0]
    dt = x_prompt.dtype
    zero_a = jnp.zeros((DEPTH, bp, CONV_K - 1, CONV_WIDTH), dt)
    zero_qkv = jnp.zeros((DEPTH, bp, DN_CONV_K - 1, 3 * DN_WIDTH), dt)
    zero_s = jnp.zeros((DEPTH, bp, DN_HEADS, DN_HEAD_DIM, DN_HEAD_DIM), dt)
    y_prompt, conv_a_p, conv_qkv_p, delta_p = trunk(x_prompt, zero_a, zero_qkv, zero_s, weights, g_norm_final)
    y_sample, conv_a_s, conv_qkv_s, delta_s = trunk(x_sample, state_conv_a, state_conv_qkv, state_delta,
                                                    weights, g_norm_final)
    return (y_prompt, y_sample, conv_a_p, conv_qkv_p, delta_p, conv_a_s, conv_qkv_s, delta_s)


_drawn_inputs = setup_inputs


def setup_inputs(seed=0):
    import zlib

    import numpy as np

    out = dict(_drawn_inputs(seed))
    spreads = {}
    factors = {'dt_bias': 2.712, 'g_dn_norm': 3.359, 'g_norm_final': 2.947}
    for name, (base, spread) in spreads.items():
        noise = np.random.default_rng([zlib.crc32(name.encode()), seed]).standard_normal(out[name].shape)
        drawn = base * np.exp(spread * noise) if base else spread * noise
        out[name] = __import__('jax').numpy.asarray(drawn.astype(out[name].dtype))
    for name, factor in factors.items():
        out[name] = (out[name] * factor).astype(out[name].dtype)
    return out
```

```python
from contextlib import ExitStack

import numpy as np

import concourse.bass as bass
from concourse import mybir

F32 = mybir.dt.float32
F32R = mybir.dt.float32r
BF16 = mybir.dt.bfloat16
U32 = mybir.dt.uint32
ALU = mybir.AluOpType
ACT = mybir.ActivationFunctionType
AX = mybir.AxisListType
ds = bass.ds

P = 128
D = 1024
KD = D // P
SEQ = 1024
NSEQ, SLEN = 8, 4
TS = NSEQ * SLEN
T = SEQ + TS
TH = T // 3
NT = SEQ // P
H = 4
NQ = 3 * H
EPS = 1e-6
NEG = -1e30
HP = 8
TOPK = 16
NKEYS = 128
PAIRS = HP * TOPK

CAND = [(0, 1, 16), (1, 1, 8), (2, 2, 5), (4, 4, 3), (8, 8, 1)]
ROW_LEN = [cols for _, rows, cols in CAND for _ in range(rows)]
ROW_START = [sum(ROW_LEN[:i]) for i in range(TOPK)]
NCAND = sum(ROW_LEN)

B_QKV, B_AB, B_Z, B_CONV, B_Y, B_O, B_WQ, NBLK = 0, 12, 13, 17, 29, 53, 61, 69

GE = 4
NG = NKEYS // GE
WT = 48
WS = 8
NWB = T // WT
S_MIX, S_FFN, S_FIN, S_CQ, S_CA, S_DN, S_ALOG, S_DT, NSMALL = 0, 8, 16, 24, 72, 84, 85, 86, 88
HQ, HA = 3, 2
PADQ, PADA = HQ + SEQ + NSEQ * (SLEN + HQ), HA + SEQ + NSEQ * (SLEN + HA)


def constants():
    i = np.arange(P)
    lo, hi = i[:, None], i[None, :]
    a, b = np.arange(TS)[:, None], np.arange(TS)[None, :]
    same = a // SLEN == b // SLEN

    def rows(x):
        return np.concatenate([x, np.zeros((P - TS, x.shape[1]))])

    def level(row, col, l):
        return (row >> (l + 1) == col >> (l + 1)) & (row >> l != col >> l) & (col > row)

    parts = {"ident": lo == hi, "ones": np.ones((P, P)), "upto": lo <= hi, "after": lo > hi,
             "neg": np.where(lo > hi, NEG, 0.0)}
    for l in range(7):
        parts[f"mask{l}"] = level(lo, hi, l)
    parts["upto_s"] = rows(same & (a <= b))
    parts["after_s"] = rows(same & (a > b))
    parts["neg_s"] = rows(np.where(same & (a <= b), 0.0, NEG))
    for l in range(2):
        parts[f"mask{l}_s"] = rows(level(a, b, l))
    seq = np.arange(TS)[None, :] // SLEN == np.arange(NSEQ)[:, None]
    parts["seqcol"] = np.tile(seq.reshape(1, -1), (P, 1))
    parts["seqrow"] = rows(seq.T)
    parts["sel"] = np.repeat(lo == np.arange(H)[None], P, axis=1)
    parts["iota16"] = np.tile(np.arange(TOPK)[None], (P, 1))
    parts["start16"] = np.tile(np.array(ROW_START)[None], (P, 1))
    at, where = 0, {}
    for name, x in parts.items():
        where[name] = (at, x.shape[1])
        at += x.shape[1]
    return np.concatenate([np.asarray(x, np.float32) for x in parts.values()], axis=1), where


CONSTANTS, CONST_AT = constants()
NCST = CONSTANTS.shape[1]


def unit_of(block):
    if block < B_Y:
        return block
    if block < B_O:
        j, r = divmod(block - B_Y, 3)
        return B_Y + 4 * j + (0, 1, 3)[r]
    return block + KD


def program(nc, xT, wall, small, keys, cst, histq, hista, s_in, u_blk, v_blk,
            yT, convq_out, conva_out, sp_out, ss_out, w_dram):
    with ExitStack() as ctx:
        def sem(name):
            return ctx.enter_context(nc.semaphore(name))

        BASE = -(-nc.sbuf_base // 64) * 64
        arena = ctx.enter_context(nc.sbuf_tensor("arena", [P, (229344 - BASE) // 4 - 8], F32))

        def at(off, name, shape, dt=F32):
            size = int(np.prod(shape[1:])) * (2 if dt == BF16 else 4)
            assert off % 4 == 0 and BASE + off + size <= 229344, (name, off, size)
            return nc.alloc_sbuf_tensor_at(name, list(shape), dt, offset=BASE + off, align_bytes=4)

        ROW = 4 * T
        XH = at(0, "XH", [P, KD, T], F32R)
        XL = at(8 * ROW, "XL", [P, KD, T], F32R)
        ring = 16 * ROW
        RAW = at(ring, "RAW", [P, 2, D])
        WH = at(ring + 8192, "WH", [P, 2, D], F32R)
        WL = at(ring + 16384, "WL", [P, 2, D], F32R)
        c0 = ring + 24576
        C = at(c0, "C", [P, NCST])
        SW = at(c0 + 4 * NCST, "SW", [P, NSMALL])
        gb_tok = at(c0 + 4 * NCST + 4 * NSMALL, "gb_tok", [P, NT + 1, 8])
        r1 = c0 + 4 * NCST + 4 * NSMALL + 288
        r2, r3, r4 = r1 + 8 * ROW, r1 + 16 * ROW, r1 + 24 * ROW

        HID = at(r1, "HID", [P, KD, T])
        sq = at(r3, "sq", [P, 2, T])
        rn = at(r3 + 2 * ROW, "rn", [P, T])
        xt = at(r3 + 3 * ROW, "xt", [P, 2, T])
        QKV = at(r2, "QKV", [P, NQ, T])
        pad = at(r1, "pad", [P, 2, PADQ])
        cy = at(r1 + 8 * PADQ, "cy", [P, 2, PADQ])
        hist = at(r1 + 16 * PADQ, "hist", [P, NQ, NSEQ, HQ])
        new_q = at(r1 + 16 * PADQ + 4 * NQ * 24, "new_q", [P, NQ, NSEQ + 1, HQ])
        ab = at(r3 + 4 * ROW, "ab", [H, 4, T])
        betaT = at(r4, "betaT", [H, T])
        sq2 = at(r1, "sq2", [P, 2, T])
        rn2 = at(r1 + 2 * ROW, "rn2", [P, 2, T])
        DN1 = at(r1, "DN1", [P, 16, 512])
        DN2 = at(r3 + 4 * ROW, "DN2", [P, 8, 512])
        S = at(r4 + ROW, "S", [P, H, P])
        SS = at(r3 + 4 * ROW, "SS", [P, NSEQ, H, P])
        kbgm = at(r1 + 12 * 2048, "kbgm", [P, H, NSEQ, TS])
        qdm = at(r1 + 14 * 2048, "qdm", [P, H, NSEQ, TS])
        gbt = at(r4 + ROW + 2112, "gbt", [P, 2, 8])
        gsc = at(r4 + ROW + 2048, "gsc", [P, 2, 4])
        ekd = at(r4 + ROW + 2080, "ekd", [P, 2, 4])
        zs = at(r1, "zs", [P, 2, T])
        on = at(r1 + 2 * ROW, "on", [P, 2, T])
        OH = at(r3, "OH", [P, H, T], F32R)
        OL = at(r3 + 4 * ROW, "OL", [P, H, T], F32R)
        BH = at(r2, "BH", [P, H, T], F32R)
        BL = at(r2 + 4 * ROW, "BL", [P, H, T], F32R)
        cbuf = at(r1 + 4 * ROW, "cbuf", [P, T])
        pada = at(r1 + 5 * ROW, "pada", [P, PADA])
        ya = at(r1 + 5 * ROW + 4 * PADA, "ya", [P, PADA])
        bc = at(r4, "bc", [P, T])
        hist_a = at(r4 + ROW, "hist_a", [P, H, NSEQ, HA])
        new_a = at(r4 + ROW + 256, "new_a", [P, H, NSEQ + 1, HA])
        sig = at(r4, "sig", [P, 2, T])
        xr = at(r3, "xr", [P, 2, T])
        QT = at(r2, "QT", [P, HP, T])
        EG = at(ring, "EG", [P, 5, T], BF16)
        KEYS = at(r3, "KEYS", [P, HP, 2 * NKEYS])
        qst = at(r3 + 8192, "qst", [P, HP, P])
        sc = at(ring + 10 * T, "sc", [P, 2 * HP, NKEYS])
        sc2 = at(r3 + 12288, "sc2", [P, 2 * HP, NKEYS])
        hot = at(r3 + 20480, "hot", [P, HP, TOPK, TOPK], BF16)
        pick = at(r3 + 24576, "pick", [P, HP, TOPK, TOPK], BF16)
        cand = at(r3 + 28672, "cand", [P, HP, NCAND])
        cand2 = at(r3 + 28672 + 32 * NCAND, "cand2", [P, HP, NCAND])
        o = [r4]

        def small_at(name, shape, dt=F32):
            t = at(o[0], name, shape, dt)
            o[0] += int(np.prod(shape[1:])) * (2 if dt == BF16 else 4)
            return t

        best = small_at("best", [P, 2 * HP, TOPK])
        besti = small_at("besti", [P, 2 * HP, TOPK], U32)
        bestf = small_at("bestf", [P, 2 * HP, TOPK], BF16)
        delta = small_at("delta", [P, HP, TOPK], BF16)
        top = small_at("top", [P, HP, TOPK])
        topi = small_at("topi", [P, HP, TOPK], U32)
        topf = small_at("topf", [P, HP, TOPK])
        e1 = small_at("e1", [P, PAIRS])
        e2 = small_at("e2", [P, PAIRS])
        gate = small_at("gate", [P, PAIRS])
        gsum = small_at("gsum", [P, HP])
        iota_b = small_at("iota_b", [P, TOPK], BF16)
        dstart = small_at("dstart", [P, TOPK], BF16)
        tick = small_at("tick", [P, 1])
        gres = small_at("gres", [P, P])
        stg = at(r2, "stg", [P, 2, NKEYS // 2, WT, 2])
        oh0 = r2 + 2 * 512 * WT
        IOTA = at(oh0, "IOTA", [P, NKEYS, WS], BF16)
        HOT1 = at(oh0 + 2048, "HOT1", [P, 2, NKEYS, WS], BF16)
        HOT2 = at(oh0 + 6144, "HOT2", [P, 2, NKEYS, WS], BF16)
        HOTG = at(oh0 + 10240, "HOTG", [P, 2, 3, NKEYS, WS], BF16)
        AH = at(r2, "AH", [P, GE + 1, T], F32R)
        AL = at(r2 + 5 * ROW, "AL", [P, GE + 1, T], F32R)
        AF = at(r2 + 5 * ROW, "AF", [P, GE + 1, T])
        VRAW = at(r2 + 10 * ROW, "VRAW", [P, 4, GE * P])
        VH = at(r2 + 10 * ROW + 8192, "VH", [P, 2, GE * P], F32R)
        VL = at(r2 + 10 * ROW + 12288, "VL", [P, 2, GE * P], F32R)
        GW = at(r2 + 10 * ROW + 16384, "GW", [P, 2, T, 2])

        PS = ctx.enter_context(nc.psum_tensor("PS", [P, 8, 512], F32))

        def const(name, rows=P):
            a, n = CONST_AT[name]
            return C[0:rows, a:a + n]

        def thirds(ap):
            return ap.rearrange("p (a b) -> p a b", a=3)

        def pset(s, rows=P):
            return PS[0:rows, 3 * s:3 * s + 3, 0:TH]

        in_c, in_x, in_w = sem("in_c"), sem("in_x"), sem("in_w")
        raw_in = [sem("raw_in0"), sem("raw_in1")]
        hi_done, lo_done, unit_done = sem("hi_done"), sem("lo_done"), sem("unit_done")

        def filled(u):
            return u + 2

        block = ctx.enter_context(nc.Block())

        def split_hi(act, n, slot, reads, before):
            act.wait_ge(raw_in[slot], reads)
            if before is not None:
                act.wait_ge(unit_done, before)
            act.activation(WH[:, slot, :], RAW[:, slot, :], ACT.Copy).then_inc(hi_done, 1)

        def split_lo(dve, count, slot):
            dve.wait_ge(hi_done, count)
            dve.tensor_tensor(WL[:, slot, :], RAW[:, slot, :], WH[:, slot, :].bitcast(F32),
                              ALU.subtract).then_inc(lo_done, 1)

        def products(pe, slot, s, xh, xl, chunks=range(KD), base=0):
            ks = list(chunks)
            for k in ks:
                cols = slice(k * P, k * P + P)
                for n, (w, x) in enumerate(((WH, xh), (WH, xl), (WL, xh))):
                    for t in range(3):
                        mm = pe.matmul(PS[:, 3 * s + t, 0:TH], w[:, slot, cols],
                                       x[:, k - base, t * TH:t * TH + TH],
                                       start=(k == ks[0] and n == 0), stop=(k == ks[-1] and n == 2))
            return mm

        rms_sems = {n: {k: sem(f"{n}_{k}") for k in ("sq", "mm", "rn", "ln")} for n in ("na", "nb", "nc")}

        def rms_act(act, src, r):
            for k in range(KD):
                if k >= 2:
                    act.wait_ge(r["mm"], k - 1)
                act.activation(sq[:, k % 2, :], src[:, k, :], ACT.Square).then_inc(r["sq"], 1)
            act.wait_ge(r["mm"], KD)
            act.activation(thirds(rn[:, :]), pset(0), ACT.Ln, scale=1.0 / D, bias=EPS).then_inc(r["ln"], 1)
            act.wait_ge(r["ln"], 1)
            act.activation(rn[:, :], rn[:, :], ACT.Exp, scale=-0.5).then_inc(r["rn"], 1)

        def rms_pe(pe, r):
            for k in range(KD):
                pe.wait_ge(r["sq"], k + 1)
                for t in range(3):
                    mm = pe.matmul(PS[:, t, 0:TH], const("ones"), sq[:, k % 2, t * TH:t * TH + TH],
                                   start=k == 0, stop=k == KD - 1)
                mm.then_inc(r["mm"], 1)

        xt_done, xh_done, xl_done = sem("xt_done"), sem("xh_done"), sem("xl_done")

        def norm_act(act, base):
            for k in range(KD):
                act.wait_ge(xt_done, base + k + 1)
                act.activation(XH[:, k, :], xt[:, k % 2, :], ACT.Copy).then_inc(xh_done, 1)

        hist_in, hist_a_in, state_in = sem("hist_in"), sem("hist_a_in"), sem("state_in")
        free_q, evac_q, hist_set, conv_q, silu_q, newq_set = (sem(n) for n in (
            "free_q", "evac_q", "hist_set", "conv_q", "silu_q", "newq_set"))
        out_q, out_a, out_s = sem("out_q"), sem("out_a"), sem("out_s")
        out_y = [sem("out_y0"), sem("out_y1")]
        ab_a, ab_v, ab_p, ab_t = sem("ab_a"), sem("ab_v"), sem("ab_p"), sem("ab_t")
        l2_sq, l2_mm, l2_ln, l2_rn, l2_done = (sem(n) for n in ("l2_sq", "l2_mm", "l2_ln", "l2_rn", "l2_done"))
        zeroed = sem("zeroed")
        dn_in, dn_bc, dn_b, dn_dt, dn_eg, dn_d, dn_e, dn_f, dn_g, dn_bt, dn_x, dn_xs, dn_tt, dn_t = (sem(f"dn_{n}") for n in (
            "in", "bc", "b", "dt", "eg", "d", "e", "f", "g", "bt", "x", "xs", "tt", "t"))
        dn_ks, dn_r, dn_v, dn_vs, dn_o, dn_os, dn_ds, dn_st = (sem(f"dn_{n}") for n in (
            "ks", "r", "v", "vs", "o", "os", "ds", "st"))
        dn_m, dn_vm = sem("dn_m"), sem("dn_vm")
        free_c, silu_z, on_done, oh_h, c_hist, bc_done, bh_done, bl_done = (sem(n) for n in (
            "free_c", "silu_z", "on_done", "oh_h", "c_hist", "bc_done", "bh_done", "bl_done"))
        ol_done = sem("ol_done")
        ya_done, newa_set = sem("ya_done"), sem("newa_set")
        sig_done, y_read, m_done, mh_done, ml_done = (sem(n) for n in ("sig_done", "y_read", "m_done", "mh_done", "ml_done"))
        xr_in = [sem("xr_in0"), sem("xr_in1")]
        free_h, free_w = sem("free_h"), sem("free_w")
        keys_in, sel_q, sel_mm, sel_sc, sel_read, sel_b, sel_e, sel_g, sel_t, sel_done = (sem(f"sel_{n}") for n in (
            "keys", "q", "mm", "sc", "read", "b", "e", "g", "t", "done"))
        iota_set = sem("iota_set")
        w_hot, w_mm, w_evac = sem("w_hot"), sem("w_mm"), sem("w_evac")
        w_out = [sem("w_out0"), sem("w_out1")]
        u_in, gw_in = [sem("u_in0"), sem("u_in1")], [sem("gw_in0"), sem("gw_in1")]
        v_in = [sem(f"v_in{k}") for k in range(4)]
        u_hi, u_lo, u_mm, a_gelu, a_mul, a_hi, a_lo = (sem(n) for n in (
            "u_hi", "u_lo", "u_mm", "a_gelu", "a_mul", "a_hi", "a_lo"))
        v_hi, v_lo, v_mm, acc_done = (sem(n) for n in ("v_hi", "v_lo", "v_mm", "acc_done"))
        y_row = sem("y_row")


        def dn(u, k):
            if u == 0:
                return DN1[:, k, :]
            return DN1[:, 12 + k, :] if k < 4 else DN2[:, k - 4, :]

        def dnh(u, k, w=P, rows=P):
            return dn(u, k)[0:rows, 0:H * w].rearrange("p (h c) -> p h c", h=H)

        def bank(b, w=P, rows=P):
            return PS[0:rows, b, 0:H * w].rearrange("p (h c) -> p h c", h=H)

        def seqs(buf, base, k, first, n):
            return buf[:, base:base + NSEQ * (SLEN + k)].rearrange(
                "p (s c) -> p s c", s=NSEQ)[:, :, first:first + n]

        KST, VST, GBC, DIFF, DT, EXPG, KB, KBG, QD, MT, QKT, KDEC = range(12)
        X, VN, TM, BT, RES, TTR, VB = VST, VST, GBC, DIFF, DIFF, DT, KB
        NPAIR = NT // 2
        LEVELS = 7
        LEVELS_S = 2

        @block.sync
        def _(sp):
            sp.dma_start(C[:, :], cst).then_inc(in_c, 16)
            sp.dma_start(SW[:, :], small).then_inc(in_w, 16)
            sp.dma_start(HID[:, :, :], xT).then_inc(in_x, 16)
            for n in range(2):
                sp.dma_start(RAW[:, n, :], wall[n]).then_inc(raw_in[n], 16)
            with sp.Fori(0, (NBLK - 3) // 2) as i:
                for r in range(2):
                    sp.wait_ge(lo_done, 2 * i + (r + 1))
                    sp.dma_start(RAW[:, r, :], wall[ds(2 * i + (r + 2), 1)].rearrange("n p c -> (n p) c")
                                 ).then_inc(raw_in[r], 16)
            sp.wait_ge(lo_done, NBLK - 2)
            sp.dma_start(RAW[:, 0, :], wall[NBLK - 1]).then_inc(raw_in[0], 16)
            for b in range(2):
                sp.sem_inc(w_out[b], 16)
            with sp.Fori(0, NWB // 2) as i:
                for b in range(2):
                    sp.wait_ge(w_evac, 12 * i + (6 * b + 9))
                    sp.dma_start(w_dram[:, :, ds(2 * WT * i + WT * b, WT), :].rearrange("q p t j -> p q (t j)"),
                                 stg[:, b, :, :, :].rearrange("p q t j -> p q (t j)")).then_inc(w_out[b], 16)
            for b in range(2):
                sp.wait_ge(w_out[b], 16 * (NWB // 2 + 1))

            def load_u(src, slot):
                sp.dma_start(RAW[:, slot, :], src).then_inc(u_in[slot], 16)

            def load_w(src, slot):
                sp.dma_start(GW[:, slot, :, :].rearrange("p t j -> p (t j)"), src).then_inc(gw_in[slot], 16)

            for n in range(2):
                load_u(u_blk[n], n)
                load_w(w_dram[n].rearrange("p t j -> p (t j)"), n)
            with sp.Fori(0, NKEYS // 4 - 1) as i:
                for r in range(2):
                    for v in range(2):
                        sp.wait_ge(u_lo, 4 * i + (2 * r + v + 1))
                        load_u(u_blk[ds(4 * i + (2 * r + v + 2), 1)].rearrange("n p c -> (n p) c"), v)
                    sp.wait_ge(a_mul, 4 * i + (2 * r + 2))
                    load_w(w_dram[ds(2 * i + (r + 2), 1)].rearrange("n p t j -> (n p) (t j)"), r)
            for v in range(2):
                sp.wait_ge(u_lo, NKEYS - 4 + v + 1)
                load_u(u_blk[NKEYS - 2 + v], v)
            for k in range(KD):
                sp.wait_ge(y_row, k + 1)
                sp.dma_start(yT[:, k, :], xt[:, k % 2, :]).then_inc(out_y[k % 2], 16)
            for b in range(2):
                sp.wait_ge(out_y[b], 16 * (KD // 2))

        @block.gpsimd
        def _(pool):
            pool.wait_ge(xl_done, KD)
            pool.dma_start(hist[:, :, :, :], histq).then_inc(hist_in, 16)
            pool.memset(pad[:, :, 0:HQ], 0.0).then_inc(zeroed, 1)
            pool.drain().then_inc(newq_set, 2)
            pool.wait_ge(hist_in, 16)

            with pool.Fori(0, NQ // 2) as i:
                for r in range(2):
                    pool.drain()
                    pool.wait_ge(conv_q, 2 * i + (r + 1))
                    pool.tensor_copy(seqs(pad[:, r, :], HQ + SEQ, HQ, 0, HQ),
                                     hist[:, ds(2 * i + r, 1), :, :].rearrange("p n s c -> p (n s) c")
                                     ).then_inc(hist_set, 1)
                    pool.wait_ge(evac_q, 2 * i + (r + 1))
                    pool.tensor_copy(new_q[:, ds(2 * i + r, 1), 0, :].rearrange("p n c -> p (n c)"),
                                     pad[:, r, SEQ:SEQ + HQ])
                    pool.tensor_copy(new_q[:, ds(2 * i + r, 1), 1:NSEQ + 1, :].rearrange("p n s c -> p (n s) c"),
                                     seqs(pad[:, r, :], HQ + SEQ, HQ, SLEN, HQ)).then_inc(newq_set, 1)
            pool.wait_ge(newq_set, NQ + 2)
            pool.dma_start(convq_out, new_q[:, :, :, :]).then_inc(out_q, 16)
            pool.wait_ge(dn_st, NT + 1)
            pool.dma_start(sp_out, S[:, :, :]).then_inc(out_s, 16)
            pool.dma_start(SS[:, :, :, :], s_in).then_inc(state_in, 16)
            pool.wait_ge(dn_st, NT + 1 + NSEQ)
            pool.dma_start(ss_out, SS[:, :, :, :]).then_inc(out_s, 16)
            pool.wait_ge(out_s, 32)
            pool.wait_ge(out_q, 16)
            pool.dma_start(hist_a[:, :, :, :], hista).then_inc(hist_a_in, 16)
            pool.wait_ge(l2_done, 3 * H)
            pool.memset(pada[:, 0:HA], 0.0)
            pool.wait_ge(hist_a_in, 16)
            for i in range(H):
                if i:
                    pool.wait_ge(ya_done, i)
                    pool.drain()
                pool.tensor_copy(seqs(pada, HA + SEQ, HA, 0, HA), hist_a[:, i, :, :]).then_inc(c_hist, 1)
                pool.wait_ge(ya_done, i + 1)
                pool.tensor_copy(new_a[:, i, 0, :], pada[:, SEQ:SEQ + HA])
                pool.tensor_copy(new_a[:, i, 1:NSEQ + 1, :], seqs(pada, HA + SEQ, HA, SLEN, HA)).then_inc(newa_set, 1)
            pool.wait_ge(newa_set, H)
            pool.dma_start(conva_out, new_a[:, :, :, :]).then_inc(out_a, 16)
            pool.wait_ge(unit_done, filled(unit_of(B_O - 1)))
            for j in range(KD):
                if j >= 2:
                    pool.wait_ge(free_h, j + 1)
                pool.dma_start(xr[:, j % 2, :], xT[:, j, :]).then_inc(xr_in[j % 2], 16)
            pool.wait_ge(xl_done, 2 * KD)
            pool.dma_start(KEYS[:, :, :], keys).then_inc(keys_in, 16)
            pool.iota(iota_b[:, :], pattern=[[1, TOPK]], base=0, channel_multiplier=0,
                      allow_small_or_imprecise_dtypes=True).then_inc(iota_set, 1)
            pool.wait_ge(sel_done, NT + 1)
            pool.iota(IOTA[:, :, :], pattern=[[1, NKEYS], [0, WS]], base=0, channel_multiplier=0,
                      allow_small_or_imprecise_dtypes=True).then_inc(iota_set, 1)
            for b in range(2):
                pool.wait_ge(w_out[b], 16 * (NWB // 2 + 1))
            for s in range(4):
                pool.dma_start(VRAW[:, s, :], v_blk[s]).then_inc(v_in[s], 16)
            with pool.Fori(0, 2 * NG - 1) as i:
                for s in range(4):
                    pool.wait_ge(v_lo, 4 * i + (s + 1))
                    pool.dma_start(VRAW[:, s, :], v_blk[ds(4 * i + (4 + s), 1)].rearrange("n p c -> (n p) c")
                                   ).then_inc(v_in[s], 16)
            pool.wait_ge(out_a, 16)

        @block.scalar
        def _(act):
            act.wait_ge(in_x, 16)
            rms_act(act, HID, rms_sems["na"])
            norm_act(act, 0)
            split_hi(act, 0, 0, 16, None)
            act.drain().then_inc(free_q, 2)
            act.drain().then_inc(silu_q, 2)
            with act.Fori(0, NQ // 2) as i:
                for r in range(2):
                    split_hi(act, None, 1 - r, 16 * i + (16 + 16 * r), 2 * i + (r + 1))
                    act.wait_ge(newq_set, 2 * i + (r + 1))
                    act.wait_ge(unit_done, 2 * i + (r + 2))
                    act.activation(pad[:, r, HQ:HQ + 2 * TH].rearrange("p (a b) -> p a b", a=2),
                                   PS[:, 3 * r:3 * r + 2, 0:TH], ACT.Copy)
                    act.activation(pad[:, r, HQ + 2 * TH:HQ + SEQ], PS[:, 3 * r + 2, 0:SEQ - 2 * TH], ACT.Copy)
                    act.activation(
                        pad[:, r, HQ + SEQ:PADQ].rearrange("p (s c) -> p s c", s=NSEQ)[:, :, HQ:HQ + SLEN],
                        PS[:, 3 * r + 2, SEQ - 2 * TH:TH].rearrange("p (s c) -> p s c", s=NSEQ), ACT.Copy
                    ).then_inc(evac_q, 1)
                    act.drain().then_inc(free_q, 1)
                    act.wait_ge(conv_q, 2 * i + (r + 3))
                    act.activation(QKV[:, ds(2 * i + r, 1), 0:SEQ].rearrange("p n t -> p (n t)"),
                                   cy[:, r, 0:SEQ], ACT.Silu)
                    act.activation(QKV[:, ds(2 * i + r, 1), SEQ:T].rearrange("p n (s c) -> p (n s) c", s=NSEQ),
                                   seqs(cy[:, r, :], HQ + SEQ, HQ, 0, SLEN), ACT.Silu).then_inc(silu_q, 1)
            split_hi(act, B_AB + 1, 1, 16 * 7, filled(B_AB - 1))
            act.wait_ge(in_w, 16)
            act.wait_ge(unit_done, filled(B_AB))
            act.activation(thirds(ab[:, 0, :]), pset(0, H), ACT.Abs, bias=SW[0:H, S_DT:S_DT + 1])
            act.activation(thirds(ab[:, 1, :]), pset(0, H), ACT.Relu, bias=SW[0:H, S_DT:S_DT + 1])
            act.activation(thirds(betaT[:, :]), PS[32:32 + H, 0:3, 0:TH], ACT.Sigmoid)
            act.drain()
            act.activation(ab[:, 2, :], ab[:, 0, :], ACT.Exp, scale=-1.0)
            act.activation(gsc[0:H, 0, 0:1], SW[0:H, S_ALOG:S_ALOG + 1], ACT.Exp)
            act.drain()
            act.activation(ab[:, 2, :], ab[:, 2, :], ACT.Ln, bias=1.0).then_inc(ab_a, 1)
            act.drain().then_inc(free_q, 1)

            def norms(first, last, src, scale):
                for c in range(first, last):
                    if c >= 2:
                        act.wait_ge(l2_mm, c - 1)
                    act.activation(sq2[:, c % 2, :], QKV[:, src(c), :], ACT.Square).then_inc(l2_sq, 1)
                    if c > first:
                        factors(c - 1, scale)
                factors(last - 1, scale)

            def factors(c, scale):
                act.wait_ge(l2_mm, c + 1)
                if c >= 2:
                    act.wait_ge(l2_done, c - 1)
                act.activation(thirds(rn2[:, c % 2, :]), pset(c % 2), ACT.Ln, scale=scale, bias=EPS).then_inc(l2_ln, 1)
                act.drain()
                act.activation(rn2[:, c % 2, :], rn2[:, c % 2, :], ACT.Exp, scale=-0.5).then_inc(l2_rn, 1)

            act.wait_ge(newq_set, NQ + 2)
            norms(0, 2 * H, lambda c: c, 1.0)

            def dn_exps(u, n, w):
                act.wait_ge(dn_dt, n)
                act.activation(dnh(u, EXPG, w), bank(3 * u, w), ACT.Exp)
                act.activation(ekd[0:w, u, :], PS[0:w, 3 * u + 2, H:2 * H], ACT.Exp)
                act.activation(dnh(u, DT, w, w), dnh(u, DIFF, w, w), ACT.Exp).then_inc(dn_eg, 1)

            def dn_scaled(u, n, w):
                act.wait_ge(dn_e, n)
                for h in range(H):
                    act.activation(dnh(u, VB, P, w)[:, h, :], PS[0:w, 3 * u, h * P:h * P + P], ACT.Copy,
                                   scale=gbt[0:w, u, H + h:H + h + 1])
                    ins = act.activation(dnh(u, KDEC, P, w)[:, h, :], PS[0:w, 6 + u, h * P:h * P + P], ACT.Copy,
                                         scale=ekd[0:w, u, h:h + 1])
                ins.then_inc(dn_g, 1)

            def dn_evac_x(u, n, w):
                act.wait_ge(dn_x, n)
                act.activation(dnh(u, X, w, w), bank(3 * u, w, w), ACT.Copy).then_inc(dn_xs, 1)

            def dn_evac_v(u, n, w):
                act.wait_ge(dn_v, n)
                act.activation(dnh(u, VN, P, w), bank(7, P, w), ACT.Copy).then_inc(dn_vs, 1)

            def dn_evac_o(u, n, w, cols):
                act.wait_ge(dn_o, n)
                act.activation(QKV[:, 0:H, cols], bank(3 * u, w), ACT.Copy).then_inc(dn_os, 1)

            act.drain().then_inc(dn_os, 2)
            with act.Fori(0, NPAIR) as i:
                for u in range(2):
                    dn_exps(u, 2 * i + (u + 1), P)
                for u in range(2):
                    dn_scaled(u, 2 * i + (u + 1), P)
                for l in range(LEVELS):
                    for u in range(2):
                        dn_evac_x(u, 2 * LEVELS * i + (2 * l + u + 1), P)
                for u in range(2):
                    dn_evac_v(u, 2 * i + (u + 1), P)
                    dn_evac_o(u, 2 * i + (u + 1), P, ds(2 * P * i + P * u, P))
            dn_exps(0, NT + 1, TS)
            dn_scaled(0, NT + 1, TS)
            for l in range(LEVELS_S):
                dn_evac_x(0, NT * LEVELS + l + 1, TS)
            dn_evac_v(0, NT + 1, TS)
            dn_evac_o(0, NT + 1, TS, slice(SEQ, T))
            act.drain()
            act.wait_ge(dn_st, NT + 1 + NSEQ)

            norms(2 * H, 3 * H, lambda c: c - 2 * H, 1.0 / P)
            for h in range(H):
                n = B_Z + h
                split_hi(act, n + 1, (n + 1) % 2, 16 * ((n + 1) // 2 + 1), filled(n - 1))
                act.wait_ge(unit_done, filled(n))
                if h >= 2:
                    act.wait_ge(on_done, h - 1)
                if h == 0:
                    act.wait_ge(l2_done, 3 * H)
                act.activation(thirds(zs[:, h % 2, :]), pset(n % 2), ACT.Silu).then_inc(silu_z, 1)
                act.wait_ge(on_done, h + 1)
                act.activation(OH[:, h, :], on[:, h % 2, :], ACT.Copy).then_inc(oh_h, 1)
            for i in range(H):
                for r in range(3):
                    n = B_CONV + 3 * i + r
                    split_hi(act, n + 1, (n + 1) % 2, 16 * ((n + 1) // 2 + 1), filled(n - 1))
                act.wait_ge(bc_done, i + 1)
                act.activation(BH[:, i, :], bc[:, :], ACT.Copy).then_inc(bh_done, 1)
            act.wait_ge(out_a, 16)
            act.wait_ge(bl_done, H)
            with act.Fori(0, KD // 2) as i:
                for q in range(2):
                    for r in range(3):
                        nxt = B_Y + 3 * q + r + 1
                        split_hi(act, None, nxt % 2, 48 * i + 16 * (nxt // 2 + 1),
                                 8 * i + filled(B_Y + 4 * q + (-1, 0, 1)[r]))
                        if r < 2:
                            if r == 0:
                                act.wait_ge(m_done, 2 * i + (q + 1))
                            act.wait_ge(unit_done, 8 * i + filled(B_Y + 4 * q + r))
                            act.activation(thirds(sig[:, r, :]), pset(1 - r), ACT.Sigmoid).then_inc(sig_done, 1)
            act.wait_ge(m_done, KD + 1)
            act.wait_ge(unit_done, filled(unit_of(B_O - 1)))
            for k in range(KD):
                act.activation(XH[:, k, :], HID[:, k, :], ACT.Copy).then_inc(mh_done, 1)
            with act.Fori(0, KD // 2) as i:
                for r in range(2):
                    nxt = B_O + r + 1
                    split_hi(act, None, nxt % 2, 16 * i + 16 * (nxt // 2 + 1),
                             2 * i + filled(unit_of(B_O) + r - 1))
            act.wait_ge(free_h, KD + 2)
            rms_act(act, HID, rms_sems["nb"])
            norm_act(act, KD)
            act.drain().then_inc(free_w, 2)
            for j in range(HP):
                n = B_WQ + j
                if n + 1 < NBLK:
                    split_hi(act, n + 1, (n + 1) % 2, 16 * ((n + 1) // 2 + 1), filled(unit_of(n - 1)))
                act.wait_ge(unit_done, filled(unit_of(n)))
                act.activation(thirds(QT[:, j, :]), pset(n % 2), ACT.Copy).then_inc(free_w, 1)

            def sel_act(cols, w, n):
                act.wait_ge(sel_mm, n)
                act.activation(qst[:, :, 0:w], QT[:, :, cols], ACT.Copy).then_inc(sel_q, 1)
                act.wait_ge(sel_read, n)
                act.wait_ge(sel_mm, n + 1)
                act.activation(sc[0:w, :, :].rearrange("p (b n) k -> p b (n k)", b=4), PS[0:w, 0:4, :],
                               ACT.Copy).then_inc(sel_sc, 1)
                act.wait_ge(sel_b, n)
                act.activation(gate[0:w, :], gate[0:w, :], ACT.Exp).then_inc(sel_e, 1)

            act.drain()
            with act.Fori(0, NT) as i:
                sel_act(ds(i * P, P), P, i + 1)
            sel_act(slice(SEQ, T), TS, NT + 1)

            act.drain().then_inc(w_evac, 3)
            with act.Fori(0, NWB // 2) as i:
                for b in range(2):
                    act.wait_ge(w_out[b], 16 * i + 16)
                    for s in range(WT // WS):
                        act.wait_ge(w_mm, 12 * i + (6 * b + s + 3))
                        act.activation(stg[:, b, :, s * WS:s * WS + WS, :].rearrange("p q t j -> p t q j"),
                                       PS[:, 2 * (s % 3):2 * (s % 3) + 2, :].rearrange(
                                           "p b (t q j) -> p (b t) q j", t=4, j=2), ACT.Copy).then_inc(w_evac, 1)

            def u_split(slot, count, before, reads):
                act.wait_ge(u_in[slot], reads)
                if before is not None:
                    act.wait_ge(u_mm, before)
                act.activation(WH[:, slot, :], RAW[:, slot, :], ACT.Copy).then_inc(u_hi, 1)

            def gelu_of(m, slot, s, freed):
                act.wait_ge(u_mm, m)
                act.wait_ge(v_mm, freed)
                act.activation(thirds(AF[:, slot, :]), pset(s), ACT.Gelu).then_inc(a_gelu, 1)
                act.wait_ge(a_mul, m)
                act.activation(AH[:, slot, :], AF[:, slot, :], ACT.Copy).then_inc(a_hi, 1)

            def v_split(d, reads, before):
                act.wait_ge(v_in[d % 4], reads)
                act.wait_ge(v_mm, before)
                act.activation(VH[:, d % 2, :], VRAW[:, d % 4, :], ACT.Copy).then_inc(v_hi, 1)

            u_split(0, 1, None, 16)
            u_split(1, 2, None, 16)
            gelu_of(1, 0, 0, 2)

            def group_act(i, q, last):
                g8, g4 = 16 * i + 8 * q, 8 * i + 4 * q
                for c in range(1, 5):
                    if last and c == 4:
                        continue
                    if not (last and c == 3):
                        u_split((c + 1) % 2, None, g4 + c, 64 * i + 32 * q + 16 * ((c + 1) // 2 + 1))
                    if c == 3:
                        for d in range(2):
                            v_split(d, 64 * i + 32 * q + 16, g8 + d + 1)
                    gelu_of(g4 + c + 1, c if c < 4 else 4 * ((q + 1) % 2), c % 2, g8 + 2)
                for d in range(6):
                    v_split(d + 2, 64 * i + 32 * q + 16 * ((d + 2) // 4 + 1), g8 + d + 3)

            with act.Fori(0, NG // 2 - 1) as i:
                for q in range(2):
                    group_act(i, q, False)
            group_act(NG // 2 - 1, 0, False)
            group_act(NG // 2 - 1, 1, True)
            act.wait_ge(acc_done, 8 * NG + 2)
            rms_act(act, HID, rms_sems["nc"])

        @block.tensor
        def _(pe):
            pe.drain().then_inc(unit_done, 1)
            pe.wait_ge(in_c, 16)
            rms_pe(pe, rms_sems["na"])
            pe.wait_ge(xl_done, KD)
            pe.wait_ge(rms_sems["na"]["rn"], 1)
            with pe.Fori(0, NQ // 2) as i:
                for r in range(2):
                    pe.wait_ge(lo_done, 2 * i + (r + 1))
                    pe.wait_ge(free_q, 2 * i + (r + 1))
                    products(pe, r, r, XH, XL).then_inc(unit_done, 1)
            pe.wait_ge(lo_done, B_AB + 1)
            pe.wait_ge(free_q, B_AB + 1)
            products(pe, 0, 0, XH, XL).then_inc(unit_done, 1)
            pe.wait_ge(ab_v, 1)
            for t in range(NT + 1):
                w = P if t < NT else TS
                for k, src in enumerate((ab[:, 3, :], betaT[:, :])):
                    mm = pe.matmul(PS[0:w, 6, 8 * t + H * k:8 * t + H * k + H], src[:, t * P:t * P + w],
                                   C[0:H, 0:H], start=True, stop=True)
            mm.then_inc(ab_p, 1)

            def norms(first, last):
                for c in range(first, last):
                    pe.wait_ge(l2_sq, c + 1)
                    if c >= 2:
                        pe.wait_ge(l2_ln, c - 1)
                    for t in range(3):
                        mm = pe.matmul(PS[:, 3 * (c % 2) + t, 0:TH], const("ones"),
                                       sq2[:, c % 2, t * TH:t * TH + TH], start=True, stop=True)
                    mm.then_inc(l2_mm, 1)

            norms(0, 2 * H)

            def mm4(out, lhs, rhs, start=True, stop=True):
                for h in range(H):
                    ins = pe.matmul(out(h), lhs(h), rhs(h), start=start, stop=stop)
                return ins

            def dn_cum(u, n, w, cols, sfx):
                upto, after = const("upto" + sfx, w)[:, 0:w], const("after" + sfx, w)[:, 0:w]
                pe.wait_ge(dn_in, n)
                pe.wait_ge(dn_os, n)
                mm4(lambda h: bank(3 * u, w)[:, h, :], lambda h: dnh(u, GBC, P, w)[:, h, :], lambda h: upto)
                mm4(lambda h: bank(3 * u + 1, w)[:, h, :], lambda h: const("sel", H)[:, h * P:h * P + P],
                    lambda h: betaT[:, cols])
                pe.matmul(PS[0:w, 3 * u + 2, 0:H], upto, gbt[0:w, u, 0:H], start=True, stop=True)
                pe.matmul(PS[0:w, 3 * u + 2, H:2 * H], after, gbt[0:w, u, 0:H], start=True, stop=True
                          ).then_inc(dn_bc, 1)

            def dn_pairs(u, n, w, cols):
                pe.wait_ge(dn_d, n)
                kst = dnh(u, KST, w)
                mm4(lambda h: bank(3 * u + 1, w, w)[:, h, :], lambda h: kst[:, h, :], lambda h: dnh(u, KB, w)[:, h, :])
                mm4(lambda h: bank(3 * u + 2, w, w)[:, h, :], lambda h: kst[:, h, :], lambda h: QKV[:, h, cols])
                mm4(lambda h: bank(3 * u, P, w)[:, h, :], lambda h: dnh(u, VST, w)[:, h, :], lambda h: const("ident"))
                mm4(lambda h: bank(6 + u, P, w)[:, h, :], lambda h: kst[:, h, :], lambda h: const("ident")
                    ).then_inc(dn_e, 1)

            def dn_level_x(u, w, ready, g):
                pe.wait_ge(dn_t, ready)
                if g is not None:
                    pe.wait_ge(dn_g, g)
                mm4(lambda h: bank(3 * u, w, w)[:, h, :], lambda h: dnh(u, BT, w, w)[:, h, :],
                    lambda h: dnh(u, TM, w, w)[:, h, :]).then_inc(dn_x, 1)

            def dn_level_t(u, w, n, last):
                pe.wait_ge(dn_xs, n)
                x, tt = dnh(u, X, w, w), dnh(u, TTR, w, w)
                if not last:
                    mm4(lambda h: bank(3 * u + 1, w, w)[:, h, :], lambda h: tt[:, h, :], lambda h: x[:, h, :])
                mm4(lambda h: bank(3 * u + 2, w, w)[:, h, :], lambda h: x[:, h, :], lambda h: tt[:, h, :]
                    ).then_inc(dn_tt, 1)

            pe.wait_ge(ab_t, 1)
            with pe.Fori(0, NPAIR) as i:
                for u in range(2):
                    dn_cum(u, 2 * i + (u + 1), P, ds(2 * P * i + P * u, P), "")
                for u in range(2):
                    dn_pairs(u, 2 * i + (u + 1), P, ds(2 * P * i + P * u, P))
                for l in range(LEVELS):
                    for u in range(2):
                        dn_level_x(u, P, 2 * (LEVELS + 1) * i + (2 * l + u + 1), 2 * i + (u + 1) if l == 0 else None)
                    for u in range(2):
                        dn_level_t(u, P, 2 * LEVELS * i + (2 * l + u + 1), l == LEVELS - 1)
                for u in range(2):
                    pe.wait_ge(dn_st, 2 * i + (u + 1))
                    mm4(lambda h: bank(6)[:, h, :], lambda h: dnh(u, KBG)[:, h, :], lambda h: S[:, h, :]).then_inc(dn_ks, 1)
                    pe.wait_ge(dn_r, 2 * i + (u + 1))
                    mm4(lambda h: bank(7)[:, h, :], lambda h: dnh(u, TTR)[:, h, :], lambda h: dnh(u, RES)[:, h, :]).then_inc(dn_v, 1)
                    pe.wait_ge(dn_vs, 2 * i + (u + 1))
                    for h in range(H):
                        pe.matmul(bank(3 * u)[:, h, :], S[:, h, :], dnh(u, QD)[:, h, :], start=True, stop=False)
                        mm = pe.matmul(bank(3 * u)[:, h, :], dnh(u, VN)[:, h, :], dnh(u, QKT)[:, h, :], start=False, stop=True)
                    mm.then_inc(dn_o, 1)
                    mm4(lambda h: bank(6)[:, h, :], lambda h: dnh(u, KDEC)[:, h, :], lambda h: dnh(u, VN)[:, h, :]).then_inc(dn_ds, 1)
            dn_cum(0, NT + 1, TS, slice(SEQ, T), "_s")
            dn_pairs(0, NT + 1, TS, slice(SEQ, T))
            for l in range(LEVELS_S):
                dn_level_x(0, TS, NT * (LEVELS + 1) + l + 1, NT + 1 if l == 0 else None)
                dn_level_t(0, TS, NT * LEVELS + l + 1, l == LEVELS_S - 1)
            pe.wait_ge(dn_m, 1)
            pe.wait_ge(state_in, 16)
            for h in range(H):
                for s in range(NSEQ):
                    mm = pe.matmul(PS[0:TS, 6, h * P:h * P + P], kbgm[:, h, s, :], SS[:, s, h, :],
                                   start=s == 0, stop=s == NSEQ - 1)
            mm.then_inc(dn_ks, 1)
            pe.wait_ge(dn_r, NT + 1)
            mm4(lambda h: bank(7, P, TS)[:, h, :], lambda h: dnh(0, TTR, TS, TS)[:, h, :],
                lambda h: dnh(0, RES, P, TS)[:, h, :]).then_inc(dn_v, 1)
            pe.wait_ge(dn_vs, NT + 1)
            for h in range(H):
                for s in range(NSEQ):
                    pe.matmul(bank(0, TS)[:, h, :], SS[:, s, h, :], qdm[:, h, s, :], start=s == 0, stop=False)
                mm = pe.matmul(bank(0, TS)[:, h, :], dnh(0, VN, P, TS)[:, h, :], dnh(0, QKT, TS, TS)[:, h, :],
                               start=False, stop=True)
            mm.then_inc(dn_o, 1)
            for s in range(NSEQ):
                pe.wait_ge(dn_vm, s + 1)
                if s >= 2:
                    pe.wait_ge(dn_st, NT + 1 + s - 1)
                vm = dnh(0, (TM, TTR)[s % 2], P, TS)
                mm4(lambda h: bank(6 + s % 2)[:, h, :], lambda h: dnh(0, KDEC, P, TS)[:, h, :],
                    lambda h: vm[:, h, :]).then_inc(dn_ds, 1)

            pe.wait_ge(dn_st, NT + 1 + NSEQ)
            norms(2 * H, 3 * H)
            pe.wait_ge(l2_rn, 3 * H)
            with pe.Fori(0, (B_Y - B_Z) // 2) as i:
                for r in range(2):
                    pe.wait_ge(lo_done, 2 * i + (B_Z + r + 1))
                    pe.wait_ge(free_c, 2 * i + (r + 1))
                    products(pe, 1 - r, 1 - r, XH, XL).then_inc(unit_done, 1)
            pe.wait_ge(ol_done, H)
            pe.wait_ge(bl_done, H)
            with pe.Fori(0, KD // 2) as i:
                for q in range(2):
                    for r in range(2):
                        pe.wait_ge(lo_done, 6 * i + (B_Y + 3 * q + r + 1))
                        pe.wait_ge(y_read, 4 * i + (2 * q + r + 1))
                        products(pe, (1 + q + r) % 2, 1 - r, XH, XL).then_inc(unit_done, 1)
                    pe.wait_ge(lo_done, 6 * i + (B_Y + 3 * q + 3))
                    pe.wait_ge(sig_done, 4 * i + (2 * q + 1))
                    products(pe, (1 + q) % 2, 1, BH, BL, range(0, H)).then_inc(unit_done, 1)
                    pe.wait_ge(sig_done, 4 * i + (2 * q + 2))
                    products(pe, (1 + q) % 2, 0, OH, OL, range(H, KD), H).then_inc(unit_done, 1)
            pe.wait_ge(ml_done, KD)
            with pe.Fori(0, KD // 2) as i:
                for r in range(2):
                    pe.wait_ge(lo_done, 2 * i + (B_O + r + 1))
                    pe.wait_ge(free_h, 2 * i + (r + 1))
                    products(pe, 1 - r, 1 - r, XH, XL).then_inc(unit_done, 1)
            rms_pe(pe, rms_sems["nb"])
            pe.wait_ge(xl_done, 2 * KD)
            with pe.Fori(0, HP // 2) as i:
                for r in range(2):
                    pe.wait_ge(lo_done, 2 * i + (B_WQ + r + 1))
                    pe.wait_ge(free_w, 2 * i + (r + 1))
                    products(pe, 1 - r, 1 - r, XH, XL).then_inc(unit_done, 1)

            def sel_pe(w, n):
                pe.wait_ge(sel_q, n)
                for h in range(HP):
                    mm = pe.matmul(PS[0:w, h // 2, (h % 2) * 256:(h % 2) * 256 + 256], qst[:, h, 0:w],
                                   KEYS[:, h, :], start=True, stop=True)
                mm.then_inc(sel_mm, 1)
                pe.wait_ge(sel_g, n)
                for k, x in enumerate((e1, e2, gate)):
                    mm = pe.matmul(PS[:, 4, k * P:k * P + w], x[0:w, :], const("ident", w)[:, 0:w],
                                   start=True, stop=True)
                mm.then_inc(sel_t, 1)

            pe.wait_ge(keys_in, 16)
            pe.drain().then_inc(sel_mm, 1)
            with pe.Fori(0, NT) as i:
                sel_pe(P, i + 1)
            sel_pe(TS, NT + 1)

            pe.wait_ge(sel_done, NT + 1)
            pe.drain().then_inc(w_mm, 2)
            with pe.Fori(0, NWB // 2) as i:
                for s in range(2 * WT // WS):
                    pe.wait_ge(w_hot, 12 * i + (s + 1))
                    pe.wait_ge(w_evac, 12 * i + (s + 1))
                    for t in range(WS):
                        for k in range(3):
                            mm = pe.matmul(PS[:, 2 * (s % 3) + t // 4, (t % 4) * P:(t % 4) * P + P],
                                           HOT1[:, s % 2, :, t], HOTG[:, s % 2, k, :, t], start=k == 0, stop=k == 2)
                    mm.then_inc(w_mm, 1)

            def u_unit(m, slot, s, first=False):
                pe.wait_ge(u_lo, m)
                return products(pe, slot, s, XH, XL)

            def v_unit(d, slots, s):
                for c in range(GE):
                    cols = slice(c * P, c * P + P)
                    for n, (w, x) in enumerate(((VH, AH), (VH, AL), (VL, AH))):
                        for t in range(3):
                            mm = pe.matmul(PS[:, 3 * s + t, 0:TH], w[:, d % 2, cols],
                                           x[:, slots[c], t * TH:t * TH + TH],
                                           start=(c == 0 and n == 0), stop=(c == GE - 1 and n == 2))
                return mm

            pe.wait_ge(w_evac, 6 * NWB + 3)
            pe.drain().then_inc(v_mm, 2)
            u_unit(1, 0, 0).then_inc(u_mm, 1)

            def group_pe(i, q, last):
                g8, g4 = 16 * i + 8 * q, 8 * i + 4 * q
                for c in range(1, 5):
                    if last and c == 4:
                        continue
                    if c < 3:
                        pe.wait_ge(acc_done, g8 + c)
                    pe.wait_ge(a_gelu, g4 + max(c - 1, 1))
                    u_unit(g4 + c + 1, c % 2, c % 2).then_inc(u_mm, 1)
                slots = [4 * (q % 2), 1, 2, 3]
                for d in range(8):
                    pe.wait_ge(v_lo, g8 + d + 1)
                    if d == 0:
                        pe.wait_ge(a_lo, g4 + 4)
                        pe.wait_ge(a_gelu, g4 + 4)
                    elif d == 1:
                        if not last:
                            pe.wait_ge(a_gelu, g4 + 5)
                    if d >= 2:
                        pe.wait_ge(acc_done, g8 + d + 1)
                    v_unit(d, slots, (d + 1) % 2).then_inc(v_mm, 1)

            with pe.Fori(0, NG // 2 - 1) as i:
                for q in range(2):
                    group_pe(i, q, False)
            group_pe(NG // 2 - 1, 0, False)
            group_pe(NG // 2 - 1, 1, True)
            rms_pe(pe, rms_sems["nc"])

        @block.vector
        def _(dve):
            def norm(src, r, col, base):
                dve.wait_ge(r["rn"], 1)

                def low(k):
                    dve.wait_ge(xh_done, base + k + 1)
                    dve.tensor_tensor(XL[:, k, :], xt[:, k % 2, :], XH[:, k, :].bitcast(F32),
                                      ALU.subtract).then_inc(xl_done, 1)

                for k in range(KD):
                    if k >= 2:
                        dve.drain()
                    dve.scalar_tensor_tensor(out=xt[:, k % 2, :], in0=src[:, k, :],
                                             scalar=SW[:, col + k:col + k + 1], in1=rn[:, :],
                                             op0=ALU.mult, op1=ALU.mult).then_inc(xt_done, 1)
                    if k >= 1:
                        low(k - 1)
                low(KD - 1)

            dve.wait_ge(in_w, 16)
            norm(HID, rms_sems["na"], S_MIX, 0)
            split_lo(dve, 1, 0)
            dve.drain().then_inc(conv_q, 2)
            dve.wait_ge(zeroed, 1)
            LQ = PADQ - HQ
            with dve.Fori(0, NQ // 2) as i:
                for r in range(2):
                    split_lo(dve, 2 * i + (r + 2), 1 - r)
                    dve.wait_ge(hist_set, 2 * i + (r + 1))
                    dve.wait_ge(silu_q, 2 * i + (r + 1))
                    dve.wait_ge(evac_q, 2 * i + (r + 1))
                    for t in range(HQ + 1):
                        weight = SW[:, ds(8 * i + (S_CQ + 4 * r + t), 1)]
                        if t == 0:
                            dve.tensor_scalar(cy[:, r, 0:LQ], pad[:, r, 0:LQ], weight, None, ALU.mult)
                        else:
                            dve.drain()
                            ins = dve.scalar_tensor_tensor(out=cy[:, r, 0:LQ], in0=pad[:, r, t:t + LQ], scalar=weight,
                                                           in1=cy[:, r, 0:LQ], op0=ALU.mult, op1=ALU.add)
                    ins.then_inc(conv_q, 1)
            split_lo(dve, B_AB + 2, 1)
            dve.wait_ge(ab_a, 1)
            dve.tensor_tensor(ab[:, 3, :], ab[:, 1, :], ab[:, 2, :], ALU.add)
            dve.drain()
            dve.tensor_scalar(ab[:, 3, :], ab[:, 3, :], gsc[0:H, 0, 0:1], -1.0, ALU.mult, ALU.mult).then_inc(ab_v, 1)
            dve.wait_ge(ab_p, 1)
            dve.tensor_copy(gb_tok[:, 0:NT, :].rearrange("p t c -> p (t c)"), PS[:, 6, 0:8 * NT])
            dve.tensor_copy(gb_tok[0:TS, NT, :], PS[0:TS, 6, 8 * NT:8 * NT + 8]).then_inc(ab_t, 1)

            def norms(first, last, row, weight):
                for c in range(first, last):
                    dve.wait_ge(l2_rn, c + 1)
                    dve.scalar_tensor_tensor(out=QKV[:, row(c), :], in0=rn2[:, c % 2, :], scalar=weight(c),
                                             in1=QKV[:, row(c), :], op0=ALU.mult, op1=ALU.mult).then_inc(l2_done, 1)

            norms(0, 2 * H, lambda c: c, lambda c: float(P) ** -0.5 if c < H else 1.0)
            dve.drain()

            def dn_inputs(u, w, cols, tile):
                dve.tensor_copy(dnh(u, KST, w), QKV[:, H:2 * H, cols])
                dve.tensor_copy(dnh(u, VST, w), QKV[:, 2 * H:3 * H, cols])
                dve.tensor_copy(gbt[0:w, u, :], tile)
                dve.tensor_copy(dnh(u, GBC, P, w), tile[:, 0:H].unsqueeze(2).broadcast_to([w, H, P])).then_inc(dn_in, 1)

            def dn_diff(u, n, w, sfx):
                dve.wait_ge(dn_bc, n)
                dve.tensor_copy(gsc[0:w, u, :], PS[0:w, 3 * u + 2, 0:H])
                dve.tensor_tensor(dnh(u, KB, w), dnh(u, KST, w), bank(3 * u + 1, w), ALU.mult)
                dve.drain()
                for h in range(H):
                    ins = dve.scalar_tensor_tensor(
                        out=dnh(u, DIFF, w, w)[:, h, :], in0=bank(3 * u, w, w)[:, h, :], scalar=gsc[0:w, u, h:h + 1],
                        in1=const("neg" + sfx, w)[:, 0:w], op0=ALU.subtract, op1=ALU.add)
                ins.then_inc(dn_dt, 1)

            def dn_decay(u, n, w, cols):
                dve.wait_ge(dn_eg, n)
                dve.tensor_tensor(dnh(u, KBG, w), dnh(u, KB, w), dnh(u, EXPG, w), ALU.mult)
                dve.tensor_tensor(dnh(u, QD, w), QKV[:, 0:H, cols], dnh(u, EXPG, w), ALU.mult).then_inc(dn_d, 1)

            def mask(l, w, sfx):
                return const(f"mask{l}{sfx}", w)[:, 0:w].unsqueeze(1).broadcast_to([w, H, w])

            def dn_start(u, n, w, sfx):
                dve.wait_ge(dn_e, n)
                dve.tensor_tensor(dnh(u, MT, w, w), bank(3 * u + 1, w, w), dnh(u, DT, w, w), ALU.mult)
                dve.tensor_tensor(dnh(u, QKT, w, w), bank(3 * u + 2, w, w), dnh(u, DT, w, w), ALU.mult)
                dve.drain()
                unit = const("ident", w)[:, 0:w].unsqueeze(1).broadcast_to([w, H, w])
                dve.tensor_copy(dnh(u, TM, w, w), unit)
                dve.tensor_copy(dnh(u, TTR, w, w), unit)
                dve.tensor_tensor(dnh(u, BT, w, w), dnh(u, MT, w, w), mask(0, w, sfx), ALU.mult).then_inc(dn_t, 1)

            def dn_update(u, n, w, l, last, sfx):
                dve.wait_ge(dn_tt, n)
                if not last:
                    dve.tensor_tensor(dnh(u, TM, w, w), dnh(u, TM, w, w), bank(3 * u + 1, w, w), ALU.subtract)
                    dve.tensor_tensor(dnh(u, BT, w, w), dnh(u, MT, w, w), mask(l + 1, w, sfx), ALU.mult)
                dve.tensor_tensor(dnh(u, TTR, w, w), dnh(u, TTR, w, w), bank(3 * u + 2, w, w), ALU.subtract
                                  ).then_inc(dn_t, 1)

            def dn_residual(u, n, w, g):
                dve.wait_ge(dn_g, g)
                dve.wait_ge(dn_ks, n)
                dve.tensor_tensor(dnh(u, RES, P, w), dnh(u, VB, P, w), bank(6, P, w), ALU.subtract).then_inc(dn_r, 1)

            dve.wait_ge(out_q, 16)
            dve.memset(S[:, :, :], 0.0).then_inc(dn_st, 1)
            with dve.Fori(0, NPAIR) as i:
                dve.drain()
                for u in range(2):
                    dn_inputs(u, P, ds(2 * P * i + P * u, P), gb_tok[:, ds(2 * i + u, 1), :].rearrange("p n c -> p (n c)"))
                for u in range(2):
                    dn_diff(u, 2 * i + (u + 1), P, "")
                for u in range(2):
                    dn_decay(u, 2 * i + (u + 1), P, ds(2 * P * i + P * u, P))
                for u in range(2):
                    dn_start(u, 2 * i + (u + 1), P, "")
                for l in range(LEVELS):
                    for u in range(2):
                        dn_update(u, 2 * LEVELS * i + (2 * l + u + 1), P, l, l == LEVELS - 1, "")
                for u in range(2):
                    dn_residual(u, 2 * i + (u + 1), P, 2 * i + 2)
                    dve.wait_ge(dn_ds, 2 * i + (u + 1))
                    for h in range(H):
                        ins = dve.scalar_tensor_tensor(out=S[:, h, :], in0=S[:, h, :], scalar=dnh(u, EXPG)[:, h, P - 1:P],
                                                       in1=bank(6)[:, h, :], op0=ALU.mult, op1=ALU.add)
                    ins.then_inc(dn_st, 1)
            dve.drain()
            dn_inputs(0, TS, slice(SEQ, T), gb_tok[0:TS, NT, :])
            dn_diff(0, NT + 1, TS, "_s")
            dn_decay(0, NT + 1, TS, slice(SEQ, T))
            dve.drain()
            seqcol = const("seqcol").rearrange("p (s c) -> p s c", s=NSEQ)
            for src, dst in ((KBG, kbgm), (QD, qdm)):
                for h in range(H):
                    ins = dve.tensor_tensor(dst[:, h, :, :], dnh(0, src, TS)[:, h, :].unsqueeze(1).broadcast_to([P, NSEQ, TS]),
                                            seqcol, ALU.mult)
            ins.then_inc(dn_m, 1)
            dn_start(0, NT + 1, TS, "_s")
            for l in range(LEVELS_S):
                dn_update(0, NT * LEVELS + l + 1, TS, l, l == LEVELS_S - 1, "_s")
            dn_residual(0, NT + 1, TS, NT + 1)
            dve.wait_ge(dn_vs, NT + 1)
            for s in range(NSEQ + 1):
                if s < NSEQ:
                    if s >= 2:
                        dve.wait_ge(dn_ds, NT + s - 1)
                    dve.tensor_scalar(dnh(0, (TM, TTR)[s % 2], P, TS), dnh(0, VN, P, TS), const("seqrow", TS)[:, s:s + 1],
                                      None, ALU.mult).then_inc(dn_vm, 1)
                if s >= 1:
                    dve.wait_ge(dn_ds, NT + s)
                    for h in range(H):
                        last = SLEN * s - 1
                        ins = dve.scalar_tensor_tensor(
                            out=SS[:, s - 1, h, :], in0=SS[:, s - 1, h, :], scalar=dnh(0, EXPG, TS)[:, h, last:last + 1],
                            in1=bank(6 + (s - 1) % 2)[:, h, :], op0=ALU.mult, op1=ALU.add)
                    ins.then_inc(dn_st, 1)
            norms(2 * H, 3 * H, lambda c: c - 2 * H, lambda c: SW[:, S_DN:S_DN + 1])
            dve.wait_ge(out_s, 32)
            dve.drain().then_inc(free_c, 2)
            for h in range(H):
                n = B_Z + h
                split_lo(dve, n + 2, (n + 1) % 2)
                dve.wait_ge(silu_z, h + 1)
                dve.tensor_tensor(on[:, h % 2, :], QKV[:, h, :], zs[:, h % 2, :], ALU.mult).then_inc(on_done, 1)
                dve.drain().then_inc(free_c, 1)
                dve.wait_ge(oh_h, h + 1)
                dve.tensor_tensor(OL[:, h, :], on[:, h % 2, :], OH[:, h, :].bitcast(F32), ALU.subtract).then_inc(ol_done, 1)
            LA = PADA - HA
            for i in range(H):
                n = B_CONV + 3 * i
                st = n % 2
                split_lo(dve, n + 2, (n + 1) % 2)
                dve.wait_ge(unit_done, filled(n))
                dve.tensor_copy(thirds(cbuf[:, :]), pset(st)).then_inc(free_c, 1)
                split_lo(dve, n + 3, n % 2)
                dve.wait_ge(unit_done, filled(n + 1))
                if i:
                    dve.wait_ge(newa_set, i)
                dve.drain()
                dve.tensor_tensor(pada[:, HA:HA + 2 * TH].rearrange("p (a b) -> p a b", a=2),
                                  PS[:, 3 * (1 - st):3 * (1 - st) + 2, 0:TH],
                                  cbuf[:, 0:2 * TH].rearrange("p (a b) -> p a b", a=2), ALU.mult)
                dve.tensor_tensor(pada[:, HA + 2 * TH:HA + SEQ], PS[:, 3 * (1 - st) + 2, 0:SEQ - 2 * TH],
                                  cbuf[:, 2 * TH:SEQ], ALU.mult)
                dve.tensor_tensor(seqs(pada, HA + SEQ, HA, HA, SLEN),
                                  PS[:, 3 * (1 - st) + 2, SEQ - 2 * TH:TH].rearrange("p (s c) -> p s c", s=NSEQ),
                                  cbuf[:, SEQ:T].rearrange("p (s c) -> p s c", s=NSEQ), ALU.mult).then_inc(free_c, 1)
                split_lo(dve, n + 4, (n + 1) % 2)
                dve.wait_ge(c_hist, i + 1)
                for t in range(HA + 1):
                    weight = SW[:, S_CA + 3 * i + t:S_CA + 3 * i + t + 1]
                    dve.drain()
                    if t == 0:
                        dve.tensor_scalar(ya[:, 0:LA], pada[:, 0:LA], weight, None, ALU.mult)
                    else:
                        ins = dve.scalar_tensor_tensor(out=ya[:, 0:LA], in0=pada[:, t:t + LA], scalar=weight,
                                                       in1=ya[:, 0:LA], op0=ALU.mult, op1=ALU.add)
                ins.then_inc(ya_done, 1)
                dve.wait_ge(unit_done, filled(n + 2))
                dve.drain()
                dve.tensor_tensor(bc[:, 0:2 * TH].rearrange("p (a b) -> p a b", a=2), PS[:, 3 * st:3 * st + 2, 0:TH],
                                  ya[:, 0:2 * TH].rearrange("p (a b) -> p a b", a=2), ALU.mult)
                dve.tensor_tensor(bc[:, 2 * TH:SEQ], PS[:, 3 * st + 2, 0:SEQ - 2 * TH], ya[:, 2 * TH:SEQ], ALU.mult)
                dve.tensor_tensor(bc[:, SEQ:T].rearrange("p (s c) -> p s c", s=NSEQ),
                                  PS[:, 3 * st + 2, SEQ - 2 * TH:TH].rearrange("p (s c) -> p s c", s=NSEQ),
                                  seqs(ya, HA + SEQ, HA, 0, SLEN), ALU.mult).then_inc(bc_done, 1)
                dve.drain().then_inc(free_c, 1)
                dve.wait_ge(bh_done, i + 1)
                dve.tensor_tensor(BL[:, i, :], bc[:, :], BH[:, i, :].bitcast(F32), ALU.subtract).then_inc(bl_done, 1)
            dve.drain().then_inc(y_read, 2)
            dve.drain().then_inc(m_done, 1)
            with dve.Fori(0, KD // 2) as i:
                for q in range(2):
                    row = thirds(HID[:, ds(2 * i + q, 1), :].rearrange("p n t -> p (n t)"))
                    for r in range(3):
                        nxt = B_Y + 3 * q + r + 1
                        split_lo(dve, 6 * i + (nxt + 1), nxt % 2)
                    dve.wait_ge(unit_done, 8 * i + filled(B_Y + 4 * q + 2))
                    dve.wait_ge(sig_done, 4 * i + (2 * q + 1))
                    dve.tensor_tensor(row, pset(1), thirds(sig[:, 0, :]), ALU.mult).then_inc(y_read, 1)
                    dve.wait_ge(unit_done, 8 * i + filled(B_Y + 4 * q + 3))
                    dve.wait_ge(sig_done, 4 * i + (2 * q + 2))
                    dve.tensor_tensor(thirds(sig[:, 1, :]), pset(0), thirds(sig[:, 1, :]), ALU.mult).then_inc(y_read, 1)
                    dve.drain()
                    dve.tensor_tensor(row, row, thirds(sig[:, 1, :]), ALU.add).then_inc(m_done, 1)
            for k in range(KD):
                dve.wait_ge(mh_done, k + 1)
                dve.tensor_tensor(XL[:, k, :], HID[:, k, :], XH[:, k, :].bitcast(F32), ALU.subtract).then_inc(ml_done, 1)
            dve.drain().then_inc(free_h, 2)
            with dve.Fori(0, KD // 2) as i:
                for r in range(2):
                    split_lo(dve, 2 * i + (B_O + r + 2), (B_O + r + 1) % 2)
                    dve.wait_ge(xr_in[r], 16 * i + 16)
                    dve.wait_ge(unit_done, 2 * i + filled(unit_of(B_O) + r))
                    dve.tensor_tensor(thirds(HID[:, ds(2 * i + r, 1), :].rearrange("p n t -> p (n t)")), pset(1 - r),
                                      thirds(xr[:, r, :]), ALU.add).then_inc(free_h, 1)
            dve.drain()
            norm(HID, rms_sems["nb"], S_FFN, KD)
            for j in range(HP - 1):
                split_lo(dve, B_WQ + j + 2, (B_WQ + j + 1) % 2)

            def sel_dve(w, n, cols):
                def r(x):
                    return x[0:w]
                dve.wait_ge(sel_sc, n)
                dve.tensor_copy(r(tick), r(sc)[:, 0, 0:1])
                for j in range(2 * HP):
                    dve.max(r(best)[:, j, 0:8], r(sc)[:, j, :])
                dve.drain()
                for j in range(2 * HP):
                    dve.match_replace(r(sc2)[:, j, :], r(best)[:, j, 0:8], r(sc)[:, j, :], -3.4e38)
                    dve.max_index(r(besti)[:, j, 0:8], r(best)[:, j, 0:8], r(sc)[:, j, :])
                dve.drain().then_inc(sel_read, 1)
                for j in range(2 * HP):
                    dve.max(r(best)[:, j, 8:16], r(sc2)[:, j, :])
                dve.drain()
                for j in range(2 * HP):
                    dve.max_index(r(besti)[:, j, 8:16], r(best)[:, j, 8:16], r(sc2)[:, j, :])
                b2 = r(best).rearrange("p (h s) k -> p h s k", s=2)
                for i0, rows, n_cols in CAND:
                    a = ROW_START[i0]
                    dve.tensor_tensor(
                        r(cand)[:, :, a:a + rows * n_cols].rearrange("p h (i j) -> p h i j", i=rows),
                        b2[:, :, 0, i0:i0 + rows].unsqueeze(3).broadcast_to([w, HP, rows, n_cols]),
                        b2[:, :, 1, 0:n_cols].unsqueeze(2).broadcast_to([w, HP, rows, n_cols]), ALU.add)
                dve.drain()
                dve.tensor_copy(r(bestf), r(besti))
                for h in range(HP):
                    dve.max(r(top)[:, h, 0:8], r(cand)[:, h, :])
                dve.drain()
                for h in range(HP):
                    dve.match_replace(r(cand2)[:, h, :], r(top)[:, h, 0:8], r(cand)[:, h, :], -3.4e38)
                    dve.max_index(r(topi)[:, h, 0:8], r(top)[:, h, 0:8], r(cand)[:, h, :])
                dve.drain()
                for h in range(HP):
                    dve.max(r(top)[:, h, 8:16], r(cand2)[:, h, :])
                dve.drain()
                for h in range(HP):
                    dve.max_index(r(topi)[:, h, 8:16], r(top)[:, h, 8:16], r(cand2)[:, h, :])
                g3 = r(gate).rearrange("p (h k) -> p h k", h=HP)
                dve.tensor_tensor(g3, r(top), r(top)[:, :, 0:1].broadcast_to([w, HP, TOPK]), ALU.subtract).then_inc(sel_b, 1)
                f2 = r(bestf).rearrange("p (h s) k -> p h s k", s=2)
                dve.tensor_copy(r(delta)[:, :, 0:1], f2[:, :, 0, 0:1])
                dve.tensor_tensor(r(delta)[:, :, 1:TOPK], f2[:, :, 0, 1:TOPK], f2[:, :, 0, 0:TOPK - 1], ALU.subtract)
                dve.drain()
                dve.tensor_copy(r(topf), r(topi))
                dve.drain()

                def over(x):
                    return x.unsqueeze(2).broadcast_to([w, HP, TOPK, TOPK])

                def each(x):
                    return x.unsqueeze(3).broadcast_to([w, HP, TOPK, TOPK])

                def row(x):
                    return x.unsqueeze(1).unsqueeze(1).broadcast_to([w, HP, TOPK, TOPK])

                e1v, e2v = (r(x).rearrange("p (h k) -> p h k", h=HP) for x in (e1, e2))
                dve.tensor_tensor(r(hot), each(r(topf)), row(const("start16", w)), ALU.is_ge)
                dve.drain()
                dve.tensor_tensor(r(pick), r(hot), over(r(delta)), ALU.mult)
                dve.drain()
                dve.tensor_reduce(e1v, r(pick), AX.X, ALU.add)
                dve.drain()
                dve.tensor_tensor(r(pick), r(hot), row(r(dstart)), ALU.mult)
                dve.drain()
                dve.tensor_reduce(e2v, r(pick), AX.X, ALU.add)
                dve.drain()
                dve.tensor_tensor(r(topf), r(topf), e2v, ALU.subtract)
                dve.drain()
                dve.tensor_tensor(r(hot), each(r(topf)), row(const("iota16", w)), ALU.is_equal)
                dve.drain()
                dve.tensor_tensor(r(pick), r(hot), over(f2[:, :, 1, :]), ALU.mult)
                dve.drain()
                dve.tensor_reduce(e2v, r(pick), AX.X, ALU.add)
                dve.wait_ge(sel_e, n)
                dve.tensor_reduce(r(gsum), g3, AX.X, ALU.add)
                dve.drain()
                dve.reciprocal(r(gsum), r(gsum))
                dve.drain()
                dve.tensor_tensor(g3, g3, r(gsum).unsqueeze(2).broadcast_to([w, HP, TOPK]), ALU.mult).then_inc(sel_g, 1)
                dve.wait_ge(sel_t, n)
                dve.tensor_copy(EG[:, 0, cols], PS[:, 4, 0:w])
                dve.tensor_copy(EG[:, 1, cols], PS[:, 4, P:P + w])
                dve.tensor_copy(EG[:, 2, cols], PS[:, 4, 2 * P:2 * P + w])
                dve.drain()
                dve.tensor_tensor(gres[:, 0:w], PS[:, 4, 2 * P:2 * P + w], EG[:, 2, cols], ALU.subtract)
                dve.drain()
                dve.tensor_copy(EG[:, 3, cols], gres[:, 0:w])
                dve.drain()
                dve.tensor_tensor(EG[:, 4, cols], gres[:, 0:w], EG[:, 3, cols], ALU.subtract).then_inc(sel_done, 1)

            dve.wait_ge(iota_set, 1)
            dve.wait_ge(free_w, HP + 2)
            dve.tensor_tensor(dstart[:, 1:TOPK], const("start16")[:, 1:TOPK], const("start16")[:, 0:TOPK - 1], ALU.subtract)
            dve.tensor_copy(dstart[:, 0:1], const("start16")[:, 0:1])
            dve.drain().then_inc(sel_read, 1)
            with dve.Fori(0, NT) as i:
                dve.drain()
                sel_dve(P, i + 1, ds(P * i, P))
            dve.drain()
            sel_dve(TS, NT + 1, slice(SEQ, T))

            dve.drain()
            dve.wait_ge(iota_set, 2)
            with dve.Fori(0, NWB // 2) as i:
                for s in range(2 * WT // WS):
                    cols = ds(2 * WT * i + WS * s, WS)

                    def row(k):
                        return EG[:, k, cols].unsqueeze(1).broadcast_to([P, NKEYS, WS])
                    dve.wait_ge(w_mm, 12 * i + (s + 1))
                    dve.tensor_tensor(HOT1[:, s % 2], IOTA[:, :, :], row(0), ALU.is_equal)
                    dve.tensor_tensor(HOT2[:, s % 2], IOTA[:, :, :], row(1), ALU.is_equal)
                    dve.drain()
                    for k in range(3):
                        ins = dve.tensor_tensor(HOTG[:, s % 2, k], HOT2[:, s % 2], row(2 + k), ALU.mult)
                    ins.then_inc(w_hot, 1)

            def u_low(m, slot):
                dve.wait_ge(u_hi, m)
                dve.tensor_tensor(WL[:, slot, :], RAW[:, slot, :], WH[:, slot, :].bitcast(F32), ALU.subtract).then_inc(u_lo, 1)

            def gated(m, slot, g, reads):
                dve.wait_ge(gw_in[g // 2], reads)
                dve.wait_ge(a_gelu, m)
                dve.tensor_tensor(AF[:, slot, :], AF[:, slot, :], GW[:, g // 2, :, g % 2], ALU.mult).then_inc(a_mul, 1)
                dve.wait_ge(a_hi, m)
                dve.tensor_tensor(AL[:, slot, :], AF[:, slot, :], AH[:, slot, :].bitcast(F32), ALU.subtract).then_inc(a_lo, 1)

            def v_low(d, s):
                dve.wait_ge(v_hi, s)
                dve.tensor_tensor(VL[:, d % 2, :], VRAW[:, d % 4, :], VH[:, d % 2, :].bitcast(F32), ALU.subtract).then_inc(v_lo, 1)

            dve.drain().then_inc(acc_done, 2)
            u_low(1, 0)
            u_low(2, 1)
            gated(1, 0, 0, 16)

            def group_dve(i, q, last):
                g8, g4 = 16 * i + 8 * q, 8 * i + 4 * q
                for c in range(1, 5):
                    if last and c == 4:
                        continue
                    if not (last and c == 3):
                        u_low(g4 + c + 2, (c + 1) % 2)
                    if c == 3:
                        for d in range(2):
                            v_low(d, g8 + d + 1)
                    gated(g4 + c + 1, c if c < 4 else 4 * ((q + 1) % 2), c % 4,
                          32 * i + 16 * q + 16 * (1 + c // 4))
                for d in range(8):
                    dve.wait_ge(v_mm, g8 + d + 3)
                    dve.tensor_tensor(thirds(HID[:, d, :]), thirds(HID[:, d, :]), pset((d + 1) % 2), ALU.add).then_inc(acc_done, 1)
                    if d < 6:
                        v_low(d + 2, g8 + d + 3)

            with dve.Fori(0, NG // 2 - 1) as i:
                for q in range(2):
                    group_dve(i, q, False)
            group_dve(NG // 2 - 1, 0, False)
            group_dve(NG // 2 - 1, 1, True)
            dve.wait_ge(rms_sems["nc"]["rn"], 1)
            for k in range(KD):
                if k >= 2:
                    dve.wait_ge(out_y[k % 2], 16 * (k // 2))
                dve.scalar_tensor_tensor(out=xt[:, k % 2, :], in0=HID[:, k, :], scalar=SW[:, S_FIN + k:S_FIN + k + 1],
                                         in1=rn[:, :], op0=ALU.mult, op1=ALU.mult).then_inc(y_row, 1)


def packed(w):
    k, n = w.shape[0] // P, w.shape[1] // P
    return w.reshape(k, P, n, P).transpose(2, 1, 0, 3)


def kernel(x_prompt, x_sample, state_conv_a, state_conv_qkv, state_delta, g_norm_mix, w_in, w_conv_a,
           w_conv_qkv, a_log, dt_bias, g_dn_norm, w_out_a, w_out_dn, w_o, g_norm_ffn, w_query, sub_keys,
           expert_u, expert_v, g_norm_final):
    import concourse.bacc as bacc
    from concourse.bass_utils import run_bass_kernel_spmd

    def chunks(w, *tail):
        return w.reshape(-1, w.shape[-1] // P, P).transpose(2, 1, 0)

    x = np.concatenate([np.asarray(x_prompt).reshape(SEQ, D), np.asarray(x_sample).reshape(TS, D)])
    w = np.asarray(w_in)[0]
    half, wide = D // 2, H * P
    at = {}
    o = 0
    for name, n in (("b", half), ("c", half), ("h", half), ("qkv", 3 * wide), ("z", wide), ("a", H), ("beta", H),
                    ("ga", D), ("gb", D)):
        at[name] = w[:, o:o + n]
        o += n
    ab = np.zeros((D, P), w.dtype)
    ab[:, 0:H], ab[:, 32:32 + H] = at["a"], at["beta"]
    pk = {n: packed(v) for n, v in at.items() if n not in ("a", "beta")}
    wa, wd = packed(np.asarray(w_out_a)[0]), packed(np.asarray(w_out_dn)[0])
    blocks = [pk["qkv"], packed(ab), pk["z"]]
    for i in range(H):
        blocks += [pk[n][i:i + 1] for n in ("c", "h", "b")]
    for j in range(KD):
        blocks += [pk["ga"][j:j + 1], pk["gb"][j:j + 1], np.concatenate([wa[j:j + 1], wd[j:j + 1]], axis=2)]
    blocks += [packed(np.asarray(w_o)[0]), packed(np.asarray(w_query)[0])]
    wall = np.ascontiguousarray(np.concatenate(blocks)).reshape(NBLK, P, D)

    small = np.zeros((P, NSMALL), w.dtype)
    for col, g in ((S_MIX, g_norm_mix), (S_FFN, g_norm_ffn), (S_FIN, g_norm_final)):
        small[:, col:col + KD] = np.asarray(g).reshape(KD, P).T
    small[:, S_CQ:S_CQ + 4 * NQ] = chunks(np.asarray(w_conv_qkv)[0]).reshape(P, 4 * NQ)
    small[:, S_CA:S_CA + 3 * H] = chunks(np.asarray(w_conv_a)[0]).reshape(P, 3 * H)
    small[:, S_DN] = np.asarray(g_dn_norm)[0]
    small[0:H, S_ALOG] = np.asarray(a_log)[0]
    small[0:H, S_DT] = np.asarray(dt_bias)[0]

    sk = np.asarray(sub_keys)[0]
    keys = np.zeros((P, HP, 2 * NKEYS), sk.dtype)
    for p in range(2):
        keys[64 * p:64 * p + 64, :, NKEYS * p:NKEYS * p + NKEYS] = sk[p].transpose(2, 0, 1)

    def history(s):
        n, k, c = s.shape
        return np.ascontiguousarray(s.reshape(n, k, c // P, P).transpose(3, 2, 0, 1))

    arrays = {
        "x_t": np.ascontiguousarray(x.reshape(T, KD, P).transpose(2, 1, 0)),
        "weights": wall,
        "small": small,
        "keys": keys,
        "constants": CONSTANTS,
        "hist_qkv": history(np.asarray(state_conv_qkv)[0]),
        "hist_a": history(np.asarray(state_conv_a)[0]),
        "state": np.ascontiguousarray(np.asarray(state_delta)[0].transpose(2, 0, 1, 3)),
        "experts_u": np.ascontiguousarray(
            np.asarray(expert_u)[0].reshape(NKEYS, NKEYS, KD, P).transpose(1, 3, 2, 0)).reshape(NKEYS, P, D),
        "experts_v": np.ascontiguousarray(
            np.asarray(expert_v)[0].reshape(NKEYS, NG, GE, KD, P).transpose(1, 3, 0, 2, 4)).reshape(NG * KD, P, GE * P),
    }
    outs = {"y_t": (P, KD, T), "new_qkv": (P, NQ, NSEQ + 1, HQ), "new_a": (P, H, NSEQ + 1, HA),
            "state_p": (P, H, P), "state_s": (P, NSEQ, H, P)}
    nc = bacc.Bacc("TRN2", target_bir_lowering=False, num_devices=1)
    ins = [nc.dram_tensor(n, a.shape, F32, kind="ExternalInput").ap() for n, a in arrays.items()]
    got = [nc.dram_tensor(n, s, F32, kind="ExternalOutput").ap() for n, s in outs.items()]
    gates = nc.dram_tensor("gate_matrices", (NKEYS // 2, P, T, 2), F32, kind="Internal").ap()
    program(nc, *ins, *got, gates)
    res = run_bass_kernel_spmd(nc, [arrays], core_ids=[0]).results[0]

    y = res["y_t"].transpose(2, 1, 0).reshape(T, D)
    new_q = res["new_qkv"].transpose(2, 3, 1, 0).reshape(NSEQ + 1, HQ, NQ * P)
    new_a = res["new_a"].transpose(2, 3, 1, 0).reshape(NSEQ + 1, HA, H * P)
    return (y[:SEQ].reshape(1, SEQ, D), y[SEQ:].reshape(NSEQ, SLEN, D),
            new_a[None, 0:1], new_q[None, 0:1], res["state_p"].transpose(1, 0, 2)[None, None],
            new_a[None, 1:], new_q[None, 1:], res["state_s"].transpose(1, 2, 0, 3)[None])
```

```python
from contextlib import ExitStack

import numpy as np

import concourse.bass as bass
from concourse import mybir

F32 = mybir.dt.float32
F32R = mybir.dt.float32r
BF16 = mybir.dt.bfloat16
F16 = mybir.dt.float16
U32 = mybir.dt.uint32
ALU = mybir.AluOpType
ACT = mybir.ActivationFunctionType
AX = mybir.AxisListType
ds = bass.ds

P = 128
D = 1024
KD = D // P
SEQ = 1024
NSEQ, SLEN = 8, 4
TS = NSEQ * SLEN
T = SEQ + TS
TH = T // 3
NT = SEQ // P
H = 4
NQ = 3 * H
EPS = 1e-6
NEG = -1e30
HP = 8
TOPK = 16
NKEYS = 128
PAIRS = HP * TOPK

CAND = [(0, 1, 16), (1, 1, 8), (2, 2, 5), (4, 4, 3), (8, 8, 1)]
ROW_LEN = [cols for _, rows, cols in CAND for _ in range(rows)]
ROW_START = [sum(ROW_LEN[:i]) for i in range(TOPK)]
NCAND = sum(ROW_LEN)

B_QKV, B_AB, B_Z, B_CONV, B_Y, B_O, B_WQ, NBLK = 0, 12, 13, 17, 29, 53, 61, 69

GE = 4
NG = NKEYS // GE
EARLY = 2
LATE = GE - EARLY
NE = NG * EARLY
SEL_E, WM_E = 4, 2
E0 = SEL_E * (SEQ // P + 1)
GSCALE = 2.0 ** 15
WT = 48
WS = 8
NWB = T // WT
S_MIX, S_FFN, S_FIN, S_CQ, S_CA, S_DN, S_ALOG, S_DT, NSMALL = 0, 8, 16, 24, 72, 84, 85, 86, 88
HQ, HA = 3, 2
PADQ, PADA = HQ + SEQ + NSEQ * (SLEN + HQ), HA + SEQ + NSEQ * (SLEN + HA)


def constants():
    i = np.arange(P)
    lo, hi = i[:, None], i[None, :]
    a, b = np.arange(TS)[:, None], np.arange(TS)[None, :]
    same = a // SLEN == b // SLEN

    def rows(x):
        return np.concatenate([x, np.zeros((P - TS, x.shape[1]))])

    def level(row, col, l):
        return (row >> (l + 1) == col >> (l + 1)) & (row >> l != col >> l) & (col > row)

    parts = {"ident": lo == hi, "ones": np.ones((P, P)),
             "iota16": np.tile(np.arange(TOPK)[None], (P, 1)),
             "start16": np.tile(np.array(ROW_START)[None], (P, 1)),
             "upto": lo <= hi, "after": lo > hi, "neg": np.where(lo > hi, NEG, 0.0)}
    for l in range(7):
        parts[f"mask{l}"] = level(lo, hi, l)
    parts["upto_s"] = rows(same & (a <= b))
    parts["after_s"] = rows(same & (a > b))
    parts["neg_s"] = rows(np.where(same & (a <= b), 0.0, NEG))
    for l in range(2):
        parts[f"mask{l}_s"] = rows(level(a, b, l))
    seq = np.arange(TS)[None, :] // SLEN == np.arange(NSEQ)[:, None]
    parts["seqcol"] = np.tile(seq.reshape(1, -1), (P, 1))
    parts["seqrow"] = rows(seq.T)
    parts["sel"] = np.repeat(lo == np.arange(H)[None], P, axis=1)
    at, where = 0, {}
    for name, x in parts.items():
        where[name] = (at, x.shape[1])
        at += x.shape[1]
    return np.concatenate([np.asarray(x, np.float32) for x in parts.values()], axis=1), where


CONSTANTS, CONST_AT = constants()
NCST = CONSTANTS.shape[1]


def unit_of(block):
    if block < B_Y:
        return block
    if block < B_O:
        j, r = divmod(block - B_Y, 3)
        return B_Y + 4 * j + (0, 1, 3)[r]
    return block + KD


def program(nc, xT, wall, small, keys, cst, histq, hista, s_in, u_blk, v_blk,
            yT, convq_out, conva_out, sp_out, ss_out, w_dram, q_dram, act_dram):
    with ExitStack() as ctx:
        def sem(name):
            return ctx.enter_context(nc.semaphore(name))

        BASE = -(-nc.sbuf_base // 64) * 64
        arena = ctx.enter_context(nc.sbuf_tensor("arena", [P, (229344 - BASE) // 4 - 8], F32))

        def at(off, name, shape, dt=F32):
            size = int(np.prod(shape[1:])) * (2 if dt in (BF16, F16) else 4)
            assert off % 4 == 0 and BASE + off + size <= 229344, (name, off, size)
            return nc.alloc_sbuf_tensor_at(name, list(shape), dt, offset=BASE + off, align_bytes=4)

        ROW = 4 * T
        XH = at(0, "XH", [P, KD, T], F32R)
        XL = at(8 * ROW, "XL", [P, KD, T], F32R)
        ring = 16 * ROW
        RAW = at(ring, "RAW", [P, 2, D])
        WH = at(ring + 8192, "WH", [P, 2, D], F32R)
        WL = at(ring + 16384, "WL", [P, 2, D], F32R)
        c0 = ring + 24576
        C = at(c0, "C", [P, NCST])
        SW = at(c0 + 4 * NCST, "SW", [P, NSMALL])
        gb_tok = at(c0 + 4 * NCST + 4 * NSMALL, "gb_tok", [P, NT + 1, 8])
        r1 = c0 + 4 * NCST + 4 * NSMALL + 288
        r2, r3, r4 = r1 + 8 * ROW, r1 + 16 * ROW, r1 + 24 * ROW

        HID = at(r1, "HID", [P, KD, T])
        sq = at(r3, "sq", [P, 2, T])
        rn = at(r3 + 2 * ROW, "rn", [P, T])
        xt = at(r3 + 3 * ROW, "xt", [P, 2, T])
        QKV = at(r2, "QKV", [P, NQ, T])
        pad = at(r1, "pad", [P, 2, PADQ])
        cy = at(r1 + 8 * PADQ, "cy", [P, 2, PADQ])
        hist = at(r1 + 16 * PADQ, "hist", [P, NQ, NSEQ, HQ])
        new_q = at(r1 + 16 * PADQ + 4 * NQ * 24, "new_q", [P, NQ, NSEQ + 1, HQ])
        ab = at(r3 + 4 * ROW, "ab", [H, 4, T])
        betaT = at(r4, "betaT", [H, T])
        sq2 = at(r1, "sq2", [P, 2, T])
        rn2 = at(r1 + 2 * ROW, "rn2", [P, 2, T])
        DN1 = at(r1, "DN1", [P, 16, 512])
        DN2 = at(r3 + 4 * ROW, "DN2", [P, 8, 512])
        S = at(r4 + ROW, "S", [P, H, P])
        SS = at(r3 + 4 * ROW, "SS", [P, NSEQ, H, P])
        kbgm = at(r1 + 12 * 2048, "kbgm", [P, H, NSEQ, TS])
        qdm = at(r1 + 14 * 2048, "qdm", [P, H, NSEQ, TS])
        gbt = at(r4 + ROW + 2112, "gbt", [P, 2, 8])
        gsc = at(r4 + ROW + 2048, "gsc", [P, 2, 4])
        ekd = at(r4 + ROW + 2080, "ekd", [P, 2, 4])
        zs = at(r1, "zs", [P, 2, T])
        on = at(r1 + 2 * ROW, "on", [P, 2, T])
        OH = at(r3, "OH", [P, H, T], F32R)
        OL = at(r3 + 4 * ROW, "OL", [P, H, T], F32R)
        BH = at(r2, "BH", [P, H, T], F32R)
        BL = at(r2 + 4 * ROW, "BL", [P, H, T], F32R)
        cbuf = at(r1 + 4 * ROW, "cbuf", [P, T])
        pada = at(r1 + 5 * ROW, "pada", [P, PADA])
        ya = at(r1 + 5 * ROW + 4 * PADA, "ya", [P, PADA])
        bc = at(r4, "bc", [P, T])
        hist_a = at(r4 + ROW, "hist_a", [P, H, NSEQ, HA])
        new_a = at(r4 + ROW + 256, "new_a", [P, H, NSEQ + 1, HA])
        sig = at(r4, "sig", [P, 2, T])
        xr = at(r3, "xr", [P, 2, T])
        KEYS = at(r2, "KEYS", [P, HP, 2 * NKEYS])
        qst = at(r2 + 8192, "qst", [P, HP, P])
        qrow = at(r2 + 12288, "qrow", [P, 2, T])
        sel0 = r2 + 12288 + 2 * ROW
        sc = at(sel0, "sc", [P, 2 * HP, NKEYS])
        sc2 = at(sel0 + 8192, "sc2", [P, 2 * HP, NKEYS])
        hot = at(sel0 + 16384, "hot", [P, HP, TOPK, TOPK], BF16)
        pick = at(sel0 + 20480, "pick", [P, HP, TOPK, TOPK], BF16)
        cand = at(sel0 + 24576, "cand", [P, HP, NCAND])
        cand2 = at(sel0 + 24576 + 32 * NCAND, "cand2", [P, HP, NCAND])
        o = [sel0 + 24576 + 64 * NCAND]

        def small_at(name, shape, dt=F32):
            t = at(o[0], name, shape, dt)
            o[0] += int(np.prod(shape[1:])) * (2 if dt == BF16 else 4)
            return t

        best = small_at("best", [P, 2 * HP, TOPK])
        besti = small_at("besti", [P, 2 * HP, TOPK], U32)
        bestf = small_at("bestf", [P, 2 * HP, TOPK], BF16)
        delta = small_at("delta", [P, HP, TOPK], BF16)
        top = small_at("top", [P, HP, TOPK])
        topi = small_at("topi", [P, HP, TOPK], U32)
        topf = small_at("topf", [P, HP, TOPK])
        e1 = small_at("e1", [P, PAIRS])
        e2 = small_at("e2", [P, PAIRS])
        gate = small_at("gate", [P, PAIRS])
        gsum = small_at("gsum", [P, HP])
        iota_b = small_at("iota_b", [P, TOPK], BF16)
        dstart = small_at("dstart", [P, TOPK], BF16)
        tick = small_at("tick", [P, 1])
        stg = at(r2, "stg", [P, 2, NG, WT, GE])
        oh0 = r2 + 2 * 512 * WT
        assert o[0] <= oh0 + 8192
        IOTA = at(oh0, "IOTA", [P, NKEYS, WS], F16)
        HOT1 = at(oh0 + 2048, "HOT1", [P, 2, NKEYS, WS], F16)
        HOT2 = at(oh0 + 6144, "HOT2", [P, NKEYS, WS], F16)
        EG = at(oh0 + 8192, "EG", [P, 4, T], F16)
        late = CONST_AT["upto"][0]
        assert 4 * (NCST - late) >= 8192
        HOTG = at(c0 + 4 * late, "HOTG", [P, 2, 2, NKEYS, WS], F16)
        AH = at(r2, "AH", [P, GE, T], F32R)
        AL = at(r2 + 4 * ROW, "AL", [P, GE, T], F32R)
        AF = at(r2 + 4 * ROW, "AF", [P, GE, T])
        VRAW = at(r2 + 8 * ROW, "VRAW", [P, 4, GE * P])
        VH = at(r2 + 8 * ROW + 8192, "VH", [P, 2, GE * P], F32R)
        VL = at(r2 + 8 * ROW + 12288, "VL", [P, 2, GE * P], F32R)
        GW = at(r2 + 8 * ROW + 16384, "GW", [P, T, GE])
        AS = at(r2 + 12 * ROW + 16384, "AS", [P, EARLY, T])

        PS = ctx.enter_context(nc.psum_tensor("PS", [P, 8, 512], F32))

        def const(name, rows=P):
            a, n = CONST_AT[name]
            return C[0:rows, a:a + n]

        def thirds(ap):
            return ap.rearrange("p (a b) -> p a b", a=3)

        def pset(s, rows=P):
            return PS[0:rows, 3 * s:3 * s + 3, 0:TH]

        in_c, in_x, in_w = sem("in_c"), sem("in_x"), sem("in_w")
        raw_in = [sem("raw_in0"), sem("raw_in1")]
        hi_done, lo_done, unit_done = sem("hi_done"), sem("lo_done"), sem("unit_done")

        def filled(u):
            return u + 2

        block = ctx.enter_context(nc.Block())

        def split_hi(act, n, slot, reads, before):
            act.wait_ge(raw_in[slot], reads)
            if before is not None:
                act.wait_ge(unit_done, before)
            act.activation(WH[:, slot, :], RAW[:, slot, :], ACT.Copy).then_inc(hi_done, 1)

        def split_lo(dve, count, slot):
            dve.wait_ge(hi_done, count)
            dve.tensor_tensor(WL[:, slot, :], RAW[:, slot, :], WH[:, slot, :].bitcast(F32),
                              ALU.subtract).then_inc(lo_done, 1)

        def products(pe, slot, s, xh, xl, chunks=range(KD), base=0, bank=None, part=slice(None)):
            first = 3 * s if bank is None else bank
            steps = [(k, n, t) for k in chunks for n in range(3) for t in range(3)]
            for k, n, t in steps[part]:
                w, x = ((WH, xh), (WH, xl), (WL, xh))[n]
                mm = pe.matmul(PS[:, first + t, 0:TH], w[:, slot, k * P:k * P + P],
                               x[:, k - base, t * TH:t * TH + TH],
                               start=(k == chunks[0] and n == 0), stop=(k == chunks[-1] and n == 2))
            return mm

        rms_sems = {n: {k: sem(f"{n}_{k}") for k in ("sq", "mm", "rn", "ln")} for n in ("na", "nb", "nc")}

        def rms_act(act, src, r):
            for k in range(KD):
                if k >= 2:
                    act.wait_ge(r["mm"], k - 1)
                act.activation(sq[:, k % 2, :], src[:, k, :], ACT.Square).then_inc(r["sq"], 1)
            act.wait_ge(r["mm"], KD)
            act.activation(thirds(rn[:, :]), pset(0), ACT.Ln, scale=1.0 / D, bias=EPS).then_inc(r["ln"], 1)
            act.wait_ge(r["ln"], 1)
            act.activation(rn[:, :], rn[:, :], ACT.Exp, scale=-0.5).then_inc(r["rn"], 1)

        def rms_pe(pe, r):
            for k in range(KD):
                pe.wait_ge(r["sq"], k + 1)
                for t in range(3):
                    mm = pe.matmul(PS[:, t, 0:TH], const("ones"), sq[:, k % 2, t * TH:t * TH + TH],
                                   start=k == 0, stop=k == KD - 1)
                mm.then_inc(r["mm"], 1)

        xt_done, xh_done, xl_done = sem("xt_done"), sem("xh_done"), sem("xl_done")

        def norm_act(act, base):
            for k in range(KD):
                act.wait_ge(xt_done, base + k + 1)
                act.activation(XH[:, k, :], xt[:, k % 2, :], ACT.Copy).then_inc(xh_done, 1)

        hist_in, hist_a_in, state_in = sem("hist_in"), sem("hist_a_in"), sem("state_in")
        free_q, evac_q, hist_set, conv_q, silu_q, newq_set = (sem(n) for n in (
            "free_q", "evac_q", "hist_set", "conv_q", "silu_q", "newq_set"))
        out_q, out_a, out_s = sem("out_q"), sem("out_a"), sem("out_s")
        out_y = [sem("out_y0"), sem("out_y1")]
        ab_a, ab_v, ab_p, ab_t = sem("ab_a"), sem("ab_v"), sem("ab_p"), sem("ab_t")
        l2_sq, l2_mm, l2_ln, l2_rn, l2_done = (sem(n) for n in ("l2_sq", "l2_mm", "l2_ln", "l2_rn", "l2_done"))
        zeroed = sem("zeroed")
        dn_in, dn_bc, dn_b, dn_dt, dn_eg, dn_d, dn_e, dn_f, dn_g, dn_bt, dn_x, dn_xs, dn_tt, dn_t = (sem(f"dn_{n}") for n in (
            "in", "bc", "b", "dt", "eg", "d", "e", "f", "g", "bt", "x", "xs", "tt", "t"))
        dn_ks, dn_r, dn_v, dn_vs, dn_o, dn_os, dn_ds, dn_st = (sem(f"dn_{n}") for n in (
            "ks", "r", "v", "vs", "o", "os", "ds", "st"))
        dn_m, dn_vm = sem("dn_m"), sem("dn_vm")
        free_c, silu_z, on_done, oh_h, c_hist, bc_done, bh_done, bl_done = (sem(n) for n in (
            "free_c", "silu_z", "on_done", "oh_h", "c_hist", "bc_done", "bh_done", "bl_done"))
        ol_done = sem("ol_done")
        ya_done, newa_set = sem("ya_done"), sem("newa_set")
        sig_done, y_read, m_done, mh_done, ml_done = (sem(n) for n in ("sig_done", "y_read", "m_done", "mh_done", "ml_done"))
        xr_in = [sem("xr_in0"), sem("xr_in1")]
        free_h, free_w = sem("free_h"), sem("free_w")
        keys_in, qst_in, sel_mm, sel_sc, sel_read, sel_b, sel_e, sel_g, sel_t, sel_done = (sem(f"sel_{n}") for n in (
            "keys", "q", "mm", "sc", "read", "b", "e", "g", "t", "done"))
        q_out = [sem("q_out0"), sem("q_out1")]
        e_in, e_out = [sem("e_in0"), sem("e_in1")], [sem("e_out0"), sem("e_out1")]
        e_hi, e_lo, e_mm, e_gelu = (sem(n) for n in ("e_hi", "e_lo", "e_mm", "e_gelu"))
        iota_set = sem("iota_set")
        w_hot, w_mm, w_evac = sem("w_hot"), sem("w_mm"), sem("w_evac")
        w_out = [sem("w_out0"), sem("w_out1")]
        u_in, gw_in, as_in = [sem("u_in0"), sem("u_in1")], sem("gw_in"), [sem("as_in0"), sem("as_in1")]
        s_mul, s_hi, s_lo = sem("s_mul"), sem("s_hi"), sem("s_lo")
        v_in = [sem(f"v_in{k}") for k in range(4)]
        u_hi, u_lo, u_mm, a_gelu, a_mul, a_hi, a_lo = (sem(n) for n in (
            "u_hi", "u_lo", "u_mm", "a_gelu", "a_mul", "a_hi", "a_lo"))
        v_hi, v_lo, v_mm, acc_done = (sem(n) for n in ("v_hi", "v_lo", "v_mm", "acc_done"))
        y_row = sem("y_row")


        def dn(u, k):
            if u == 0:
                return DN1[:, k, :]
            return DN1[:, 12 + k, :] if k < 4 else DN2[:, k - 4, :]

        def dnh(u, k, w=P, rows=P):
            return dn(u, k)[0:rows, 0:H * w].rearrange("p (h c) -> p h c", h=H)

        def bank(b, w=P, rows=P):
            return PS[0:rows, b, 0:H * w].rearrange("p (h c) -> p h c", h=H)

        def seqs(buf, base, k, first, n):
            return buf[:, base:base + NSEQ * (SLEN + k)].rearrange(
                "p (s c) -> p s c", s=NSEQ)[:, :, first:first + n]

        KST, VST, GBC, DIFF, DT, EXPG, KB, KBG, QD, MT, QKT, KDEC = range(12)
        X, VN, TM, BT, RES, TTR, VB = VST, VST, GBC, DIFF, DIFF, DT, KB
        NPAIR = NT // 2
        LEVELS = 7
        LEVELS_S = 2

        @block.sync
        def _(sp):
            sp.dma_start(C[:, :], cst).then_inc(in_c, 16)
            sp.dma_start(SW[:, :], small).then_inc(in_w, 16)
            sp.dma_start(HID[:, :, :], xT).then_inc(in_x, 16)
            for n in range(2):
                sp.dma_start(RAW[:, n, :], wall[n]).then_inc(raw_in[n], 16)
            with sp.Fori(0, (NBLK - 3) // 2) as i:
                for r in range(2):
                    sp.wait_ge(lo_done, 2 * i + (r + 1))
                    sp.dma_start(RAW[:, r, :], wall[ds(2 * i + (r + 2), 1)].rearrange("n p c -> (n p) c")
                                 ).then_inc(raw_in[r], 16)
            sp.wait_ge(lo_done, NBLK - 2)
            sp.dma_start(RAW[:, 0, :], wall[NBLK - 1]).then_inc(raw_in[0], 16)
            for r in range(2):
                sp.sem_inc(e_out[r], 16)
            for r in range(2):
                sp.wait_ge(lo_done, NBLK - r)
                sp.dma_start(RAW[:, r, :], u_blk[r]).then_inc(e_in[r], 16)
            with sp.Fori(0, NE // 2 - 1) as i:
                for r in range(2):
                    sp.wait_ge(e_lo, 2 * i + (r + 1))
                    sp.dma_start(RAW[:, r, :], u_blk[ds(2 * i + (r + 2), 1)].rearrange("n p c -> (n p) c")
                                 ).then_inc(e_in[r], 16)
                    sp.wait_ge(e_gelu, 2 * i + (r + 2))
                    sp.dma_start(act_dram[ds(2 * i + r, 1)].rearrange("n p c -> (n p) c"), AS[:, r, :]
                                 ).then_inc(e_out[r], 16)
            for r in range(2):
                sp.wait_ge(e_lo, NE - 1 + r)
                sp.dma_start(RAW[:, r, :], u_blk[NE + r]).then_inc(u_in[r], 16)
                sp.wait_ge(e_gelu, NE + r)
                sp.dma_start(act_dram[NE - 2 + r], AS[:, r, :]).then_inc(e_out[r], 16)
            for b in range(2):
                sp.wait_ge(w_out[b], 16 * (NWB // 2 + 1))
            sp.dma_start(GW[:, :, :], w_dram[0]).then_inc(gw_in, 16)
            for r in range(2):
                sp.wait_ge(e_out[r], 16 * (NE // 2 + 1))
            for r in range(2):
                sp.dma_start(AS[:, r, :], act_dram[r]).then_inc(as_in[r], 16)
            with sp.Fori(0, NG - 1) as i:
                for r in range(2):
                    sp.wait_ge(u_lo, 2 * i + (r + 1))
                    sp.dma_start(RAW[:, r, :], u_blk[ds(2 * i + (NE + 2 + r), 1)].rearrange("n p c -> (n p) c")
                                 ).then_inc(u_in[r], 16)
                for r in range(2):
                    sp.wait_ge(s_lo, 2 * i + (r + 1))
                    sp.dma_start(AS[:, r, :], act_dram[ds(2 * i + (2 + r), 1)].rearrange("n p c -> (n p) c")
                                 ).then_inc(as_in[r], 16)
                sp.wait_ge(a_mul, 2 * i + 2)
                sp.dma_start(GW[:, :, :].rearrange("p t j -> p (t j)"),
                             w_dram[ds(i + 1, 1)].rearrange("n p t j -> (n p) (t j)")).then_inc(gw_in, 16)
            for k in range(KD):
                sp.wait_ge(y_row, k + 1)
                sp.dma_start(yT[:, k, :], xt[:, k % 2, :]).then_inc(out_y[k % 2], 16)
            for b in range(2):
                sp.wait_ge(out_y[b], 16 * (KD // 2))

        @block.gpsimd
        def _(pool):
            pool.wait_ge(xl_done, KD)
            pool.dma_start(hist[:, :, :, :], histq).then_inc(hist_in, 16)
            pool.memset(pad[:, :, 0:HQ], 0.0).then_inc(zeroed, 1)
            pool.drain().then_inc(newq_set, 2)
            pool.wait_ge(hist_in, 16)

            with pool.Fori(0, NQ // 2) as i:
                for r in range(2):
                    pool.drain()
                    pool.wait_ge(conv_q, 2 * i + (r + 1))
                    pool.tensor_copy(seqs(pad[:, r, :], HQ + SEQ, HQ, 0, HQ),
                                     hist[:, ds(2 * i + r, 1), :, :].rearrange("p n s c -> p (n s) c")
                                     ).then_inc(hist_set, 1)
                    pool.wait_ge(evac_q, 2 * i + (r + 1))
                    pool.tensor_copy(new_q[:, ds(2 * i + r, 1), 0, :].rearrange("p n c -> p (n c)"),
                                     pad[:, r, SEQ:SEQ + HQ])
                    pool.tensor_copy(new_q[:, ds(2 * i + r, 1), 1:NSEQ + 1, :].rearrange("p n s c -> p (n s) c"),
                                     seqs(pad[:, r, :], HQ + SEQ, HQ, SLEN, HQ)).then_inc(newq_set, 1)
            pool.wait_ge(newq_set, NQ + 2)
            pool.dma_start(convq_out, new_q[:, :, :, :]).then_inc(out_q, 16)
            pool.wait_ge(dn_st, NT + 1)
            pool.dma_start(sp_out, S[:, :, :]).then_inc(out_s, 16)
            pool.dma_start(SS[:, :, :, :], s_in).then_inc(state_in, 16)
            pool.wait_ge(dn_st, NT + 1 + NSEQ)
            pool.dma_start(ss_out, SS[:, :, :, :]).then_inc(out_s, 16)
            pool.wait_ge(out_s, 32)
            pool.wait_ge(out_q, 16)
            pool.dma_start(hist_a[:, :, :, :], hista).then_inc(hist_a_in, 16)
            pool.wait_ge(l2_done, 3 * H)
            pool.memset(pada[:, 0:HA], 0.0)
            pool.wait_ge(hist_a_in, 16)
            for i in range(H):
                if i:
                    pool.wait_ge(ya_done, i)
                    pool.drain()
                pool.tensor_copy(seqs(pada, HA + SEQ, HA, 0, HA), hist_a[:, i, :, :]).then_inc(c_hist, 1)
                pool.wait_ge(ya_done, i + 1)
                pool.tensor_copy(new_a[:, i, 0, :], pada[:, SEQ:SEQ + HA])
                pool.tensor_copy(new_a[:, i, 1:NSEQ + 1, :], seqs(pada, HA + SEQ, HA, SLEN, HA)).then_inc(newa_set, 1)
            pool.wait_ge(newa_set, H)
            pool.dma_start(conva_out, new_a[:, :, :, :]).then_inc(out_a, 16)
            pool.wait_ge(unit_done, filled(unit_of(B_O - 1)))
            for j in range(KD):
                if j >= 2:
                    pool.wait_ge(free_h, j + 1)
                pool.dma_start(xr[:, j % 2, :], xT[:, j, :]).then_inc(xr_in[j % 2], 16)
            pool.wait_ge(xl_done, 2 * KD)
            pool.dma_start(KEYS[:, :, :], keys).then_inc(keys_in, 16)
            pool.iota(iota_b[:, :], pattern=[[1, TOPK]], base=0, channel_multiplier=0,
                      allow_small_or_imprecise_dtypes=True).then_inc(iota_set, 1)
            for j in range(HP):
                pool.wait_ge(free_w, j + 3)
                pool.dma_start(q_dram[:, j, :], qrow[:, j % 2, :]).then_inc(q_out[j % 2], 16)
            for b in range(2):
                pool.wait_ge(q_out[b], 16 * (HP // 2))
            pool.dma_start(qst[:, :, :], q_dram[:, :, 0:P]).then_inc(qst_in, 16)
            with pool.Fori(0, NT - 1) as i:
                pool.wait_ge(sel_mm, i + 1)
                pool.dma_start(qst[:, :, :], q_dram[:, :, ds(P * i + P, P)]).then_inc(qst_in, 16)
            pool.wait_ge(sel_mm, NT)
            pool.dma_start(qst[:, :, :], q_dram[:, :, T - P:T]).then_inc(qst_in, 16)
            pool.wait_ge(sel_done, NT + 1)
            pool.iota(IOTA[:, :, :], pattern=[[1, NKEYS], [0, WS]], base=0, channel_multiplier=0,
                      allow_small_or_imprecise_dtypes=True).then_inc(iota_set, 1)
            for b in range(2):
                pool.wait_ge(w_out[b], 16 * (NWB // 2 + 1))
            for s in range(4):
                pool.dma_start(VRAW[:, s, :], v_blk[s]).then_inc(v_in[s], 16)
            with pool.Fori(0, 2 * NG - 1) as i:
                for s in range(4):
                    pool.wait_ge(v_lo, 4 * i + (s + 1))
                    pool.dma_start(VRAW[:, s, :], v_blk[ds(4 * i + (4 + s), 1)].rearrange("n p c -> (n p) c")
                                   ).then_inc(v_in[s], 16)
            pool.wait_ge(out_a, 16)

        @block.scalar
        def _(act):
            act.wait_ge(in_x, 16)
            rms_act(act, HID, rms_sems["na"])
            norm_act(act, 0)
            split_hi(act, 0, 0, 16, None)
            act.drain().then_inc(free_q, 2)
            act.drain().then_inc(silu_q, 2)
            with act.Fori(0, NQ // 2) as i:
                for r in range(2):
                    split_hi(act, None, 1 - r, 16 * i + (16 + 16 * r), 2 * i + (r + 1))
                    act.wait_ge(newq_set, 2 * i + (r + 1))
                    act.wait_ge(unit_done, 2 * i + (r + 2))
                    act.activation(pad[:, r, HQ:HQ + 2 * TH].rearrange("p (a b) -> p a b", a=2),
                                   PS[:, 3 * r:3 * r + 2, 0:TH], ACT.Copy)
                    act.activation(pad[:, r, HQ + 2 * TH:HQ + SEQ], PS[:, 3 * r + 2, 0:SEQ - 2 * TH], ACT.Copy)
                    act.activation(
                        pad[:, r, HQ + SEQ:PADQ].rearrange("p (s c) -> p s c", s=NSEQ)[:, :, HQ:HQ + SLEN],
                        PS[:, 3 * r + 2, SEQ - 2 * TH:TH].rearrange("p (s c) -> p s c", s=NSEQ), ACT.Copy
                    ).then_inc(evac_q, 1)
                    act.drain().then_inc(free_q, 1)
                    act.wait_ge(conv_q, 2 * i + (r + 3))
                    act.activation(QKV[:, ds(2 * i + r, 1), 0:SEQ].rearrange("p n t -> p (n t)"),
                                   cy[:, r, 0:SEQ], ACT.Silu)
                    act.activation(QKV[:, ds(2 * i + r, 1), SEQ:T].rearrange("p n (s c) -> p (n s) c", s=NSEQ),
                                   seqs(cy[:, r, :], HQ + SEQ, HQ, 0, SLEN), ACT.Silu).then_inc(silu_q, 1)
            split_hi(act, B_AB + 1, 1, 16 * 7, filled(B_AB - 1))
            act.wait_ge(in_w, 16)
            act.wait_ge(unit_done, filled(B_AB))
            act.activation(thirds(ab[:, 0, :]), pset(0, H), ACT.Abs, bias=SW[0:H, S_DT:S_DT + 1])
            act.activation(thirds(ab[:, 1, :]), pset(0, H), ACT.Relu, bias=SW[0:H, S_DT:S_DT + 1])
            act.activation(thirds(betaT[:, :]), PS[32:32 + H, 0:3, 0:TH], ACT.Sigmoid)
            act.drain()
            act.activation(ab[:, 2, :], ab[:, 0, :], ACT.Exp, scale=-1.0)
            act.activation(gsc[0:H, 0, 0:1], SW[0:H, S_ALOG:S_ALOG + 1], ACT.Exp)
            act.drain()
            act.activation(ab[:, 2, :], ab[:, 2, :], ACT.Ln, bias=1.0).then_inc(ab_a, 1)
            act.drain().then_inc(free_q, 1)

            def norms(first, last, src, scale):
                for c in range(first, last):
                    if c >= 2:
                        act.wait_ge(l2_mm, c - 1)
                    act.activation(sq2[:, c % 2, :], QKV[:, src(c), :], ACT.Square).then_inc(l2_sq, 1)
                    if c > first:
                        factors(c - 1, scale)
                factors(last - 1, scale)

            def factors(c, scale):
                act.wait_ge(l2_mm, c + 1)
                if c >= 2:
                    act.wait_ge(l2_done, c - 1)
                act.activation(thirds(rn2[:, c % 2, :]), pset(c % 2), ACT.Ln, scale=scale, bias=EPS).then_inc(l2_ln, 1)
                act.drain()
                act.activation(rn2[:, c % 2, :], rn2[:, c % 2, :], ACT.Exp, scale=-0.5).then_inc(l2_rn, 1)

            act.wait_ge(newq_set, NQ + 2)
            norms(0, 2 * H, lambda c: c, 1.0)

            def dn_exps(u, n, w):
                act.wait_ge(dn_dt, n)
                act.activation(dnh(u, EXPG, w), bank(3 * u, w), ACT.Exp)
                act.activation(ekd[0:w, u, :], PS[0:w, 3 * u + 2, H:2 * H], ACT.Exp)
                act.activation(dnh(u, DT, w, w), dnh(u, DIFF, w, w), ACT.Exp).then_inc(dn_eg, 1)

            def dn_scaled(u, n, w):
                act.wait_ge(dn_e, n)
                for h in range(H):
                    act.activation(dnh(u, VB, P, w)[:, h, :], PS[0:w, 3 * u, h * P:h * P + P], ACT.Copy,
                                   scale=gbt[0:w, u, H + h:H + h + 1])
                    ins = act.activation(dnh(u, KDEC, P, w)[:, h, :], PS[0:w, 6 + u, h * P:h * P + P], ACT.Copy,
                                         scale=ekd[0:w, u, h:h + 1])
                ins.then_inc(dn_g, 1)

            def dn_evac_x(u, n, w):
                act.wait_ge(dn_x, n)
                act.activation(dnh(u, X, w, w), bank(3 * u, w, w), ACT.Copy).then_inc(dn_xs, 1)

            def dn_evac_v(u, n, w):
                act.wait_ge(dn_v, n)
                act.activation(dnh(u, VN, P, w), bank(7, P, w), ACT.Copy).then_inc(dn_vs, 1)

            def dn_evac_o(u, n, w, cols):
                act.wait_ge(dn_o, n)
                act.activation(QKV[:, 0:H, cols], bank(3 * u, w), ACT.Copy).then_inc(dn_os, 1)

            act.drain().then_inc(dn_os, 2)
            with act.Fori(0, NPAIR) as i:
                for u in range(2):
                    dn_exps(u, 2 * i + (u + 1), P)
                for u in range(2):
                    dn_scaled(u, 2 * i + (u + 1), P)
                for l in range(LEVELS):
                    for u in range(2):
                        dn_evac_x(u, 2 * LEVELS * i + (2 * l + u + 1), P)
                for u in range(2):
                    dn_evac_v(u, 2 * i + (u + 1), P)
                    dn_evac_o(u, 2 * i + (u + 1), P, ds(2 * P * i + P * u, P))
            dn_exps(0, NT + 1, TS)
            dn_scaled(0, NT + 1, TS)
            for l in range(LEVELS_S):
                dn_evac_x(0, NT * LEVELS + l + 1, TS)
            dn_evac_v(0, NT + 1, TS)
            dn_evac_o(0, NT + 1, TS, slice(SEQ, T))
            act.drain()
            act.wait_ge(dn_st, NT + 1 + NSEQ)

            norms(2 * H, 3 * H, lambda c: c - 2 * H, 1.0 / P)
            for h in range(H):
                n = B_Z + h
                split_hi(act, n + 1, (n + 1) % 2, 16 * ((n + 1) // 2 + 1), filled(n - 1))
                act.wait_ge(unit_done, filled(n))
                if h >= 2:
                    act.wait_ge(on_done, h - 1)
                if h == 0:
                    act.wait_ge(l2_done, 3 * H)
                act.activation(thirds(zs[:, h % 2, :]), pset(n % 2), ACT.Silu).then_inc(silu_z, 1)
                act.wait_ge(on_done, h + 1)
                act.activation(OH[:, h, :], on[:, h % 2, :], ACT.Copy).then_inc(oh_h, 1)
            for i in range(H):
                for r in range(3):
                    n = B_CONV + 3 * i + r
                    split_hi(act, n + 1, (n + 1) % 2, 16 * ((n + 1) // 2 + 1), filled(n - 1))
                act.wait_ge(bc_done, i + 1)
                act.activation(BH[:, i, :], bc[:, :], ACT.Copy).then_inc(bh_done, 1)
            act.wait_ge(out_a, 16)
            act.wait_ge(bl_done, H)
            with act.Fori(0, KD // 2) as i:
                for q in range(2):
                    for r in range(3):
                        nxt = B_Y + 3 * q + r + 1
                        split_hi(act, None, nxt % 2, 48 * i + 16 * (nxt // 2 + 1),
                                 8 * i + filled(B_Y + 4 * q + (-1, 0, 1)[r]))
                        if r < 2:
                            if r == 0:
                                act.wait_ge(m_done, 2 * i + (q + 1))
                            act.wait_ge(unit_done, 8 * i + filled(B_Y + 4 * q + r))
                            act.activation(thirds(sig[:, r, :]), pset(1 - r), ACT.Sigmoid).then_inc(sig_done, 1)
            act.wait_ge(m_done, KD + 1)
            act.wait_ge(unit_done, filled(unit_of(B_O - 1)))
            for k in range(KD):
                act.activation(XH[:, k, :], HID[:, k, :], ACT.Copy).then_inc(mh_done, 1)
            with act.Fori(0, KD // 2) as i:
                for r in range(2):
                    nxt = B_O + r + 1
                    split_hi(act, None, nxt % 2, 16 * i + 16 * (nxt // 2 + 1),
                             2 * i + filled(unit_of(B_O) + r - 1))
            act.wait_ge(free_h, KD + 2)
            rms_act(act, HID, rms_sems["nb"])
            norm_act(act, KD)
            act.drain().then_inc(free_w, 2)
            for j in range(HP):
                n = B_WQ + j
                if n + 1 < NBLK:
                    split_hi(act, n + 1, (n + 1) % 2, 16 * ((n + 1) // 2 + 1), filled(unit_of(n - 1)))
                if j >= 2:
                    act.wait_ge(q_out[j % 2], 16 * (j // 2))
                act.wait_ge(unit_done, filled(unit_of(n)))
                act.activation(thirds(qrow[:, j % 2, :]), pset(n % 2), ACT.Copy).then_inc(free_w, 1)

            def e_split(slot, used, reads):
                act.wait_ge(e_in[slot], reads)
                act.wait_ge(e_mm, used)
                act.activation(WH[:, slot, :], RAW[:, slot, :], ACT.Copy).then_inc(e_hi, 1)

            def e_block(n, slot, reads, more=True):
                if more:
                    e_split(1 - slot, n + 2, reads + 16 * slot)
                act.wait_ge(e_out[slot], reads)
                act.wait_ge(e_mm, n + 3)
                act.activation(thirds(AS[:, slot, :]), PS[:, 5:8, 0:TH], ACT.Gelu).then_inc(e_gelu, 1)

            def sel_scores():
                act.activation(sc[:, :, :].rearrange("p (b n) k -> p b (n k)", b=4), PS[:, 0:4, :],
                               ACT.Copy).then_inc(sel_sc, 1)

            act.drain().then_inc(e_gelu, 1)
            act.wait_ge(unit_done, filled(unit_of(NBLK - 1)))
            e_split(0, 2, 16)
            act.wait_ge(sel_mm, 1)
            sel_scores()

            def sel_act(i, last):
                for r in range(SEL_E):
                    e_block(SEL_E * i + r, r % 2, 16 * (SEL_E // 2) * i + 16 * (r // 2 + 1))
                    if r == 0 and not last:
                        act.wait_ge(sel_mm, i + 2)
                        act.wait_ge(sel_read, i + 1)
                        sel_scores()
                    if r == 2:
                        act.wait_ge(sel_b, i + 1)
                        act.activation(gate[:, :], gate[:, :], ACT.Exp).then_inc(sel_e, 1)

            with act.Fori(0, NT) as i:
                sel_act(i, False)
            sel_act(NT, True)

            act.drain().then_inc(w_evac, 2)
            for b in range(2):
                act.sem_inc(w_out[b], 16)
            with act.Fori(0, NWB // 2) as i:
                for b in range(2):
                    act.wait_ge(w_out[b], 16 * i + 16)
                    for s in range(WT // WS):
                        act.wait_ge(w_mm, 12 * i + (6 * b + s + 3))
                        act.activation(stg[:, b, :, s * WS:s * WS + WS, :].rearrange("p q t j -> p t q j"),
                                       PS[:, 2 * (s % 2):2 * (s % 2) + 2, :].rearrange(
                                           "p b (t q j) -> p (b t) q j", t=4, j=GE), ACT.Copy, scale=1.0 / GSCALE
                                       ).then_inc(w_evac, 1)
                        if s == 1:
                            e_split(1 - b, WM_E * i + (E0 + b + 2), 16 * i + 8 * (E0 + 2) + 16 * b)
                    act.wait_ge(w_evac, 12 * i + (6 * b + 8))
                    act.dma_start(w_dram[:, :, ds(2 * WT * i + WT * b, WT), :].rearrange("q p t j -> p q (t j)"),
                                  stg[:, b, :, :, :].rearrange("p q t j -> p q (t j)")).then_inc(w_out[b], 16)
                    e_block(WM_E * i + (E0 + b), b, 16 * i + 8 * (E0 + 2), False)
            for n in range(E0 + WM_E * (NWB // 2), NE):
                e_block(n, n % 2, 16 * (n // 2 + 1), n + 1 < NE)

            def u_split(slot, reads, used=None):
                act.wait_ge(u_in[slot], reads)
                if used is not None:
                    act.wait_ge(u_mm, used)
                act.activation(WH[:, slot, :], RAW[:, slot, :], ACT.Copy).then_inc(u_hi, 1)

            def v_split(d, reads, before):
                act.wait_ge(v_in[d % 4], reads)
                act.wait_ge(v_mm, before)
                act.activation(VH[:, d % 2, :], VRAW[:, d % 4, :], ACT.Copy).then_inc(v_hi, 1)

            act.wait_ge(e_mm, NE + 2)
            u_split(0, 16)
            u_split(1, 16)

            def group_act(g, last):
                act.wait_ge(v_mm, 8 * g + 2)
                for e in range(EARLY):
                    act.wait_ge(s_mul, 2 * g + (e + 1))
                    act.activation(AH[:, e, :], AS[:, e, :], ACT.Copy).then_inc(s_hi, 1)
                for d in range(2):
                    v_split(d, 32 * g + 16, 8 * g + (d + 1))
                for c in range(LATE):
                    act.wait_ge(u_mm, 2 * g + (c + 1))
                    act.activation(thirds(AF[:, EARLY + c, :]), pset(c), ACT.Gelu).then_inc(a_gelu, 1)
                    if c == 0 and not last:
                        u_split(0, 16 * g + 32, 2 * g + 1)
                    act.wait_ge(a_mul, 2 * g + (c + 1))
                    act.activation(AH[:, EARLY + c, :], AF[:, EARLY + c, :], ACT.Copy).then_inc(a_hi, 1)
                if not last:
                    u_split(1, 16 * g + 32, 2 * g + 2)
                for d in range(2, 8):
                    v_split(d, 32 * g + 16 * (d // 4 + 1), 8 * g + (d + 1))

            with act.Fori(0, NG - 1) as g:
                group_act(g, False)
            group_act(NG - 1, True)
            act.wait_ge(acc_done, 8 * NG + 2)
            rms_act(act, HID, rms_sems["nc"])

        @block.tensor
        def _(pe):
            pe.drain().then_inc(unit_done, 1)
            pe.wait_ge(in_c, 16)
            rms_pe(pe, rms_sems["na"])
            pe.wait_ge(xl_done, KD)
            pe.wait_ge(rms_sems["na"]["rn"], 1)
            with pe.Fori(0, NQ // 2) as i:
                for r in range(2):
                    pe.wait_ge(lo_done, 2 * i + (r + 1))
                    pe.wait_ge(free_q, 2 * i + (r + 1))
                    products(pe, r, r, XH, XL).then_inc(unit_done, 1)
            pe.wait_ge(lo_done, B_AB + 1)
            pe.wait_ge(free_q, B_AB + 1)
            products(pe, 0, 0, XH, XL).then_inc(unit_done, 1)
            pe.wait_ge(ab_v, 1)
            for t in range(NT + 1):
                w = P if t < NT else TS
                for k, src in enumerate((ab[:, 3, :], betaT[:, :])):
                    mm = pe.matmul(PS[0:w, 6, 8 * t + H * k:8 * t + H * k + H], src[:, t * P:t * P + w],
                                   C[0:H, 0:H], start=True, stop=True)
            mm.then_inc(ab_p, 1)

            def norms(first, last):
                for c in range(first, last):
                    pe.wait_ge(l2_sq, c + 1)
                    if c >= 2:
                        pe.wait_ge(l2_ln, c - 1)
                    for t in range(3):
                        mm = pe.matmul(PS[:, 3 * (c % 2) + t, 0:TH], const("ones"),
                                       sq2[:, c % 2, t * TH:t * TH + TH], start=True, stop=True)
                    mm.then_inc(l2_mm, 1)

            norms(0, 2 * H)

            def mm4(out, lhs, rhs, start=True, stop=True):
                for h in range(H):
                    ins = pe.matmul(out(h), lhs(h), rhs(h), start=start, stop=stop)
                return ins

            def dn_cum(u, n, w, cols, sfx):
                upto, after = const("upto" + sfx, w)[:, 0:w], const("after" + sfx, w)[:, 0:w]
                pe.wait_ge(dn_in, n)
                pe.wait_ge(dn_os, n)
                mm4(lambda h: bank(3 * u, w)[:, h, :], lambda h: dnh(u, GBC, P, w)[:, h, :], lambda h: upto)
                mm4(lambda h: bank(3 * u + 1, w)[:, h, :], lambda h: const("sel", H)[:, h * P:h * P + P],
                    lambda h: betaT[:, cols])
                pe.matmul(PS[0:w, 3 * u + 2, 0:H], upto, gbt[0:w, u, 0:H], start=True, stop=True)
                pe.matmul(PS[0:w, 3 * u + 2, H:2 * H], after, gbt[0:w, u, 0:H], start=True, stop=True
                          ).then_inc(dn_bc, 1)

            def dn_pairs(u, n, w, cols):
                pe.wait_ge(dn_d, n)
                kst = dnh(u, KST, w)
                mm4(lambda h: bank(3 * u + 1, w, w)[:, h, :], lambda h: kst[:, h, :], lambda h: dnh(u, KB, w)[:, h, :])
                mm4(lambda h: bank(3 * u + 2, w, w)[:, h, :], lambda h: kst[:, h, :], lambda h: QKV[:, h, cols])
                mm4(lambda h: bank(3 * u, P, w)[:, h, :], lambda h: dnh(u, VST, w)[:, h, :], lambda h: const("ident"))
                mm4(lambda h: bank(6 + u, P, w)[:, h, :], lambda h: kst[:, h, :], lambda h: const("ident")
                    ).then_inc(dn_e, 1)

            def dn_level_x(u, w, ready, g):
                pe.wait_ge(dn_t, ready)
                if g is not None:
                    pe.wait_ge(dn_g, g)
                mm4(lambda h: bank(3 * u, w, w)[:, h, :], lambda h: dnh(u, BT, w, w)[:, h, :],
                    lambda h: dnh(u, TM, w, w)[:, h, :]).then_inc(dn_x, 1)

            def dn_level_t(u, w, n, last):
                pe.wait_ge(dn_xs, n)
                x, tt = dnh(u, X, w, w), dnh(u, TTR, w, w)
                if not last:
                    mm4(lambda h: bank(3 * u + 1, w, w)[:, h, :], lambda h: tt[:, h, :], lambda h: x[:, h, :])
                mm4(lambda h: bank(3 * u + 2, w, w)[:, h, :], lambda h: x[:, h, :], lambda h: tt[:, h, :]
                    ).then_inc(dn_tt, 1)

            pe.wait_ge(ab_t, 1)
            with pe.Fori(0, NPAIR) as i:
                for u in range(2):
                    dn_cum(u, 2 * i + (u + 1), P, ds(2 * P * i + P * u, P), "")
                for u in range(2):
                    dn_pairs(u, 2 * i + (u + 1), P, ds(2 * P * i + P * u, P))
                for l in range(LEVELS):
                    for u in range(2):
                        dn_level_x(u, P, 2 * (LEVELS + 1) * i + (2 * l + u + 1), 2 * i + (u + 1) if l == 0 else None)
                    for u in range(2):
                        dn_level_t(u, P, 2 * LEVELS * i + (2 * l + u + 1), l == LEVELS - 1)
                for u in range(2):
                    pe.wait_ge(dn_st, 2 * i + (u + 1))
                    mm4(lambda h: bank(6)[:, h, :], lambda h: dnh(u, KBG)[:, h, :], lambda h: S[:, h, :]).then_inc(dn_ks, 1)
                    pe.wait_ge(dn_r, 2 * i + (u + 1))
                    mm4(lambda h: bank(7)[:, h, :], lambda h: dnh(u, TTR)[:, h, :], lambda h: dnh(u, RES)[:, h, :]).then_inc(dn_v, 1)
                    pe.wait_ge(dn_vs, 2 * i + (u + 1))
                    for h in range(H):
                        pe.matmul(bank(3 * u)[:, h, :], S[:, h, :], dnh(u, QD)[:, h, :], start=True, stop=False)
                        mm = pe.matmul(bank(3 * u)[:, h, :], dnh(u, VN)[:, h, :], dnh(u, QKT)[:, h, :], start=False, stop=True)
                    mm.then_inc(dn_o, 1)
                    mm4(lambda h: bank(6)[:, h, :], lambda h: dnh(u, KDEC)[:, h, :], lambda h: dnh(u, VN)[:, h, :]).then_inc(dn_ds, 1)
            dn_cum(0, NT + 1, TS, slice(SEQ, T), "_s")
            dn_pairs(0, NT + 1, TS, slice(SEQ, T))
            for l in range(LEVELS_S):
                dn_level_x(0, TS, NT * (LEVELS + 1) + l + 1, NT + 1 if l == 0 else None)
                dn_level_t(0, TS, NT * LEVELS + l + 1, l == LEVELS_S - 1)
            pe.wait_ge(dn_m, 1)
            pe.wait_ge(state_in, 16)
            for h in range(H):
                for s in range(NSEQ):
                    mm = pe.matmul(PS[0:TS, 6, h * P:h * P + P], kbgm[:, h, s, :], SS[:, s, h, :],
                                   start=s == 0, stop=s == NSEQ - 1)
            mm.then_inc(dn_ks, 1)
            pe.wait_ge(dn_r, NT + 1)
            mm4(lambda h: bank(7, P, TS)[:, h, :], lambda h: dnh(0, TTR, TS, TS)[:, h, :],
                lambda h: dnh(0, RES, P, TS)[:, h, :]).then_inc(dn_v, 1)
            pe.wait_ge(dn_vs, NT + 1)
            for h in range(H):
                for s in range(NSEQ):
                    pe.matmul(bank(0, TS)[:, h, :], SS[:, s, h, :], qdm[:, h, s, :], start=s == 0, stop=False)
                mm = pe.matmul(bank(0, TS)[:, h, :], dnh(0, VN, P, TS)[:, h, :], dnh(0, QKT, TS, TS)[:, h, :],
                               start=False, stop=True)
            mm.then_inc(dn_o, 1)
            for s in range(NSEQ):
                pe.wait_ge(dn_vm, s + 1)
                if s >= 2:
                    pe.wait_ge(dn_st, NT + 1 + s - 1)
                vm = dnh(0, (TM, TTR)[s % 2], P, TS)
                mm4(lambda h: bank(6 + s % 2)[:, h, :], lambda h: dnh(0, KDEC, P, TS)[:, h, :],
                    lambda h: vm[:, h, :]).then_inc(dn_ds, 1)

            pe.wait_ge(dn_st, NT + 1 + NSEQ)
            norms(2 * H, 3 * H)
            pe.wait_ge(l2_rn, 3 * H)
            with pe.Fori(0, (B_Y - B_Z) // 2) as i:
                for r in range(2):
                    pe.wait_ge(lo_done, 2 * i + (B_Z + r + 1))
                    pe.wait_ge(free_c, 2 * i + (r + 1))
                    products(pe, 1 - r, 1 - r, XH, XL).then_inc(unit_done, 1)
            pe.wait_ge(ol_done, H)
            pe.wait_ge(bl_done, H)
            with pe.Fori(0, KD // 2) as i:
                for q in range(2):
                    for r in range(2):
                        pe.wait_ge(lo_done, 6 * i + (B_Y + 3 * q + r + 1))
                        pe.wait_ge(y_read, 4 * i + (2 * q + r + 1))
                        products(pe, (1 + q + r) % 2, 1 - r, XH, XL).then_inc(unit_done, 1)
                    pe.wait_ge(lo_done, 6 * i + (B_Y + 3 * q + 3))
                    pe.wait_ge(sig_done, 4 * i + (2 * q + 1))
                    products(pe, (1 + q) % 2, 1, BH, BL, range(0, H)).then_inc(unit_done, 1)
                    pe.wait_ge(sig_done, 4 * i + (2 * q + 2))
                    products(pe, (1 + q) % 2, 0, OH, OL, range(H, KD), H).then_inc(unit_done, 1)
            pe.wait_ge(ml_done, KD)
            with pe.Fori(0, KD // 2) as i:
                for r in range(2):
                    pe.wait_ge(lo_done, 2 * i + (B_O + r + 1))
                    pe.wait_ge(free_h, 2 * i + (r + 1))
                    products(pe, 1 - r, 1 - r, XH, XL).then_inc(unit_done, 1)
            rms_pe(pe, rms_sems["nb"])
            pe.wait_ge(xl_done, 2 * KD)
            with pe.Fori(0, HP // 2) as i:
                for r in range(2):
                    pe.wait_ge(lo_done, 2 * i + (B_WQ + r + 1))
                    pe.wait_ge(free_w, 2 * i + (r + 1))
                    products(pe, 1 - r, 1 - r, XH, XL).then_inc(unit_done, 1)

            def sel_scores(n):
                pe.wait_ge(qst_in, 16 * n + 16)
                for h in range(HP):
                    mm = pe.matmul(PS[:, h // 2, (h % 2) * 256:(h % 2) * 256 + 256], qst[:, h, :],
                                   KEYS[:, h, :], start=True, stop=True)
                mm.then_inc(sel_mm, 1)

            def e_block(n, slot, part=slice(None)):
                if not part.start:
                    pe.wait_ge(e_lo, n + 1)
                    pe.wait_ge(e_gelu, n + 1)
                mm = products(pe, slot, 0, XH, XL, bank=5, part=part)
                if part.stop is None:
                    mm.then_inc(e_mm, 1)

            def sel_pe(i, last):
                for r in range(SEL_E):
                    e_block(SEL_E * i + r, r % 2)
                    if r == 0 and not last:
                        pe.wait_ge(sel_sc, i + 1)
                        sel_scores(i + 1)
                pe.wait_ge(sel_g, i + 1)
                for k, x in enumerate((e1, e2, gate)):
                    mm = pe.matmul(PS[:, 4, k * P:k * P + P], x[:, :], const("ident"), start=True, stop=True)
                mm.then_inc(sel_t, 1)

            pe.wait_ge(keys_in, 16)
            pe.wait_ge(free_w, HP + 2)
            pe.drain().then_inc(e_mm, 2)
            sel_scores(0)
            with pe.Fori(0, NT) as i:
                sel_pe(i, False)
            sel_pe(NT, True)

            pe.wait_ge(sel_done, NT + 1)
            pe.drain().then_inc(w_mm, 2)
            parts = 2 * WT // WS
            each = KD * 9 * WM_E // parts
            with pe.Fori(0, NWB // 2) as i:
                for s in range(parts):
                    pe.wait_ge(w_hot, 12 * i + (s + 1))
                    pe.wait_ge(w_evac, 12 * i + (s + 1))
                    for t in range(WS):
                        for k in range(2):
                            mm = pe.matmul(PS[:, 2 * (s % 2) + t // 4, (t % 4) * P:(t % 4) * P + P],
                                           HOT1[:, s % 2, :, t], HOTG[:, s % 2, k, :, t], start=k == 0, stop=k == 1)
                    mm.then_inc(w_mm, 1)
                    e, v = divmod(s, parts // WM_E)
                    stop = None if v == parts // WM_E - 1 else each * (v + 1)
                    e_block(WM_E * i + (E0 + e), e, slice(each * v, stop))
            for n in range(E0 + WM_E * (NWB // 2), NE):
                e_block(n, n % 2)

            pe.wait_ge(e_gelu, NE + 1)
            pe.drain().then_inc(v_mm, 2)

            def group_pe(g):
                for c in range(LATE):
                    pe.wait_ge(u_lo, 2 * g + (c + 1))
                    pe.wait_ge(acc_done, 8 * g + (c + 1))
                    products(pe, c, c, XH, XL).then_inc(u_mm, 1)
                for d in range(8):
                    pe.wait_ge(v_lo, 8 * g + (d + 1))
                    if d < 2:
                        pe.wait_ge(a_gelu, 2 * g + (d + 1))
                    else:
                        pe.wait_ge(acc_done, 8 * g + (d + 1))
                    for c in range(GE):
                        if d == 0 and c == 0:
                            pe.wait_ge(s_lo, 2 * g + EARLY)
                        if d == 0 and c >= EARLY:
                            pe.wait_ge(a_lo, 2 * g + (c - EARLY + 1))
                        for n, (w, x) in enumerate(((VH, AH), (VH, AL), (VL, AH))):
                            for t in range(3):
                                mm = pe.matmul(PS[:, 3 * (d % 2) + t, 0:TH], w[:, d % 2, c * P:c * P + P],
                                               x[:, c, t * TH:t * TH + TH],
                                               start=(c == 0 and n == 0), stop=(c == GE - 1 and n == 2))
                    mm.then_inc(v_mm, 1)

            with pe.Fori(0, NG) as g:
                group_pe(g)
            pe.wait_ge(acc_done, 8 * NG + 2)
            rms_pe(pe, rms_sems["nc"])

        @block.vector
        def _(dve):
            def norm(src, r, col, base):
                dve.wait_ge(r["rn"], 1)

                def low(k):
                    dve.wait_ge(xh_done, base + k + 1)
                    dve.tensor_tensor(XL[:, k, :], xt[:, k % 2, :], XH[:, k, :].bitcast(F32),
                                      ALU.subtract).then_inc(xl_done, 1)

                for k in range(KD):
                    if k >= 2:
                        dve.drain()
                    dve.scalar_tensor_tensor(out=xt[:, k % 2, :], in0=src[:, k, :],
                                             scalar=SW[:, col + k:col + k + 1], in1=rn[:, :],
                                             op0=ALU.mult, op1=ALU.mult).then_inc(xt_done, 1)
                    if k >= 1:
                        low(k - 1)
                low(KD - 1)

            dve.wait_ge(in_w, 16)
            norm(HID, rms_sems["na"], S_MIX, 0)
            split_lo(dve, 1, 0)
            dve.drain().then_inc(conv_q, 2)
            dve.wait_ge(zeroed, 1)
            LQ = PADQ - HQ
            with dve.Fori(0, NQ // 2) as i:
                for r in range(2):
                    split_lo(dve, 2 * i + (r + 2), 1 - r)
                    dve.wait_ge(hist_set, 2 * i + (r + 1))
                    dve.wait_ge(silu_q, 2 * i + (r + 1))
                    dve.wait_ge(evac_q, 2 * i + (r + 1))
                    for t in range(HQ + 1):
                        weight = SW[:, ds(8 * i + (S_CQ + 4 * r + t), 1)]
                        if t == 0:
                            dve.tensor_scalar(cy[:, r, 0:LQ], pad[:, r, 0:LQ], weight, None, ALU.mult)
                        else:
                            dve.drain()
                            ins = dve.scalar_tensor_tensor(out=cy[:, r, 0:LQ], in0=pad[:, r, t:t + LQ], scalar=weight,
                                                           in1=cy[:, r, 0:LQ], op0=ALU.mult, op1=ALU.add)
                    ins.then_inc(conv_q, 1)
            split_lo(dve, B_AB + 2, 1)
            dve.wait_ge(ab_a, 1)
            dve.tensor_tensor(ab[:, 3, :], ab[:, 1, :], ab[:, 2, :], ALU.add)
            dve.drain()
            dve.tensor_scalar(ab[:, 3, :], ab[:, 3, :], gsc[0:H, 0, 0:1], -1.0, ALU.mult, ALU.mult).then_inc(ab_v, 1)
            dve.wait_ge(ab_p, 1)
            dve.tensor_copy(gb_tok[:, 0:NT, :].rearrange("p t c -> p (t c)"), PS[:, 6, 0:8 * NT])
            dve.tensor_copy(gb_tok[0:TS, NT, :], PS[0:TS, 6, 8 * NT:8 * NT + 8]).then_inc(ab_t, 1)

            def norms(first, last, row, weight):
                for c in range(first, last):
                    dve.wait_ge(l2_rn, c + 1)
                    dve.scalar_tensor_tensor(out=QKV[:, row(c), :], in0=rn2[:, c % 2, :], scalar=weight(c),
                                             in1=QKV[:, row(c), :], op0=ALU.mult, op1=ALU.mult).then_inc(l2_done, 1)

            norms(0, 2 * H, lambda c: c, lambda c: float(P) ** -0.5 if c < H else 1.0)
            dve.drain()

            def dn_inputs(u, w, cols, tile):
                dve.tensor_copy(dnh(u, KST, w), QKV[:, H:2 * H, cols])
                dve.tensor_copy(dnh(u, VST, w), QKV[:, 2 * H:3 * H, cols])
                dve.tensor_copy(gbt[0:w, u, :], tile)
                dve.tensor_copy(dnh(u, GBC, P, w), tile[:, 0:H].unsqueeze(2).broadcast_to([w, H, P])).then_inc(dn_in, 1)

            def dn_diff(u, n, w, sfx):
                dve.wait_ge(dn_bc, n)
                dve.tensor_copy(gsc[0:w, u, :], PS[0:w, 3 * u + 2, 0:H])
                dve.tensor_tensor(dnh(u, KB, w), dnh(u, KST, w), bank(3 * u + 1, w), ALU.mult)
                dve.drain()
                for h in range(H):
                    ins = dve.scalar_tensor_tensor(
                        out=dnh(u, DIFF, w, w)[:, h, :], in0=bank(3 * u, w, w)[:, h, :], scalar=gsc[0:w, u, h:h + 1],
                        in1=const("neg" + sfx, w)[:, 0:w], op0=ALU.subtract, op1=ALU.add)
                ins.then_inc(dn_dt, 1)

            def dn_decay(u, n, w, cols):
                dve.wait_ge(dn_eg, n)
                dve.tensor_tensor(dnh(u, KBG, w), dnh(u, KB, w), dnh(u, EXPG, w), ALU.mult)
                dve.tensor_tensor(dnh(u, QD, w), QKV[:, 0:H, cols], dnh(u, EXPG, w), ALU.mult).then_inc(dn_d, 1)

            def mask(l, w, sfx):
                return const(f"mask{l}{sfx}", w)[:, 0:w].unsqueeze(1).broadcast_to([w, H, w])

            def dn_start(u, n, w, sfx):
                dve.wait_ge(dn_e, n)
                dve.tensor_tensor(dnh(u, MT, w, w), bank(3 * u + 1, w, w), dnh(u, DT, w, w), ALU.mult)
                dve.tensor_tensor(dnh(u, QKT, w, w), bank(3 * u + 2, w, w), dnh(u, DT, w, w), ALU.mult)
                dve.drain()
                unit = const("ident", w)[:, 0:w].unsqueeze(1).broadcast_to([w, H, w])
                dve.tensor_copy(dnh(u, TM, w, w), unit)
                dve.tensor_copy(dnh(u, TTR, w, w), unit)
                dve.tensor_tensor(dnh(u, BT, w, w), dnh(u, MT, w, w), mask(0, w, sfx), ALU.mult).then_inc(dn_t, 1)

            def dn_update(u, n, w, l, last, sfx):
                dve.wait_ge(dn_tt, n)
                if not last:
                    dve.tensor_tensor(dnh(u, TM, w, w), dnh(u, TM, w, w), bank(3 * u + 1, w, w), ALU.subtract)
                    dve.tensor_tensor(dnh(u, BT, w, w), dnh(u, MT, w, w), mask(l + 1, w, sfx), ALU.mult)
                dve.tensor_tensor(dnh(u, TTR, w, w), dnh(u, TTR, w, w), bank(3 * u + 2, w, w), ALU.subtract
                                  ).then_inc(dn_t, 1)

            def dn_residual(u, n, w, g):
                dve.wait_ge(dn_g, g)
                dve.wait_ge(dn_ks, n)
                dve.tensor_tensor(dnh(u, RES, P, w), dnh(u, VB, P, w), bank(6, P, w), ALU.subtract).then_inc(dn_r, 1)

            dve.wait_ge(out_q, 16)
            dve.memset(S[:, :, :], 0.0).then_inc(dn_st, 1)
            with dve.Fori(0, NPAIR) as i:
                dve.drain()
                for u in range(2):
                    dn_inputs(u, P, ds(2 * P * i + P * u, P), gb_tok[:, ds(2 * i + u, 1), :].rearrange("p n c -> p (n c)"))
                for u in range(2):
                    dn_diff(u, 2 * i + (u + 1), P, "")
                for u in range(2):
                    dn_decay(u, 2 * i + (u + 1), P, ds(2 * P * i + P * u, P))
                for u in range(2):
                    dn_start(u, 2 * i + (u + 1), P, "")
                for l in range(LEVELS):
                    for u in range(2):
                        dn_update(u, 2 * LEVELS * i + (2 * l + u + 1), P, l, l == LEVELS - 1, "")
                for u in range(2):
                    dn_residual(u, 2 * i + (u + 1), P, 2 * i + 2)
                    dve.wait_ge(dn_ds, 2 * i + (u + 1))
                    for h in range(H):
                        ins = dve.scalar_tensor_tensor(out=S[:, h, :], in0=S[:, h, :], scalar=dnh(u, EXPG)[:, h, P - 1:P],
                                                       in1=bank(6)[:, h, :], op0=ALU.mult, op1=ALU.add)
                    ins.then_inc(dn_st, 1)
            dve.drain()
            dn_inputs(0, TS, slice(SEQ, T), gb_tok[0:TS, NT, :])
            dn_diff(0, NT + 1, TS, "_s")
            dn_decay(0, NT + 1, TS, slice(SEQ, T))
            dve.drain()
            seqcol = const("seqcol").rearrange("p (s c) -> p s c", s=NSEQ)
            for src, dst in ((KBG, kbgm), (QD, qdm)):
                for h in range(H):
                    ins = dve.tensor_tensor(dst[:, h, :, :], dnh(0, src, TS)[:, h, :].unsqueeze(1).broadcast_to([P, NSEQ, TS]),
                                            seqcol, ALU.mult)
            ins.then_inc(dn_m, 1)
            dn_start(0, NT + 1, TS, "_s")
            for l in range(LEVELS_S):
                dn_update(0, NT * LEVELS + l + 1, TS, l, l == LEVELS_S - 1, "_s")
            dn_residual(0, NT + 1, TS, NT + 1)
            dve.wait_ge(dn_vs, NT + 1)
            for s in range(NSEQ + 1):
                if s < NSEQ:
                    if s >= 2:
                        dve.wait_ge(dn_ds, NT + s - 1)
                    dve.tensor_scalar(dnh(0, (TM, TTR)[s % 2], P, TS), dnh(0, VN, P, TS), const("seqrow", TS)[:, s:s + 1],
                                      None, ALU.mult).then_inc(dn_vm, 1)
                if s >= 1:
                    dve.wait_ge(dn_ds, NT + s)
                    for h in range(H):
                        last = SLEN * s - 1
                        ins = dve.scalar_tensor_tensor(
                            out=SS[:, s - 1, h, :], in0=SS[:, s - 1, h, :], scalar=dnh(0, EXPG, TS)[:, h, last:last + 1],
                            in1=bank(6 + (s - 1) % 2)[:, h, :], op0=ALU.mult, op1=ALU.add)
                    ins.then_inc(dn_st, 1)
            norms(2 * H, 3 * H, lambda c: c - 2 * H, lambda c: SW[:, S_DN:S_DN + 1])
            dve.wait_ge(out_s, 32)
            dve.drain().then_inc(free_c, 2)
            for h in range(H):
                n = B_Z + h
                split_lo(dve, n + 2, (n + 1) % 2)
                dve.wait_ge(silu_z, h + 1)
                dve.tensor_tensor(on[:, h % 2, :], QKV[:, h, :], zs[:, h % 2, :], ALU.mult).then_inc(on_done, 1)
                dve.drain().then_inc(free_c, 1)
                dve.wait_ge(oh_h, h + 1)
                dve.tensor_tensor(OL[:, h, :], on[:, h % 2, :], OH[:, h, :].bitcast(F32), ALU.subtract).then_inc(ol_done, 1)
            LA = PADA - HA
            for i in range(H):
                n = B_CONV + 3 * i
                st = n % 2
                split_lo(dve, n + 2, (n + 1) % 2)
                dve.wait_ge(unit_done, filled(n))
                dve.tensor_copy(thirds(cbuf[:, :]), pset(st)).then_inc(free_c, 1)
                split_lo(dve, n + 3, n % 2)
                dve.wait_ge(unit_done, filled(n + 1))
                if i:
                    dve.wait_ge(newa_set, i)
                dve.drain()
                dve.tensor_tensor(pada[:, HA:HA + 2 * TH].rearrange("p (a b) -> p a b", a=2),
                                  PS[:, 3 * (1 - st):3 * (1 - st) + 2, 0:TH],
                                  cbuf[:, 0:2 * TH].rearrange("p (a b) -> p a b", a=2), ALU.mult)
                dve.tensor_tensor(pada[:, HA + 2 * TH:HA + SEQ], PS[:, 3 * (1 - st) + 2, 0:SEQ - 2 * TH],
                                  cbuf[:, 2 * TH:SEQ], ALU.mult)
                dve.tensor_tensor(seqs(pada, HA + SEQ, HA, HA, SLEN),
                                  PS[:, 3 * (1 - st) + 2, SEQ - 2 * TH:TH].rearrange("p (s c) -> p s c", s=NSEQ),
                                  cbuf[:, SEQ:T].rearrange("p (s c) -> p s c", s=NSEQ), ALU.mult).then_inc(free_c, 1)
                split_lo(dve, n + 4, (n + 1) % 2)
                dve.wait_ge(c_hist, i + 1)
                for t in range(HA + 1):
                    weight = SW[:, S_CA + 3 * i + t:S_CA + 3 * i + t + 1]
                    dve.drain()
                    if t == 0:
                        dve.tensor_scalar(ya[:, 0:LA], pada[:, 0:LA], weight, None, ALU.mult)
                    else:
                        ins = dve.scalar_tensor_tensor(out=ya[:, 0:LA], in0=pada[:, t:t + LA], scalar=weight,
                                                       in1=ya[:, 0:LA], op0=ALU.mult, op1=ALU.add)
                ins.then_inc(ya_done, 1)
                dve.wait_ge(unit_done, filled(n + 2))
                dve.drain()
                dve.tensor_tensor(bc[:, 0:2 * TH].rearrange("p (a b) -> p a b", a=2), PS[:, 3 * st:3 * st + 2, 0:TH],
                                  ya[:, 0:2 * TH].rearrange("p (a b) -> p a b", a=2), ALU.mult)
                dve.tensor_tensor(bc[:, 2 * TH:SEQ], PS[:, 3 * st + 2, 0:SEQ - 2 * TH], ya[:, 2 * TH:SEQ], ALU.mult)
                dve.tensor_tensor(bc[:, SEQ:T].rearrange("p (s c) -> p s c", s=NSEQ),
                                  PS[:, 3 * st + 2, SEQ - 2 * TH:TH].rearrange("p (s c) -> p s c", s=NSEQ),
                                  seqs(ya, HA + SEQ, HA, 0, SLEN), ALU.mult).then_inc(bc_done, 1)
                dve.drain().then_inc(free_c, 1)
                dve.wait_ge(bh_done, i + 1)
                dve.tensor_tensor(BL[:, i, :], bc[:, :], BH[:, i, :].bitcast(F32), ALU.subtract).then_inc(bl_done, 1)
            dve.drain().then_inc(y_read, 2)
            dve.drain().then_inc(m_done, 1)
            with dve.Fori(0, KD // 2) as i:
                for q in range(2):
                    row = thirds(HID[:, ds(2 * i + q, 1), :].rearrange("p n t -> p (n t)"))
                    for r in range(3):
                        nxt = B_Y + 3 * q + r + 1
                        split_lo(dve, 6 * i + (nxt + 1), nxt % 2)
                    dve.wait_ge(unit_done, 8 * i + filled(B_Y + 4 * q + 2))
                    dve.wait_ge(sig_done, 4 * i + (2 * q + 1))
                    dve.tensor_tensor(row, pset(1), thirds(sig[:, 0, :]), ALU.mult).then_inc(y_read, 1)
                    dve.wait_ge(unit_done, 8 * i + filled(B_Y + 4 * q + 3))
                    dve.wait_ge(sig_done, 4 * i + (2 * q + 2))
                    dve.tensor_tensor(thirds(sig[:, 1, :]), pset(0), thirds(sig[:, 1, :]), ALU.mult).then_inc(y_read, 1)
                    dve.drain()
                    dve.tensor_tensor(row, row, thirds(sig[:, 1, :]), ALU.add).then_inc(m_done, 1)
            for k in range(KD):
                dve.wait_ge(mh_done, k + 1)
                dve.tensor_tensor(XL[:, k, :], HID[:, k, :], XH[:, k, :].bitcast(F32), ALU.subtract).then_inc(ml_done, 1)
            dve.drain().then_inc(free_h, 2)
            with dve.Fori(0, KD // 2) as i:
                for r in range(2):
                    split_lo(dve, 2 * i + (B_O + r + 2), (B_O + r + 1) % 2)
                    dve.wait_ge(xr_in[r], 16 * i + 16)
                    dve.wait_ge(unit_done, 2 * i + filled(unit_of(B_O) + r))
                    dve.tensor_tensor(thirds(HID[:, ds(2 * i + r, 1), :].rearrange("p n t -> p (n t)")), pset(1 - r),
                                      thirds(xr[:, r, :]), ALU.add).then_inc(free_h, 1)
            dve.drain()
            norm(HID, rms_sems["nb"], S_FFN, KD)
            for j in range(HP - 1):
                split_lo(dve, B_WQ + j + 2, (B_WQ + j + 1) % 2)

            def e_low(n, slot):
                dve.wait_ge(e_hi, n + 1)
                dve.tensor_tensor(WL[:, slot, :], RAW[:, slot, :], WH[:, slot, :].bitcast(F32), ALU.subtract).then_inc(e_lo, 1)

            def sel_dve(i, cols):
                w, n = P, i + 1

                def r(x):
                    return x[0:w]
                dve.wait_ge(sel_sc, n)
                dve.tensor_copy(r(tick), r(sc)[:, 0, 0:1])
                for j in range(2 * HP):
                    dve.max(r(best)[:, j, 0:8], r(sc)[:, j, :])
                dve.drain()
                for j in range(2 * HP):
                    dve.match_replace(r(sc2)[:, j, :], r(best)[:, j, 0:8], r(sc)[:, j, :], -3.4e38)
                    dve.max_index(r(besti)[:, j, 0:8], r(best)[:, j, 0:8], r(sc)[:, j, :])
                dve.drain().then_inc(sel_read, 1)
                e_low(SEL_E * i + 1, 1)
                for j in range(2 * HP):
                    dve.max(r(best)[:, j, 8:16], r(sc2)[:, j, :])
                dve.drain()
                for j in range(2 * HP):
                    dve.max_index(r(besti)[:, j, 8:16], r(best)[:, j, 8:16], r(sc2)[:, j, :])
                e_low(SEL_E * i + 2, 0)
                b2 = r(best).rearrange("p (h s) k -> p h s k", s=2)
                for i0, rows, n_cols in CAND:
                    a = ROW_START[i0]
                    dve.tensor_tensor(
                        r(cand)[:, :, a:a + rows * n_cols].rearrange("p h (i j) -> p h i j", i=rows),
                        b2[:, :, 0, i0:i0 + rows].unsqueeze(3).broadcast_to([w, HP, rows, n_cols]),
                        b2[:, :, 1, 0:n_cols].unsqueeze(2).broadcast_to([w, HP, rows, n_cols]), ALU.add)
                dve.drain()
                dve.tensor_copy(r(bestf), r(besti))
                for h in range(HP):
                    dve.max(r(top)[:, h, 0:8], r(cand)[:, h, :])
                dve.drain()
                for h in range(HP):
                    dve.match_replace(r(cand2)[:, h, :], r(top)[:, h, 0:8], r(cand)[:, h, :], -3.4e38)
                    dve.max_index(r(topi)[:, h, 0:8], r(top)[:, h, 0:8], r(cand)[:, h, :])
                dve.drain()
                for h in range(HP):
                    dve.max(r(top)[:, h, 8:16], r(cand2)[:, h, :])
                dve.drain()
                for h in range(HP):
                    dve.max_index(r(topi)[:, h, 8:16], r(top)[:, h, 8:16], r(cand2)[:, h, :])
                e_low(SEL_E * i + 3, 1)
                g3 = r(gate).rearrange("p (h k) -> p h k", h=HP)
                dve.tensor_tensor(g3, r(top), r(top)[:, :, 0:1].broadcast_to([w, HP, TOPK]), ALU.subtract).then_inc(sel_b, 1)
                f2 = r(bestf).rearrange("p (h s) k -> p h s k", s=2)
                dve.tensor_copy(r(delta)[:, :, 0:1], f2[:, :, 0, 0:1])
                dve.tensor_tensor(r(delta)[:, :, 1:TOPK], f2[:, :, 0, 1:TOPK], f2[:, :, 0, 0:TOPK - 1], ALU.subtract)
                dve.drain()
                dve.tensor_copy(r(topf), r(topi))
                dve.drain()

                def over(x):
                    return x.unsqueeze(2).broadcast_to([w, HP, TOPK, TOPK])

                def each(x):
                    return x.unsqueeze(3).broadcast_to([w, HP, TOPK, TOPK])

                def row(x):
                    return x.unsqueeze(1).unsqueeze(1).broadcast_to([w, HP, TOPK, TOPK])

                e1v, e2v = (r(x).rearrange("p (h k) -> p h k", h=HP) for x in (e1, e2))
                dve.tensor_tensor(r(hot), each(r(topf)), row(const("start16", w)), ALU.is_ge)
                dve.drain()
                dve.tensor_tensor(r(pick), r(hot), over(r(delta)), ALU.mult)
                dve.drain()
                dve.tensor_reduce(e1v, r(pick), AX.X, ALU.add)
                dve.drain()
                dve.tensor_tensor(r(pick), r(hot), row(r(dstart)), ALU.mult)
                dve.drain()
                dve.tensor_reduce(e2v, r(pick), AX.X, ALU.add)
                dve.drain()
                dve.tensor_tensor(r(topf), r(topf), e2v, ALU.subtract)
                dve.drain()
                dve.tensor_tensor(r(hot), each(r(topf)), row(const("iota16", w)), ALU.is_equal)
                dve.drain()
                dve.tensor_tensor(r(pick), r(hot), over(f2[:, :, 1, :]), ALU.mult)
                dve.drain()
                dve.tensor_reduce(e2v, r(pick), AX.X, ALU.add)
                dve.wait_ge(sel_e, n)
                dve.tensor_reduce(r(gsum), g3, AX.X, ALU.add)
                dve.drain()
                dve.reciprocal(r(gsum), r(gsum))
                dve.drain()
                dve.tensor_tensor(g3, g3, r(gsum).unsqueeze(2).broadcast_to([w, HP, TOPK]), ALU.mult).then_inc(sel_g, 1)
                e_low(SEL_E * i + 4, 0)
                dve.wait_ge(sel_t, n)
                dve.tensor_copy(EG[:, 0, cols], PS[:, 4, 0:w])
                dve.tensor_copy(EG[:, 1, cols], PS[:, 4, P:P + w])
                dve.tensor_scalar(EG[:, 2, cols], PS[:, 4, 2 * P:2 * P + w], GSCALE, None, ALU.mult)
                dve.drain()
                dve.scalar_tensor_tensor(out=EG[:, 3, cols], in0=PS[:, 4, 2 * P:2 * P + w], scalar=GSCALE,
                                         in1=EG[:, 2, cols], op0=ALU.mult, op1=ALU.subtract).then_inc(sel_done, 1)

            dve.wait_ge(iota_set, 1)
            dve.tensor_tensor(dstart[:, 1:TOPK], const("start16")[:, 1:TOPK], const("start16")[:, 0:TOPK - 1], ALU.subtract)
            dve.tensor_copy(dstart[:, 0:1], const("start16")[:, 0:1])
            e_low(0, 0)
            with dve.Fori(0, NT) as i:
                dve.drain()
                sel_dve(i, ds(P * i, P))
            dve.drain()
            sel_dve(NT, slice(T - P, T))

            dve.drain()
            dve.wait_ge(iota_set, 2)
            with dve.Fori(0, NWB // 2) as i:
                for s in range(2 * WT // WS):
                    cols = ds(2 * WT * i + WS * s, WS)

                    def row(k):
                        return EG[:, k, cols].unsqueeze(1).broadcast_to([P, NKEYS, WS])
                    dve.wait_ge(w_mm, 12 * i + (s + 1))
                    dve.tensor_tensor(HOT1[:, s % 2], IOTA[:, :, :], row(0), ALU.is_equal)
                    dve.tensor_tensor(HOT2[:, :, :], IOTA[:, :, :], row(1), ALU.is_equal)
                    dve.drain()
                    for k in range(2):
                        ins = dve.tensor_tensor(HOTG[:, s % 2, k], HOT2[:, :, :], row(2 + k), ALU.mult)
                    ins.then_inc(w_hot, 1)
                    dve.drain()
                    if s % 6 == 3:
                        e = s // 6
                        e_low(WM_E * i + (E0 + 1 + e), 1 - e)
            for n in range(E0 + WM_E * (NWB // 2) + 1, NE):
                e_low(n, n % 2)

            def u_low(m, slot):
                dve.wait_ge(u_hi, m)
                dve.tensor_tensor(WL[:, slot, :], RAW[:, slot, :], WH[:, slot, :].bitcast(F32), ALU.subtract).then_inc(u_lo, 1)

            def s_gated(g, e):
                if e == 0:
                    dve.wait_ge(gw_in, 16 * g + 16)
                dve.wait_ge(as_in[e], 16 * g + 16)
                dve.tensor_tensor(AS[:, e, :], AS[:, e, :], GW[:, :, e], ALU.mult).then_inc(s_mul, 1)

            def v_low(d, s):
                dve.wait_ge(v_hi, s)
                dve.tensor_tensor(VL[:, d % 2, :], VRAW[:, d % 4, :], VH[:, d % 2, :].bitcast(F32), ALU.subtract).then_inc(v_lo, 1)

            dve.drain().then_inc(acc_done, 2)
            u_low(1, 0)
            u_low(2, 1)
            for e in range(EARLY):
                s_gated(0, e)

            def group_dve(g, last):
                dve.drain()
                for e in range(EARLY):
                    dve.wait_ge(s_hi, 2 * g + (e + 1))
                    dve.tensor_tensor(AL[:, e, :], AS[:, e, :], AH[:, e, :].bitcast(F32), ALU.subtract).then_inc(s_lo, 1)
                for d in range(2):
                    v_low(d, 8 * g + (d + 1))
                for c in range(LATE):
                    k = EARLY + c
                    dve.wait_ge(a_gelu, 2 * g + (c + 1))
                    dve.tensor_tensor(AF[:, k, :], AF[:, k, :], GW[:, :, k], ALU.mult).then_inc(a_mul, 1)
                    dve.wait_ge(a_hi, 2 * g + (c + 1))
                    dve.tensor_tensor(AL[:, k, :], AF[:, k, :], AH[:, k, :].bitcast(F32), ALU.subtract).then_inc(a_lo, 1)
                    if c == 0 and not last:
                        u_low(2 * g + 3, 0)
                if not last:
                    u_low(2 * g + 4, 1)
                for d in range(8):
                    dve.wait_ge(v_mm, 8 * g + (d + 3))
                    dve.tensor_tensor(thirds(HID[:, d, :]), thirds(HID[:, d, :]), pset(d % 2), ALU.add).then_inc(acc_done, 1)
                    if d < 6:
                        v_low(d + 2, 8 * g + (d + 3))
                    if d in (5, 6) and not last:
                        s_gated(g + 1, d - 5)

            with dve.Fori(0, NG - 1) as g:
                group_dve(g, False)
            group_dve(NG - 1, True)
            dve.drain()
            dve.wait_ge(rms_sems["nc"]["rn"], 1)
            for k in range(KD):
                if k >= 2:
                    dve.wait_ge(out_y[k % 2], 16 * (k // 2))
                dve.scalar_tensor_tensor(out=xt[:, k % 2, :], in0=HID[:, k, :], scalar=SW[:, S_FIN + k:S_FIN + k + 1],
                                         in1=rn[:, :], op0=ALU.mult, op1=ALU.mult).then_inc(y_row, 1)


def packed(w):
    k, n = w.shape[0] // P, w.shape[1] // P
    return w.reshape(k, P, n, P).transpose(2, 1, 0, 3)


def kernel(x_prompt, x_sample, state_conv_a, state_conv_qkv, state_delta, g_norm_mix, w_in, w_conv_a,
           w_conv_qkv, a_log, dt_bias, g_dn_norm, w_out_a, w_out_dn, w_o, g_norm_ffn, w_query, sub_keys,
           expert_u, expert_v, g_norm_final):
    import concourse.bacc as bacc
    from concourse.bass_utils import run_bass_kernel_spmd

    def chunks(w, *tail):
        return w.reshape(-1, w.shape[-1] // P, P).transpose(2, 1, 0)

    x = np.concatenate([np.asarray(x_prompt).reshape(SEQ, D), np.asarray(x_sample).reshape(TS, D)])
    w = np.asarray(w_in)[0]
    half, wide = D // 2, H * P
    at = {}
    o = 0
    for name, n in (("b", half), ("c", half), ("h", half), ("qkv", 3 * wide), ("z", wide), ("a", H), ("beta", H),
                    ("ga", D), ("gb", D)):
        at[name] = w[:, o:o + n]
        o += n
    ab = np.zeros((D, P), w.dtype)
    ab[:, 0:H], ab[:, 32:32 + H] = at["a"], at["beta"]
    pk = {n: packed(v) for n, v in at.items() if n not in ("a", "beta")}
    wa, wd = packed(np.asarray(w_out_a)[0]), packed(np.asarray(w_out_dn)[0])
    blocks = [pk["qkv"], packed(ab), pk["z"]]
    for i in range(H):
        blocks += [pk[n][i:i + 1] for n in ("c", "h", "b")]
    for j in range(KD):
        blocks += [pk["ga"][j:j + 1], pk["gb"][j:j + 1], np.concatenate([wa[j:j + 1], wd[j:j + 1]], axis=2)]
    blocks += [packed(np.asarray(w_o)[0]), packed(np.asarray(w_query)[0])]
    wall = np.ascontiguousarray(np.concatenate(blocks)).reshape(NBLK, P, D)

    small = np.zeros((P, NSMALL), w.dtype)
    for col, g in ((S_MIX, g_norm_mix), (S_FFN, g_norm_ffn), (S_FIN, g_norm_final)):
        small[:, col:col + KD] = np.asarray(g).reshape(KD, P).T
    small[:, S_CQ:S_CQ + 4 * NQ] = chunks(np.asarray(w_conv_qkv)[0]).reshape(P, 4 * NQ)
    small[:, S_CA:S_CA + 3 * H] = chunks(np.asarray(w_conv_a)[0]).reshape(P, 3 * H)
    small[:, S_DN] = np.asarray(g_dn_norm)[0]
    small[0:H, S_ALOG] = np.asarray(a_log)[0]
    small[0:H, S_DT] = np.asarray(dt_bias)[0]

    sk = np.asarray(sub_keys)[0]
    keys = np.zeros((P, HP, 2 * NKEYS), sk.dtype)
    for p in range(2):
        keys[64 * p:64 * p + 64, :, NKEYS * p:NKEYS * p + NKEYS] = sk[p].transpose(2, 0, 1)

    def history(s):
        n, k, c = s.shape
        return np.ascontiguousarray(s.reshape(n, k, c // P, P).transpose(3, 2, 0, 1))

    second = np.arange(NKEYS).reshape(NG, GE)
    order = np.concatenate([second[:, :EARLY].ravel(), second[:, EARLY:].ravel()])
    arrays = {
        "x_t": np.ascontiguousarray(x.reshape(T, KD, P).transpose(2, 1, 0)),
        "weights": wall,
        "small": small,
        "keys": keys,
        "constants": CONSTANTS,
        "hist_qkv": history(np.asarray(state_conv_qkv)[0]),
        "hist_a": history(np.asarray(state_conv_a)[0]),
        "state": np.ascontiguousarray(np.asarray(state_delta)[0].transpose(2, 0, 1, 3)),
        "experts_u": np.ascontiguousarray(
            np.asarray(expert_u)[0].reshape(NKEYS, NKEYS, KD, P).transpose(1, 3, 2, 0)[order]).reshape(NKEYS, P, D),
        "experts_v": np.ascontiguousarray(
            np.asarray(expert_v)[0].reshape(NKEYS, NG, GE, KD, P).transpose(1, 3, 0, 2, 4)).reshape(NG * KD, P, GE * P),
    }
    outs = {"y_t": (P, KD, T), "new_qkv": (P, NQ, NSEQ + 1, HQ), "new_a": (P, H, NSEQ + 1, HA),
            "state_p": (P, H, P), "state_s": (P, NSEQ, H, P)}
    nc = bacc.Bacc("TRN2", target_bir_lowering=False, num_devices=1)
    ins = [nc.dram_tensor(n, a.shape, F32, kind="ExternalInput").ap() for n, a in arrays.items()]
    got = [nc.dram_tensor(n, s, F32, kind="ExternalOutput").ap() for n, s in outs.items()]
    kept = [nc.dram_tensor(n, s, F32, kind="Internal").ap() for n, s in {
        "gate_matrices": (NG, P, T, GE), "queries": (P, HP, T), "activations": (NE, P, T)}.items()]
    program(nc, *ins, *got, *kept)
    res = run_bass_kernel_spmd(nc, [arrays], core_ids=[0]).results[0]

    y = res["y_t"].transpose(2, 1, 0).reshape(T, D)
    new_q = res["new_qkv"].transpose(2, 3, 1, 0).reshape(NSEQ + 1, HQ, NQ * P)
    new_a = res["new_a"].transpose(2, 3, 1, 0).reshape(NSEQ + 1, HA, H * P)
    return (y[:SEQ].reshape(1, SEQ, D), y[SEQ:].reshape(NSEQ, SLEN, D),
            new_a[None, 0:1], new_q[None, 0:1], res["state_p"].transpose(1, 0, 2)[None, None],
            new_a[None, 1:], new_q[None, 1:], res["state_s"].transpose(1, 2, 0, 3)[None])
```

```python
from contextlib import ExitStack

import numpy as np

import concourse.bass as bass
from concourse import mybir

F32 = mybir.dt.float32
F32R = mybir.dt.float32r
BF16 = mybir.dt.bfloat16
F16 = mybir.dt.float16
U32 = mybir.dt.uint32
ALU = mybir.AluOpType
ACT = mybir.ActivationFunctionType
AX = mybir.AxisListType
ds = bass.ds

P = 128
D = 1024
KD = D // P
SEQ = 1024
NSEQ, SLEN = 8, 4
TS = NSEQ * SLEN
T = SEQ + TS
TH = T // 3
NT = SEQ // P
H = 4
NQ = 3 * H
EPS = 1e-6
NEG = -1e30
HP = 8
TOPK = 16
NKEYS = 128
PAIRS = HP * TOPK

CAND = [(0, 1, 16), (1, 1, 8), (2, 2, 5), (4, 4, 3), (8, 8, 1)]
ROW_LEN = [cols for _, rows, cols in CAND for _ in range(rows)]
ROW_START = [sum(ROW_LEN[:i]) for i in range(TOPK)]
NCAND = sum(ROW_LEN)

B_QKV, B_AB, B_G, B_Z, B_CONV, B_Y, B_O, B_WQ, NBLK = 0, 12, 13, 29, 33, 45, 53, 61, 69

GE = 4
NG = NKEYS // GE
EARLY = 2
LATE = GE - EARLY
NE = NG * EARLY
SEL_E, WM_E = 4, 2
PRE = 2
E0 = PRE + SEL_E * (SEQ // P + 1)
GSCALE = 2.0 ** 15
WT = 48
WS = 8
NWB = T // WT
S_MIX, S_FFN, S_FIN, S_CQ, S_CA, S_DN, S_ALOG, S_DT, NSMALL = 0, 8, 16, 24, 72, 84, 85, 86, 88
HQ, HA = 3, 2
PADQ, PADA = HQ + SEQ + NSEQ * (SLEN + HQ), HA + SEQ + NSEQ * (SLEN + HA)


def constants():
    i = np.arange(P)
    lo, hi = i[:, None], i[None, :]
    a, b = np.arange(TS)[:, None], np.arange(TS)[None, :]
    same = a // SLEN == b // SLEN

    def rows(x):
        return np.concatenate([x, np.zeros((P - TS, x.shape[1]))])

    def level(row, col, l):
        return (row >> (l + 1) == col >> (l + 1)) & (row >> l != col >> l) & (col > row)

    parts = {"ident": lo == hi, "ones": np.ones((P, P)),
             "iota16": np.tile(np.arange(TOPK)[None], (P, 1)),
             "start16": np.tile(np.array(ROW_START)[None], (P, 1)),
             "upto": lo <= hi, "after": lo > hi, "neg": np.where(lo > hi, NEG, 0.0)}
    for l in range(7):
        parts[f"mask{l}"] = level(lo, hi, l)
    parts["upto_s"] = rows(same & (a <= b))
    parts["after_s"] = rows(same & (a > b))
    parts["neg_s"] = rows(np.where(same & (a <= b), 0.0, NEG))
    for l in range(2):
        parts[f"mask{l}_s"] = rows(level(a, b, l))
    seq = np.arange(TS)[None, :] // SLEN == np.arange(NSEQ)[:, None]
    parts["seqcol"] = np.tile(seq.reshape(1, -1), (P, 1))
    parts["seqrow"] = rows(seq.T)
    parts["sel"] = np.repeat(lo == np.arange(H)[None], P, axis=1)
    at, where = 0, {}
    for name, x in parts.items():
        where[name] = (at, x.shape[1])
        at += x.shape[1]
    return np.concatenate([np.asarray(x, np.float32) for x in parts.values()], axis=1), where


CONSTANTS, CONST_AT = constants()
NCST = CONSTANTS.shape[1]


def unit_of(block):
    if block < B_Y:
        return block
    if block < B_O:
        return B_Y + 2 * (block - B_Y) + 1
    return block + KD


def program(nc, xT, wall, small, keys, cst, histq, hista, s_in, u_blk, v_blk,
            yT, convq_out, conva_out, sp_out, ss_out, w_dram, q_dram, act_dram, g_dram):
    with ExitStack() as ctx:
        def sem(name):
            return ctx.enter_context(nc.semaphore(name))

        BASE = -(-nc.sbuf_base // 64) * 64
        arena = ctx.enter_context(nc.sbuf_tensor("arena", [P, (229344 - BASE) // 4 - 8], F32))

        def at(off, name, shape, dt=F32):
            size = int(np.prod(shape[1:])) * (2 if dt in (BF16, F16) else 4)
            assert off % 4 == 0 and BASE + off + size <= 229344, (name, off, size)
            return nc.alloc_sbuf_tensor_at(name, list(shape), dt, offset=BASE + off, align_bytes=4)

        ROW = 4 * T
        XH = at(0, "XH", [P, KD, T], F32R)
        XL = at(8 * ROW, "XL", [P, KD, T], F32R)
        ring = 16 * ROW
        RAW = at(ring, "RAW", [P, 2, D])
        WH = at(ring + 8192, "WH", [P, 2, D], F32R)
        WL = at(ring + 16384, "WL", [P, 2, D], F32R)
        c0 = ring + 24576
        C = at(c0, "C", [P, NCST])
        SW = at(c0 + 4 * NCST, "SW", [P, NSMALL])
        gb_tok = at(c0 + 4 * NCST + 4 * NSMALL, "gb_tok", [P, NT + 1, 8])
        r1 = c0 + 4 * NCST + 4 * NSMALL + 288
        r2, r3, r4 = r1 + 8 * ROW, r1 + 16 * ROW, r1 + 24 * ROW

        HID = at(r1, "HID", [P, KD, T])
        sq = at(r3, "sq", [P, 2, T])
        sqb = at(r2, "sqb", [P, 2, T])
        rn = at(r3 + 2 * ROW, "rn", [P, T])
        xt = at(r3 + 3 * ROW, "xt", [P, 2, T])
        QKV = at(r2, "QKV", [P, NQ, T])
        pad = at(r1, "pad", [P, 2, PADQ])
        cy = at(r1 + 8 * PADQ, "cy", [P, 2, PADQ])
        hist = at(r1 + 16 * PADQ, "hist", [P, NQ, NSEQ, HQ])
        new_q = at(r1 + 16 * PADQ + 4 * NQ * 24, "new_q", [P, NQ, NSEQ + 1, HQ])
        ab = at(r3 + 4 * ROW, "ab", [H, 4, T])
        betaT = at(r4, "betaT", [H, T])
        sq2 = at(r1, "sq2", [P, 2, T])
        rn4 = at(r1 + 2 * ROW, "rn4", [H, 2, T])
        DN1 = at(r1, "DN1", [P, 16, 512])
        DN2 = at(r3 + 4 * ROW, "DN2", [P, 8, 512])
        S = at(r4 + ROW, "S", [P, H, P])
        SS = at(r3 + 4 * ROW, "SS", [P, NSEQ, H, P])
        kbgm = at(r1 + 12 * 2048, "kbgm", [P, H, NSEQ, TS])
        qdm = at(r1 + 14 * 2048, "qdm", [P, H, NSEQ, TS])
        gbt = at(r4 + ROW + 2112, "gbt", [P, 2, 8])
        gsc = at(r4 + ROW + 2048, "gsc", [P, 2, 4])
        ekd = at(r4 + ROW + 2080, "ekd", [P, 2, 4])
        gst = at(r4 + ROW + 2176, "gst", [P, TH])
        zs = at(r1, "zs", [P, 2, T])
        on = at(r1 + 2 * ROW, "on", [P, 2, T])
        OH = at(r3, "OH", [P, H, T], F32R)
        OL = at(r3 + 4 * ROW, "OL", [P, H, T], F32R)
        BH = at(r2, "BH", [P, H, T], F32R)
        BL = at(r2 + 4 * ROW, "BL", [P, H, T], F32R)
        cbuf = at(r1 + 4 * ROW, "cbuf", [P, T])
        pada = at(r1 + 5 * ROW, "pada", [P, PADA])
        ya = at(r1 + 5 * ROW + 4 * PADA, "ya", [P, PADA])
        bc = at(r4, "bc", [P, T])
        hist_a = at(r4 + ROW, "hist_a", [P, H, NSEQ, HA])
        new_a = at(r4 + ROW + 256, "new_a", [P, H, NSEQ + 1, HA])
        sig = at(r4, "sig", [P, 2, T])
        xr = at(r3, "xr", [P, 2, T])
        KEYS = at(r2, "KEYS", [P, HP, 2 * NKEYS])
        qst = at(r2 + 8192, "qst", [P, HP, P])
        qrow = at(r2 + 12288, "qrow", [P, 2, T])
        sel0 = r2 + 12288 + 2 * ROW
        sc = at(sel0, "sc", [P, 2 * HP, NKEYS])
        sc2 = at(sel0 + 8192, "sc2", [P, 2 * HP, NKEYS])
        hot = at(sel0 + 16384, "hot", [P, HP, TOPK, TOPK], BF16)
        pick = at(sel0 + 20480, "pick", [P, HP, TOPK, TOPK], BF16)
        cand = at(sel0 + 24576, "cand", [P, HP, NCAND])
        cand2 = at(sel0 + 24576 + 32 * NCAND, "cand2", [P, HP, NCAND])
        o = [sel0 + 24576 + 64 * NCAND]

        def small_at(name, shape, dt=F32):
            t = at(o[0], name, shape, dt)
            o[0] += int(np.prod(shape[1:])) * (2 if dt == BF16 else 4)
            return t

        best = small_at("best", [P, 2 * HP, TOPK])
        besti = small_at("besti", [P, 2 * HP, TOPK], U32)
        bestf = small_at("bestf", [P, 2 * HP, TOPK], BF16)
        delta = small_at("delta", [P, HP, TOPK], BF16)
        top = small_at("top", [P, HP, TOPK])
        topi = small_at("topi", [P, HP, TOPK], U32)
        topf = small_at("topf", [P, HP, TOPK])
        e1 = small_at("e1", [P, PAIRS])
        e2 = small_at("e2", [P, PAIRS])
        gate = small_at("gate", [P, PAIRS])
        gsum = small_at("gsum", [P, HP])
        iota_b = small_at("iota_b", [P, TOPK], BF16)
        dstart = small_at("dstart", [P, TOPK], BF16)
        tick = small_at("tick", [P, 1])
        stg = at(r2, "stg", [P, 2, NG, WT, GE])
        oh0 = r2 + 2 * 512 * WT
        IOTA = at(oh0, "IOTA", [P, NKEYS, WS], F16)
        HOT1 = at(oh0 + 2048, "HOT1", [P, 2, NKEYS, WS], F16)
        HOT2 = at(oh0 + 6144, "HOT2", [P, 2, NKEYS, WS], F16)
        HOTG = at(oh0 + 10240, "HOTG", [P, 2, 2, NKEYS, WS], F16)
        as0 = oh0 + 10240 + 8192 + 64
        assert o[0] <= as0
        AS = at(as0, "AS", [P, EARLY, T])
        sqc = at(as0, "sqc", [P, 2, T])
        late = CONST_AT["upto"][0]
        assert 4 * (NCST - late) >= 8 * T
        EG = at(c0 + 4 * late, "EG", [P, 4, T], F16)
        AH = at(r2, "AH", [P, GE, T], F32R)
        AL = at(r2 + 4 * ROW, "AL", [P, GE, T], F32R)
        AF = at(r2 + 4 * ROW, "AF", [P, GE, T])
        VRAW = at(r2 + 8 * ROW, "VRAW", [P, 4, GE * P])
        VH = at(r2 + 8 * ROW + 8192, "VH", [P, 2, GE * P], F32R)
        VL = at(r2 + 8 * ROW + 12288, "VL", [P, 2, GE * P], F32R)
        GW = at(r2 + 8 * ROW + 16384, "GW", [P, T, GE])
        totc = at(r2 + 8 * ROW + 16384, "totc", [P, T])
        assert r2 + 12 * ROW + 16384 <= as0

        PS = ctx.enter_context(nc.psum_tensor("PS", [P, 8, 512], F32))

        def const(name, rows=P):
            a, n = CONST_AT[name]
            return C[0:rows, a:a + n]

        def thirds(ap):
            return ap.rearrange("p (a b) -> p a b", a=3)

        def pset(s, rows=P):
            return PS[0:rows, 3 * s:3 * s + 3, 0:TH]

        in_c, in_w, in_x = sem("in_c"), sem("in_w"), [sem(f"in_x{k}") for k in range(KD // 2)]
        raw_in = [sem("raw_in0"), sem("raw_in1")]
        hi_done, lo_done, unit_done = sem("hi_done"), sem("lo_done"), sem("unit_done")

        def filled(u):
            return u + 2

        block = ctx.enter_context(nc.Block())

        def split_hi(act, slot, reads, before):
            act.wait_ge(raw_in[slot], reads)
            if before is not None:
                act.wait_ge(unit_done, before)
            act.activation(WH[:, slot, :], RAW[:, slot, :], ACT.Copy).then_inc(hi_done, 1)

        def split_lo(dve, count, slot):
            dve.wait_ge(hi_done, count)
            dve.tensor_tensor(WL[:, slot, :], RAW[:, slot, :], WH[:, slot, :].bitcast(F32),
                              ALU.subtract).then_inc(lo_done, 1)

        def products(pe, slot, s, xh, xl, chunks=range(KD), base=0, ready=None):
            steps = [(k, n, t) for k in chunks for n in range(3) for t in range(3)]
            for k, n, t in steps:
                if ready is not None and n == 0 and t == 0:
                    pe.wait_ge(ready[0], ready[1] + k + 1)
                w, x = ((WH, xh), (WH, xl), (WL, xh))[n]
                mm = pe.matmul(PS[:, 3 * s + t, 0:TH], w[:, slot, k * P:k * P + P],
                               x[:, k - base, t * TH:t * TH + TH],
                               start=(k == chunks[0] and n == 0), stop=(k == chunks[-1] and n == 2))
            return mm

        rms_sems = {n: {k: sem(f"{n}_{k}") for k in ("sq", "sum", "mm", "ln", "rn")} for n in ("na", "nb", "nc")}

        def rms_square(act, row, k, slot, r, sq):
            act.wait_ge(r["sum"], k + 1)
            act.activation(sq[:, slot, :], row, ACT.Square).then_inc(r["sq"], 1)

        def rms_zero(dve, r, total):
            dve.memset(total[:, :], 0.0)
            dve.drain().then_inc(r["sum"], 2)

        def rms_add(dve, k, slot, r, sq, total):
            dve.wait_ge(r["sq"], k + 1)
            dve.wait_ge(r["sum"], k + 2)
            dve.tensor_tensor(total[:, :], total[:, :], sq[:, slot, :], ALU.add).then_inc(r["sum"], 1)

        def rms_act(act, r):
            act.wait_ge(r["mm"], 1)
            act.activation(thirds(rn[:, :]), pset(0), ACT.Ln, scale=1.0 / D, bias=EPS).then_inc(r["ln"], 1)
            act.wait_ge(r["ln"], 1)
            act.activation(rn[:, :], rn[:, :], ACT.Exp, scale=-0.5).then_inc(r["rn"], 1)

        def rms_pe(pe, r, total):
            pe.wait_ge(r["sum"], KD + 2)
            for t in range(3):
                mm = pe.matmul(PS[:, t, 0:TH], const("ones"), total[:, t * TH:t * TH + TH], start=True, stop=True)
            mm.then_inc(r["mm"], 1)

        xt_done, xh_done, xl_done = sem("xt_done"), sem("xh_done"), sem("xl_done")

        def norm_act(act, base):
            for k in range(KD):
                act.wait_ge(xt_done, base + k + 1)
                act.activation(XH[:, k, :], xt[:, k % 2, :], ACT.Copy).then_inc(xh_done, 1)

        hist_in, hist_a_in, state_in = sem("hist_in"), sem("hist_a_in"), sem("state_in")
        free_q, evac_q, hist_set, conv_q, silu_q, newq_set = (sem(n) for n in (
            "free_q", "evac_q", "hist_set", "conv_q", "silu_q", "newq_set"))
        out_q, out_a, out_s = sem("out_q"), sem("out_a"), sem("out_s")
        out_y = [sem("out_y0"), sem("out_y1")]
        ab_a, ab_v, ab_p, ab_t = sem("ab_a"), sem("ab_v"), sem("ab_p"), sem("ab_t")
        l2_sq, l2_mm, l2_ln, l2_rn, l2_bc, l2_done = (sem(n) for n in ("l2_sq", "l2_mm", "l2_ln", "l2_rn", "l2_bc", "l2_done"))
        zeroed = sem("zeroed")
        g_mm, g_evac, g_out = sem("g_mm"), sem("g_evac"), sem("g_out")
        g_in = [sem("g_in0"), sem("g_in1")]
        dn_in, dn_bc, dn_dt, dn_eg, dn_d, dn_e, dn_g, dn_x, dn_xs, dn_tt, dn_t = (sem(f"dn_{n}") for n in (
            "in", "bc", "dt", "eg", "d", "e", "g", "x", "xs", "tt", "t"))
        dn_ks, dn_r, dn_v, dn_vs, dn_o, dn_os, dn_ds, dn_st = (sem(f"dn_{n}") for n in (
            "ks", "r", "v", "vs", "o", "os", "ds", "st"))
        dn_m, dn_vm = sem("dn_m"), sem("dn_vm")
        free_c, silu_z, on_done, oh_h, c_hist, bc_done, bh_done, bl_done = (sem(n) for n in (
            "free_c", "silu_z", "on_done", "oh_h", "c_hist", "bc_done", "bh_done", "bl_done"))
        ol_done = sem("ol_done")
        ya_done, newa_set = sem("ya_done"), sem("newa_set")
        sig_done, y_read, m_done, mh_done, ml_done = (sem(n) for n in ("sig_done", "y_read", "m_done", "mh_done", "ml_done"))
        xr_in = [sem("xr_in0"), sem("xr_in1")]
        free_h, free_w = sem("free_h"), sem("free_w")
        keys_in, qst_in, sel_mm, sel_sc, sel_read, sel_b, sel_e, sel_g, sel_t, sel_done = (sem(f"sel_{n}") for n in (
            "keys", "q", "mm", "sc", "read", "b", "e", "g", "t", "done"))
        q_out = [sem("q_out0"), sem("q_out1")]
        e_in, e_out = [sem("e_in0"), sem("e_in1")], [sem("e_out0"), sem("e_out1")]
        e_hi, e_lo, e_mm, e_gelu = (sem(n) for n in ("e_hi", "e_lo", "e_mm", "e_gelu"))
        iota_set = sem("iota_set")
        w_second, w_hot, w_mm, w_evac = sem("w_second"), sem("w_hot"), sem("w_mm"), sem("w_evac")
        w_out = [sem("w_out0"), sem("w_out1")]
        u_in, gw_in, as_in = [sem("u_in0"), sem("u_in1")], sem("gw_in"), [sem("as_in0"), sem("as_in1")]
        s_mul, s_hi, s_lo = sem("s_mul"), sem("s_hi"), sem("s_lo")
        v_in = [sem(f"v_in{k}") for k in range(4)]
        u_hi, u_lo, u_mm, a_gelu, a_mul, a_hi, a_lo = (sem(n) for n in (
            "u_hi", "u_lo", "u_mm", "a_gelu", "a_mul", "a_hi", "a_lo"))
        v_hi, v_lo, v_mm, acc_done = (sem(n) for n in ("v_hi", "v_lo", "v_mm", "acc_done"))
        y_row = sem("y_row")


        def dn(u, k):
            if u == 0:
                return DN1[:, k, :]
            return DN1[:, 12 + k, :] if k < 4 else DN2[:, k - 4, :]

        def dnh(u, k, w=P, rows=P):
            return dn(u, k)[0:rows, 0:H * w].rearrange("p (h c) -> p h c", h=H)

        def bank(b, w=P, rows=P):
            return PS[0:rows, b, 0:H * w].rearrange("p (h c) -> p h c", h=H)

        def seqs(buf, base, k, first, n):
            return buf[:, base:base + NSEQ * (SLEN + k)].rearrange(
                "p (s c) -> p s c", s=NSEQ)[:, :, first:first + n]

        def e_bank(slot, t):
            return PS[:, (6 + slot, 4, 5)[t], 0:TH]

        KST, VST, GBC, DIFF, DT, EXPG, KB, KBG, QD, MT, QKT, KDEC = range(12)
        X, VN, TM, BT, RES, TTR, VB = VST, VST, GBC, DIFF, DIFF, DT, KB
        NPAIR = NT // 2
        LEVELS = 7
        LEVELS_S = 2

        @block.sync
        def _(sp):
            for k in range(KD // 2):
                sp.dma_start(HID[:, 2 * k:2 * k + 2, :], xT[:, 2 * k:2 * k + 2, :]).then_inc(in_x[k], 16)
            sp.dma_start(SW[:, :], small).then_inc(in_w, 16)
            sp.dma_start(C[:, :], cst).then_inc(in_c, 16)
            for n in range(2):
                sp.dma_start(RAW[:, n, :], wall[n]).then_inc(raw_in[n], 16)
            with sp.Fori(0, (NBLK - 3) // 2) as i:
                for r in range(2):
                    sp.wait_ge(lo_done, 2 * i + (r + 1))
                    sp.dma_start(RAW[:, r, :], wall[ds(2 * i + (r + 2), 1)].rearrange("n p c -> (n p) c")
                                 ).then_inc(raw_in[r], 16)
            sp.wait_ge(lo_done, NBLK - 2)
            sp.dma_start(RAW[:, 0, :], wall[NBLK - 1]).then_inc(raw_in[0], 16)
            for r in range(2):
                sp.sem_inc(e_out[r], 16)
            for r in range(2):
                sp.wait_ge(lo_done, NBLK - r)
                sp.dma_start(RAW[:, r, :], u_blk[r]).then_inc(e_in[r], 16)
            with sp.Fori(0, NE // 2 - 1) as i:
                for r in range(2):
                    sp.wait_ge(e_lo, 2 * i + (r + 1))
                    sp.dma_start(RAW[:, r, :], u_blk[ds(2 * i + (r + 2), 1)].rearrange("n p c -> (n p) c")
                                 ).then_inc(e_in[r], 16)
                    sp.wait_ge(e_gelu, 6 * i + (3 * r + 6))
                    sp.dma_start(act_dram[ds(2 * i + r, 1)].rearrange("n p c -> (n p) c"), AS[:, r, :]
                                 ).then_inc(e_out[r], 16)
            for r in range(2):
                sp.wait_ge(e_lo, NE - 1 + r)
                sp.dma_start(RAW[:, r, :], u_blk[NE + r]).then_inc(u_in[r], 16)
                sp.wait_ge(e_gelu, 3 * (NE + r))
                sp.dma_start(act_dram[NE - 2 + r], AS[:, r, :]).then_inc(e_out[r], 16)
            for b in range(2):
                sp.wait_ge(w_out[b], 16 * (NWB // 2 + 1))
            sp.dma_start(GW[:, :, :], w_dram[0]).then_inc(gw_in, 16)
            for r in range(2):
                sp.wait_ge(e_out[r], 16 * (NE // 2 + 1))
            for r in range(2):
                sp.dma_start(AS[:, r, :], act_dram[r]).then_inc(as_in[r], 16)
            with sp.Fori(0, NG - 1) as i:
                for r in range(2):
                    sp.wait_ge(u_lo, 2 * i + (r + 1))
                    sp.dma_start(RAW[:, r, :], u_blk[ds(2 * i + (NE + 2 + r), 1)].rearrange("n p c -> (n p) c")
                                 ).then_inc(u_in[r], 16)
                for r in range(2):
                    sp.wait_ge(s_lo, 2 * i + (r + 1))
                    sp.dma_start(AS[:, r, :], act_dram[ds(2 * i + (2 + r), 1)].rearrange("n p c -> (n p) c")
                                 ).then_inc(as_in[r], 16)
                sp.wait_ge(a_mul, 2 * i + 2)
                sp.dma_start(GW[:, :, :].rearrange("p t j -> p (t j)"),
                             w_dram[ds(i + 1, 1)].rearrange("n p t j -> (n p) (t j)")).then_inc(gw_in, 16)
            for k in range(KD):
                sp.wait_ge(y_row, k + 1)
                sp.dma_start(yT[:, k, :], xt[:, k % 2, :]).then_inc(out_y[k % 2], 16)
            for b in range(2):
                sp.wait_ge(out_y[b], 16 * (KD // 2))

        @block.gpsimd
        def _(pool):
            pool.wait_ge(xl_done, KD)
            pool.dma_start(hist[:, :, :, :], histq).then_inc(hist_in, 16)
            pool.memset(pad[:, :, 0:HQ], 0.0).then_inc(zeroed, 1)
            pool.drain().then_inc(newq_set, 2)
            pool.wait_ge(hist_in, 16)

            with pool.Fori(0, NQ // 2) as i:
                for r in range(2):
                    pool.drain()
                    pool.wait_ge(conv_q, 2 * i + (r + 1))
                    pool.tensor_copy(seqs(pad[:, r, :], HQ + SEQ, HQ, 0, HQ),
                                     hist[:, ds(2 * i + r, 1), :, :].rearrange("p n s c -> p (n s) c")
                                     ).then_inc(hist_set, 1)
                    pool.wait_ge(evac_q, 2 * i + (r + 1))
                    pool.tensor_copy(new_q[:, ds(2 * i + r, 1), 0, :].rearrange("p n c -> p (n c)"),
                                     pad[:, r, SEQ:SEQ + HQ])
                    pool.tensor_copy(new_q[:, ds(2 * i + r, 1), 1:NSEQ + 1, :].rearrange("p n s c -> p (n s) c"),
                                     seqs(pad[:, r, :], HQ + SEQ, HQ, SLEN, HQ)).then_inc(newq_set, 1)
            pool.wait_ge(newq_set, NQ + 2)
            pool.dma_start(convq_out, new_q[:, :, :, :]).then_inc(out_q, 16)
            pool.wait_ge(dn_st, NT + 1)
            pool.dma_start(sp_out, S[:, :, :]).then_inc(out_s, 16)
            pool.dma_start(SS[:, :, :, :], s_in).then_inc(state_in, 16)
            pool.wait_ge(dn_st, NT + 1 + NSEQ)
            pool.dma_start(ss_out, SS[:, :, :, :]).then_inc(out_s, 16)
            pool.wait_ge(out_s, 32)
            pool.wait_ge(out_q, 16)
            pool.dma_start(hist_a[:, :, :, :], hista).then_inc(hist_a_in, 16)
            pool.wait_ge(l2_done, 3 * H)
            pool.memset(pada[:, 0:HA], 0.0)
            pool.wait_ge(hist_a_in, 16)
            for i in range(H):
                if i:
                    pool.wait_ge(ya_done, i)
                    pool.drain()
                pool.tensor_copy(seqs(pada, HA + SEQ, HA, 0, HA), hist_a[:, i, :, :]).then_inc(c_hist, 1)
                pool.wait_ge(ya_done, i + 1)
                pool.tensor_copy(new_a[:, i, 0, :], pada[:, SEQ:SEQ + HA])
                pool.tensor_copy(new_a[:, i, 1:NSEQ + 1, :], seqs(pada, HA + SEQ, HA, SLEN, HA)).then_inc(newa_set, 1)
            pool.wait_ge(newa_set, H)
            pool.dma_start(conva_out, new_a[:, :, :, :]).then_inc(out_a, 16)
            pool.wait_ge(g_out, 16 * (6 * KD + 1))
            pool.wait_ge(out_a, 16)
            pool.wait_ge(bl_done, H)
            for j in range(2):
                pool.dma_start(HID[:, j, :], g_dram[2 * j]).then_inc(g_in[j], 16)
                pool.dma_start(sig[:, j, :], g_dram[2 * j + 1]).then_inc(g_in[j], 16)
            with pool.Fori(0, KD // 2 - 1) as i:
                for q in range(2):
                    pool.wait_ge(m_done, 2 * i + (q + 1))
                    pool.dma_start(HID[:, ds(2 * i + (q + 2), 1), :].rearrange("p n t -> p (n t)"),
                                   g_dram[ds(4 * i + (2 * q + 4), 1)].rearrange("n p c -> (n p) c")).then_inc(g_in[q], 16)
                    pool.dma_start(sig[:, q, :], g_dram[ds(4 * i + (2 * q + 5), 1)].rearrange("n p c -> (n p) c")
                                   ).then_inc(g_in[q], 16)
            pool.wait_ge(unit_done, filled(unit_of(B_O - 1)))
            for j in range(KD):
                if j >= 2:
                    pool.wait_ge(free_h, j + 1)
                pool.dma_start(xr[:, j % 2, :], xT[:, j, :]).then_inc(xr_in[j % 2], 16)
            pool.wait_ge(xl_done, 2 * KD)
            pool.dma_start(KEYS[:, :, :], keys).then_inc(keys_in, 16)
            pool.iota(iota_b[:, :], pattern=[[1, TOPK]], base=0, channel_multiplier=0,
                      allow_small_or_imprecise_dtypes=True).then_inc(iota_set, 1)
            for j in range(HP):
                pool.wait_ge(free_w, j + 3)
                pool.dma_start(q_dram[:, j, :], qrow[:, j % 2, :]).then_inc(q_out[j % 2], 16)
            for b in range(2):
                pool.wait_ge(q_out[b], 16 * (HP // 2))
            pool.dma_start(qst[:, :, :], q_dram[:, :, 0:P]).then_inc(qst_in, 16)
            with pool.Fori(0, NT - 1) as i:
                pool.wait_ge(sel_mm, i + 1)
                pool.dma_start(qst[:, :, :], q_dram[:, :, ds(P * i + P, P)]).then_inc(qst_in, 16)
            pool.wait_ge(sel_mm, NT)
            pool.dma_start(qst[:, :, :], q_dram[:, :, T - P:T]).then_inc(qst_in, 16)
            pool.wait_ge(sel_done, NT + 2)
            pool.iota(IOTA[:, :, :], pattern=[[1, NKEYS], [0, WS]], base=0, channel_multiplier=0,
                      allow_small_or_imprecise_dtypes=True).then_inc(iota_set, 1)
            for b in range(2):
                pool.wait_ge(w_out[b], 16 * (NWB // 2 + 1))
            for s in range(4):
                pool.dma_start(VRAW[:, s, :], v_blk[s]).then_inc(v_in[s], 16)
            with pool.Fori(0, 2 * NG - 1) as i:
                for s in range(4):
                    pool.wait_ge(v_lo, 4 * i + (s + 1))
                    pool.dma_start(VRAW[:, s, :], v_blk[ds(4 * i + (4 + s), 1)].rearrange("n p c -> (n p) c")
                                   ).then_inc(v_in[s], 16)
            pool.wait_ge(out_a, 16)

        @block.scalar
        def _(act):
            for k in range(KD):
                if k % 2 == 0:
                    act.wait_ge(in_x[k // 2], 16)
                rms_square(act, HID[:, k, :], k, k % 2, rms_sems["na"], sq)
            split_hi(act, 0, 16, None)
            rms_act(act, rms_sems["na"])
            act.drain().then_inc(free_q, 2)
            norm_act(act, 0)
            act.drain().then_inc(silu_q, 2)
            with act.Fori(0, NQ // 2) as i:
                for r in range(2):
                    split_hi(act, 1 - r, 16 * i + (16 + 16 * r), 2 * i + (r + 1))
                    act.wait_ge(newq_set, 2 * i + (r + 1))
                    act.wait_ge(unit_done, 2 * i + (r + 2))
                    act.activation(pad[:, r, HQ:HQ + 2 * TH].rearrange("p (a b) -> p a b", a=2),
                                   PS[:, 3 * r:3 * r + 2, 0:TH], ACT.Copy)
                    act.activation(pad[:, r, HQ + 2 * TH:HQ + SEQ], PS[:, 3 * r + 2, 0:SEQ - 2 * TH], ACT.Copy)
                    act.activation(
                        pad[:, r, HQ + SEQ:PADQ].rearrange("p (s c) -> p s c", s=NSEQ)[:, :, HQ:HQ + SLEN],
                        PS[:, 3 * r + 2, SEQ - 2 * TH:TH].rearrange("p (s c) -> p s c", s=NSEQ), ACT.Copy
                    ).then_inc(evac_q, 1)
                    act.drain().then_inc(free_q, 1)
                    act.wait_ge(conv_q, 2 * i + (r + 3))
                    act.activation(QKV[:, ds(2 * i + r, 1), 0:SEQ].rearrange("p n t -> p (n t)"),
                                   cy[:, r, 0:SEQ], ACT.Silu)
                    act.activation(QKV[:, ds(2 * i + r, 1), SEQ:T].rearrange("p n (s c) -> p (n s) c", s=NSEQ),
                                   seqs(cy[:, r, :], HQ + SEQ, HQ, 0, SLEN), ACT.Silu).then_inc(silu_q, 1)

            def square(c, row):
                if c >= 2:
                    act.wait_ge(l2_mm, c - 1)
                act.activation(sq2[:, c % 2, :], QKV[:, row, :], ACT.Square).then_inc(l2_sq, 1)

            def factors(g, scale):
                act.wait_ge(l2_mm, H * g + H)
                if g == 2:
                    act.wait_ge(l2_bc, 2 * H)
                act.activation(thirds(rn4[:, g % 2, :]), pset((g + 1) % 2, H), ACT.Ln, scale=scale, bias=EPS).then_inc(l2_ln, 1)
                act.drain()
                act.activation(rn4[:, g % 2, :], rn4[:, g % 2, :], ACT.Exp, scale=-0.5).then_inc(l2_rn, 1)

            split_hi(act, 1, 16 * 7, filled(B_AB - 1))
            act.wait_ge(newq_set, NQ + 2)
            for c in range(2):
                square(c, c)
            act.wait_ge(in_w, 16)
            act.wait_ge(unit_done, filled(B_AB))
            act.activation(thirds(ab[:, 0, :]), pset(0, H), ACT.Abs, bias=SW[0:H, S_DT:S_DT + 1])
            act.activation(thirds(ab[:, 1, :]), pset(0, H), ACT.Relu, bias=SW[0:H, S_DT:S_DT + 1])
            act.activation(thirds(betaT[:, :]), PS[32:32 + H, 0:3, 0:TH], ACT.Sigmoid)
            act.drain().then_inc(free_q, 1)
            for c in range(2, 6):
                square(c, c)
            factors(0, 1.0)
            for c in range(6, 8):
                square(c, c)
            factors(1, 1.0)
            act.activation(ab[:, 2, :], ab[:, 0, :], ACT.Exp, scale=-1.0)
            act.activation(gsc[0:H, 0, 0:1], SW[0:H, S_ALOG:S_ALOG + 1], ACT.Exp)
            act.drain()
            act.activation(ab[:, 2, :], ab[:, 2, :], ACT.Ln, bias=1.0).then_inc(ab_a, 1)

            def dn_exps(u, n, w):
                act.wait_ge(dn_dt, n)
                act.activation(dnh(u, EXPG, w), bank(3 * u, w), ACT.Exp)
                act.activation(ekd[0:w, u, :], PS[0:w, 3 * u + 2, H:2 * H], ACT.Exp)
                act.activation(dnh(u, DT, w, w), dnh(u, DIFF, w, w), ACT.Exp).then_inc(dn_eg, 1)

            def dn_scaled(u, n, w):
                act.wait_ge(dn_e, n)
                for h in range(H):
                    act.activation(dnh(u, VB, P, w)[:, h, :], PS[0:w, 3 * u, h * P:h * P + P], ACT.Copy,
                                   scale=gbt[0:w, u, H + h:H + h + 1])
                    ins = act.activation(dnh(u, KDEC, P, w)[:, h, :], PS[0:w, 6, h * P:h * P + P], ACT.Copy,
                                         scale=ekd[0:w, u, h:h + 1])
                ins.then_inc(dn_g, 1)

            def dn_evac_x(u, n, w):
                act.wait_ge(dn_x, n)
                act.activation(dnh(u, X, w, w), bank(3 * u, w, w), ACT.Copy).then_inc(dn_xs, 1)

            def dn_evac_v(u, n, w):
                act.wait_ge(dn_v, n)
                act.activation(dnh(u, VN, P, w), bank(3 * u + 1, P, w), ACT.Copy).then_inc(dn_vs, 1)

            def dn_evac_o(u, n, w, cols):
                act.wait_ge(dn_o, n)
                act.activation(QKV[:, 0:H, cols], bank(3 * u, w), ACT.Copy).then_inc(dn_os, 1)

            def g_step(i, p):
                if p % 3 != 2:
                    return
                m = p // 3
                act.wait_ge(g_mm, 12 * i + (m + 1))
                act.wait_ge(g_out, 192 * i + 16 * (m + 1))
                act.activation(gst[:, :], PS[:, 7, 0:TH], ACT.Copy).then_inc(g_evac, 1)
                act.wait_ge(g_evac, 12 * i + (m + 2))
                act.dma_start(g_dram[ds(4 * i + m // 3, 1), :, (m % 3) * TH:(m % 3) * TH + TH].rearrange(
                    "n p c -> (n p) c"), gst[:, :]).then_inc(g_out, 16)
                if m % 3 == 0:
                    nxt = B_G + m // 3 + 1
                    split_hi(act, nxt % 2, 32 * i + 16 * (nxt // 2 + 1), None)

            act.drain().then_inc(dn_os, 2)
            act.drain().then_inc(g_evac, 1)
            act.sem_inc(g_out, 16)
            with act.Fori(0, NPAIR) as i:
                for u in range(2):
                    dn_exps(u, 2 * i + (u + 1), P)
                for u in range(2):
                    g_step(i, 2 + u)
                    dn_scaled(u, 2 * i + (u + 1), P)
                for l in range(LEVELS):
                    for u in range(2):
                        g_step(i, 4 + 4 * l + u)
                        dn_evac_x(u, 2 * LEVELS * i + (2 * l + u + 1), P)
                    for u in range(2):
                        g_step(i, 6 + 4 * l + u)
                for u in range(2):
                    g_step(i, 32 + 2 * u)
                    g_step(i, 33 + 2 * u)
                    dn_evac_v(u, 2 * i + (u + 1), P)
                    dn_evac_o(u, 2 * i + (u + 1), P, ds(2 * P * i + P * u, P))
            dn_exps(0, NT + 1, TS)
            dn_scaled(0, NT + 1, TS)
            for l in range(LEVELS_S):
                dn_evac_x(0, NT * LEVELS + l + 1, TS)
            dn_evac_v(0, NT + 1, TS)
            dn_evac_o(0, NT + 1, TS, slice(SEQ, T))
            act.drain()
            act.wait_ge(dn_st, NT + 1 + NSEQ)

            for c in range(2 * H, 3 * H):
                square(c, c - 2 * H)
            factors(2, 1.0 / P)
            for h in range(H):
                n = B_Z + h
                split_hi(act, (n + 1) % 2, 16 * ((n + 1) // 2 + 1), filled(n - 1))
                act.wait_ge(unit_done, filled(n))
                if h >= 2:
                    act.wait_ge(on_done, h - 1)
                if h == 0:
                    act.wait_ge(l2_done, 3 * H)
                act.activation(thirds(zs[:, h % 2, :]), pset(n % 2), ACT.Silu).then_inc(silu_z, 1)
                act.wait_ge(on_done, h + 1)
                act.activation(OH[:, h, :], on[:, h % 2, :], ACT.Copy).then_inc(oh_h, 1)
            for i in range(H):
                for r in range(3):
                    n = B_CONV + 3 * i + r
                    split_hi(act, (n + 1) % 2, 16 * ((n + 1) // 2 + 1), filled(n - 1))
                act.wait_ge(bc_done, i + 1)
                act.activation(BH[:, i, :], bc[:, :], ACT.Copy).then_inc(bh_done, 1)
            with act.Fori(0, KD // 2) as i:
                for q in range(2):
                    nxt = B_Y + q + 1
                    split_hi(act, nxt % 2, 16 * i + 16 * (nxt // 2 + 1), 4 * i + filled(B_Y + 2 * q - 1))
                    act.wait_ge(g_in[q], 32 * i + 32)
                    row = HID[:, ds(2 * i + q, 1), :].rearrange("p n t -> p (n t)")
                    act.activation(row, row, ACT.Sigmoid).then_inc(sig_done, 1)
                    act.activation(sig[:, q, :], sig[:, q, :], ACT.Sigmoid).then_inc(sig_done, 1)
            act.wait_ge(m_done, KD)
            act.wait_ge(unit_done, filled(unit_of(B_O - 1)))
            for k in range(KD):
                act.activation(XH[:, k, :], HID[:, k, :], ACT.Copy).then_inc(mh_done, 1)
            with act.Fori(0, KD // 2) as i:
                for r in range(2):
                    nxt = B_O + r + 1
                    split_hi(act, nxt % 2, 16 * i + 16 * (nxt // 2 + 1),
                             2 * i + filled(unit_of(B_O) + r - 1))
                    act.wait_ge(free_h, 2 * i + (r + 3))
                    rms_square(act, HID[:, ds(2 * i + r, 1), :].rearrange("p n t -> p (n t)"), 2 * i + r, r,
                               rms_sems["nb"], sqb)
            rms_act(act, rms_sems["nb"])
            act.drain().then_inc(free_w, 2)
            norm_act(act, KD)
            for j in range(HP):
                n = B_WQ + j
                if n + 1 < NBLK:
                    split_hi(act, (n + 1) % 2, 16 * ((n + 1) // 2 + 1), filled(unit_of(n - 1)))
                if j >= 2:
                    act.wait_ge(q_out[j % 2], 16 * (j // 2))
                act.wait_ge(unit_done, filled(unit_of(n)))
                act.activation(thirds(qrow[:, j % 2, :]), pset(n % 2), ACT.Copy).then_inc(free_w, 1)

            def e_split(slot, used, reads):
                act.wait_ge(e_in[slot], reads)
                act.wait_ge(e_mm, used)
                act.activation(WH[:, slot, :], RAW[:, slot, :], ACT.Copy).then_inc(e_hi, 1)

            def e_block(n, slot, reads, more=True):
                if more:
                    e_split(1 - slot, n + 2, reads + 16 * slot)
                act.wait_ge(e_out[slot], reads)
                act.wait_ge(e_mm, n + 3)
                for t in (1, 2, 0):
                    act.activation(AS[:, slot, t * TH:t * TH + TH], e_bank(slot, t), ACT.Gelu).then_inc(e_gelu, 1)

            def sel_scores():
                act.activation(sc[:, :, :].rearrange("p (b n) k -> p b (n k)", b=4), PS[:, 0:4, :],
                               ACT.Copy).then_inc(sel_sc, 1)

            act.drain().then_inc(e_gelu, 3)
            act.wait_ge(unit_done, filled(unit_of(NBLK - 1)))
            e_split(0, 2, 16)
            e_block(0, 0, 16)
            act.wait_ge(sel_mm, 1)
            sel_scores()
            e_block(1, 1, 16)

            def sel_act(i, last):
                for r in range(SEL_E):
                    e_block(SEL_E * i + (PRE + r), r % 2, 8 * SEL_E * i + 16 * ((PRE + r) // 2 + 1))
                    if r == 0 and not last:
                        act.wait_ge(sel_mm, i + 2)
                        act.wait_ge(sel_read, i + 1)
                        sel_scores()
                    if r == 2:
                        act.wait_ge(sel_b, i + 1)
                        act.activation(gate[:, :], gate[:, :], ACT.Exp).then_inc(sel_e, 1)

            with act.Fori(0, NT) as i:
                sel_act(i, False)
            sel_act(NT, True)

            act.drain().then_inc(w_evac, 2)
            for b in range(2):
                act.sem_inc(w_out[b], 16)
            with act.Fori(0, NWB // 2) as i:
                for b in range(2):
                    act.wait_ge(w_out[b], 16 * i + 16)
                    for s in range(WT // WS):
                        act.wait_ge(w_mm, 12 * i + (6 * b + s + 3))
                        act.activation(stg[:, b, :, s * WS:s * WS + WS, :].rearrange("p q t j -> p t q j"),
                                       PS[:, 2 * (s % 2):2 * (s % 2) + 2, :].rearrange(
                                           "p b (t q j) -> p (b t) q j", t=4, j=GE), ACT.Copy, scale=1.0 / GSCALE
                                       ).then_inc(w_evac, 1)
                        if s == 1:
                            e_split(1 - b, WM_E * i + (E0 + b + 2), 16 * i + 8 * (E0 + 2) + 16 * b)
                    act.wait_ge(w_evac, 12 * i + (6 * b + 8))
                    act.dma_start(w_dram[:, :, ds(2 * WT * i + WT * b, WT), :].rearrange("q p t j -> p q (t j)"),
                                  stg[:, b, :, :, :].rearrange("p q t j -> p q (t j)")).then_inc(w_out[b], 16)
                    e_block(WM_E * i + (E0 + b), b, 16 * i + 8 * (E0 + 2), False)
            for n in range(E0 + WM_E * (NWB // 2), NE):
                e_block(n, n % 2, 16 * (n // 2 + 1), n + 1 < NE)

            def u_split(slot, reads, used=None):
                act.wait_ge(u_in[slot], reads)
                if used is not None:
                    act.wait_ge(u_mm, used)
                act.activation(WH[:, slot, :], RAW[:, slot, :], ACT.Copy).then_inc(u_hi, 1)

            def v_split(d, reads, before):
                act.wait_ge(v_in[d % 4], reads)
                act.wait_ge(v_mm, before)
                act.activation(VH[:, d % 2, :], VRAW[:, d % 4, :], ACT.Copy).then_inc(v_hi, 1)

            act.wait_ge(e_mm, NE + 2)
            u_split(0, 16)
            u_split(1, 16)

            def group_act(g, last):
                act.wait_ge(v_mm, 8 * g + 2)
                for e in range(EARLY):
                    act.wait_ge(s_mul, 2 * g + (e + 1))
                    act.activation(AH[:, e, :], AS[:, e, :], ACT.Copy).then_inc(s_hi, 1)
                for d in range(2):
                    v_split(d, 32 * g + 16, 8 * g + (d + 1))
                for c in range(LATE):
                    act.wait_ge(u_mm, 2 * g + (c + 1))
                    act.activation(thirds(AF[:, EARLY + c, :]), pset(c), ACT.Gelu).then_inc(a_gelu, 1)
                    if c == 0 and not last:
                        u_split(0, 16 * g + 32, 2 * g + 1)
                    act.wait_ge(a_mul, 2 * g + (c + 1))
                    act.activation(AH[:, EARLY + c, :], AF[:, EARLY + c, :], ACT.Copy).then_inc(a_hi, 1)
                if not last:
                    u_split(1, 16 * g + 32, 2 * g + 2)
                for d in range(2, 8):
                    v_split(d, 32 * g + 16 * (d // 4 + 1), 8 * g + (d + 1))
                    if last:
                        last_square(d - 2)

            def last_square(d):
                act.wait_ge(acc_done, 8 * (NG - 1) + d + 3)
                rms_square(act, HID[:, d, :], d, d % 2, rms_sems["nc"], sqc)

            with act.Fori(0, NG - 1) as g:
                group_act(g, False)
            group_act(NG - 1, True)
            for d in (6, 7):
                last_square(d)
            rms_act(act, rms_sems["nc"])

        @block.tensor
        def _(pe):
            pe.drain().then_inc(unit_done, 1)
            pe.wait_ge(in_c, 16)
            rms_pe(pe, rms_sems["na"], rn)
            pe.wait_ge(rms_sems["na"]["rn"], 1)
            with pe.Fori(0, NQ // 2) as i:
                for r in range(2):
                    pe.wait_ge(lo_done, 2 * i + (r + 1))
                    pe.wait_ge(free_q, 2 * i + (r + 1))
                    products(pe, r, r, XH, XL, ready=(xl_done, 0) if r == 0 else None).then_inc(unit_done, 1)
            pe.wait_ge(lo_done, B_AB + 1)
            pe.wait_ge(free_q, B_AB + 1)
            products(pe, 0, 0, XH, XL).then_inc(unit_done, 1)

            def sums(g):
                for c in range(H):
                    pe.wait_ge(l2_sq, H * g + c + 1)
                    first = CONST_AT["seqcol"][0] + 3 * TS + 4 * (3 - c)
                    for t in range(3):
                        mm = pe.matmul(PS[0:H, 3 * ((g + 1) % 2) + t, 0:TH], C[:, first:first + 16:4],
                                       sq2[:, c % 2, t * TH:t * TH + TH], start=c == 0, stop=c == H - 1)
                    mm.then_inc(l2_mm, 1)

            def spread(g):
                pe.wait_ge(l2_rn, g + 1)
                for c in range(H * g, H * g + H):
                    if c == 1:
                        pe.wait_ge(l2_ln, 2)
                    if c >= 2:
                        pe.wait_ge(l2_done, c - 1)
                    h = c % H
                    for t in range(3):
                        mm = pe.matmul(PS[:, 3 * ((c + 1) % 2) + t, 0:TH], const("sel", H)[:, h * P:h * P + P],
                                       rn4[:, g % 2, t * TH:t * TH + TH], start=True, stop=True)
                    mm.then_inc(l2_bc, 1)

            pe.wait_ge(free_q, NQ + 2)
            sums(0)
            pe.wait_ge(free_q, NQ + 3)
            sums(1)
            spread(0)
            spread(1)
            pe.wait_ge(ab_v, 1)
            for t in range(NT + 1):
                w = P if t < NT else TS
                for k, src in enumerate((ab[:, 3, :], betaT[:, :])):
                    mm = pe.matmul(PS[0:w, 6, 8 * t + H * k:8 * t + H * k + H], src[:, t * P:t * P + w],
                                   C[0:H, 0:H], start=True, stop=True)
            mm.then_inc(ab_p, 1)

            def mm4(out, lhs, rhs, start=True, stop=True):
                for h in range(H):
                    ins = pe.matmul(out(h), lhs(h), rhs(h), start=start, stop=stop)
                return ins

            def dn_cum(u, n, w, cols, sfx):
                upto, after = const("upto" + sfx, w)[:, 0:w], const("after" + sfx, w)[:, 0:w]
                pe.wait_ge(dn_in, n)
                pe.wait_ge(dn_os, n)
                mm4(lambda h: bank(3 * u, w)[:, h, :], lambda h: dnh(u, GBC, P, w)[:, h, :], lambda h: upto)
                mm4(lambda h: bank(3 * u + 1, w)[:, h, :], lambda h: const("sel", H)[:, h * P:h * P + P],
                    lambda h: betaT[:, cols])
                pe.matmul(PS[0:w, 3 * u + 2, 0:H], upto, gbt[0:w, u, 0:H], start=True, stop=True)
                pe.matmul(PS[0:w, 3 * u + 2, H:2 * H], after, gbt[0:w, u, 0:H], start=True, stop=True
                          ).then_inc(dn_bc, 1)

            STEP = 8

            def g_step(i, p):
                third, part = divmod(p, 3)
                b, t = divmod(third, 3)
                slot = (B_G + b) % 2
                if t == 0 and part == 0:
                    pe.wait_ge(lo_done, 4 * i + (B_G + b + 1))
                if part == 0:
                    pe.wait_ge(g_evac, 12 * i + (third + 1))
                for n in range(STEP * part, STEP * part + STEP):
                    k, v = divmod(n, 3)
                    w, x = ((WH, XH), (WH, XL), (WL, XH))[v]
                    mm = pe.matmul(PS[:, 7, 0:TH], w[:, slot, k * P:k * P + P], x[:, k, t * TH:t * TH + TH],
                                   start=n == 0, stop=n == 3 * KD - 1)
                if part == 2:
                    mm.then_inc(g_mm, 1)

            def dn_pairs(u, n, w, cols):
                pe.wait_ge(dn_d, n)
                kst = dnh(u, KST, w)
                mm4(lambda h: bank(3 * u + 1, w, w)[:, h, :], lambda h: kst[:, h, :], lambda h: dnh(u, KB, w)[:, h, :])
                mm4(lambda h: bank(3 * u + 2, w, w)[:, h, :], lambda h: kst[:, h, :], lambda h: QKV[:, h, cols])
                mm4(lambda h: bank(3 * u, P, w)[:, h, :], lambda h: dnh(u, VST, w)[:, h, :], lambda h: const("ident"))
                if u == 0:
                    pe.wait_ge(dn_st, n)
                else:
                    pe.wait_ge(dn_g, n - 1)
                mm4(lambda h: bank(6, P, w)[:, h, :], lambda h: kst[:, h, :], lambda h: const("ident")
                    ).then_inc(dn_e, 1)

            def dn_level_x(u, w, ready, g):
                pe.wait_ge(dn_t, ready)
                if g is not None:
                    pe.wait_ge(dn_g, g)
                mm4(lambda h: bank(3 * u, w, w)[:, h, :], lambda h: dnh(u, BT, w, w)[:, h, :],
                    lambda h: dnh(u, TM, w, w)[:, h, :]).then_inc(dn_x, 1)

            def dn_level_t(u, w, n, last):
                pe.wait_ge(dn_xs, n)
                x, tt = dnh(u, X, w, w), dnh(u, TTR, w, w)
                if not last:
                    mm4(lambda h: bank(3 * u + 1, w, w)[:, h, :], lambda h: tt[:, h, :], lambda h: x[:, h, :])
                mm4(lambda h: bank(3 * u + 2, w, w)[:, h, :], lambda h: x[:, h, :], lambda h: tt[:, h, :]
                    ).then_inc(dn_tt, 1)

            pe.wait_ge(ab_t, 1)
            with pe.Fori(0, NPAIR) as i:
                for u in range(2):
                    g_step(i, u)
                    dn_cum(u, 2 * i + (u + 1), P, ds(2 * P * i + P * u, P), "")
                for u in range(2):
                    g_step(i, 2 + u)
                    dn_pairs(u, 2 * i + (u + 1), P, ds(2 * P * i + P * u, P))
                for l in range(LEVELS):
                    for u in range(2):
                        g_step(i, 4 + 4 * l + u)
                        dn_level_x(u, P, 2 * (LEVELS + 1) * i + (2 * l + u + 1), 2 * i + (u + 1) if l == 0 else None)
                    for u in range(2):
                        g_step(i, 6 + 4 * l + u)
                        dn_level_t(u, P, 2 * LEVELS * i + (2 * l + u + 1), l == LEVELS - 1)
                for u in range(2):
                    g_step(i, 32 + 2 * u)
                    pe.wait_ge(dn_st, 2 * i + (u + 1))
                    mm4(lambda h: bank(6)[:, h, :], lambda h: dnh(u, KBG)[:, h, :], lambda h: S[:, h, :]).then_inc(dn_ks, 1)
                    g_step(i, 33 + 2 * u)
                    pe.wait_ge(dn_r, 2 * i + (u + 1))
                    mm4(lambda h: bank(3 * u + 1)[:, h, :], lambda h: dnh(u, TTR)[:, h, :], lambda h: dnh(u, RES)[:, h, :]
                        ).then_inc(dn_v, 1)
                    pe.wait_ge(dn_vs, 2 * i + (u + 1))
                    for h in range(H):
                        pe.matmul(bank(3 * u)[:, h, :], S[:, h, :], dnh(u, QD)[:, h, :], start=True, stop=False)
                        mm = pe.matmul(bank(3 * u)[:, h, :], dnh(u, VN)[:, h, :], dnh(u, QKT)[:, h, :], start=False, stop=True)
                    mm.then_inc(dn_o, 1)
                    mm4(lambda h: bank(6)[:, h, :], lambda h: dnh(u, KDEC)[:, h, :], lambda h: dnh(u, VN)[:, h, :]).then_inc(dn_ds, 1)
            pe.wait_ge(g_evac, 6 * KD + 1)
            pe.drain().then_inc(unit_done, 2 * KD)
            dn_cum(0, NT + 1, TS, slice(SEQ, T), "_s")
            dn_pairs(0, NT + 1, TS, slice(SEQ, T))
            for l in range(LEVELS_S):
                dn_level_x(0, TS, NT * (LEVELS + 1) + l + 1, NT + 1 if l == 0 else None)
                dn_level_t(0, TS, NT * LEVELS + l + 1, l == LEVELS_S - 1)
            pe.wait_ge(dn_m, 1)
            pe.wait_ge(state_in, 16)
            for h in range(H):
                for s in range(NSEQ):
                    mm = pe.matmul(PS[0:TS, 6, h * P:h * P + P], kbgm[:, h, s, :], SS[:, s, h, :],
                                   start=s == 0, stop=s == NSEQ - 1)
            mm.then_inc(dn_ks, 1)
            pe.wait_ge(dn_r, NT + 1)
            mm4(lambda h: bank(1, P, TS)[:, h, :], lambda h: dnh(0, TTR, TS, TS)[:, h, :],
                lambda h: dnh(0, RES, P, TS)[:, h, :]).then_inc(dn_v, 1)
            pe.wait_ge(dn_vs, NT + 1)
            for h in range(H):
                for s in range(NSEQ):
                    pe.matmul(bank(0, TS)[:, h, :], SS[:, s, h, :], qdm[:, h, s, :], start=s == 0, stop=False)
                mm = pe.matmul(bank(0, TS)[:, h, :], dnh(0, VN, P, TS)[:, h, :], dnh(0, QKT, TS, TS)[:, h, :],
                               start=False, stop=True)
            mm.then_inc(dn_o, 1)
            for s in range(NSEQ):
                pe.wait_ge(dn_vm, s + 1)
                if s >= 2:
                    pe.wait_ge(dn_st, NT + 1 + s - 1)
                vm = dnh(0, (TM, TTR)[s % 2], P, TS)
                mm4(lambda h: bank(6 + s % 2)[:, h, :], lambda h: dnh(0, KDEC, P, TS)[:, h, :],
                    lambda h: vm[:, h, :]).then_inc(dn_ds, 1)

            pe.wait_ge(dn_st, NT + 1 + NSEQ)
            sums(2)
            spread(2)
            with pe.Fori(0, (B_Y - B_Z) // 2) as i:
                for r in range(2):
                    pe.wait_ge(lo_done, 2 * i + (B_Z + r + 1))
                    pe.wait_ge(free_c, 2 * i + (r + 1))
                    products(pe, 1 - r, 1 - r, XH, XL).then_inc(unit_done, 1)
            pe.wait_ge(ol_done, H)
            pe.wait_ge(bl_done, H)
            with pe.Fori(0, KD // 2) as i:
                for q in range(2):
                    pe.wait_ge(lo_done, 2 * i + (B_Y + q + 1))
                    pe.wait_ge(y_read, 4 * i + (2 * q + 1))
                    products(pe, (1 + q) % 2, 1, BH, BL, range(0, H)).then_inc(unit_done, 1)
                    pe.wait_ge(y_read, 4 * i + (2 * q + 2))
                    products(pe, (1 + q) % 2, 0, OH, OL, range(H, KD), H).then_inc(unit_done, 1)
            with pe.Fori(0, KD // 2) as i:
                for r in range(2):
                    pe.wait_ge(lo_done, 2 * i + (B_O + r + 1))
                    pe.wait_ge(free_h, 2 * i + (r + 1))
                    products(pe, 1 - r, 1 - r, XH, XL, ready=(ml_done, 0) if r == 0 else None).then_inc(unit_done, 1)
            pe.wait_ge(free_h, KD + 2)
            rms_pe(pe, rms_sems["nb"], rn)
            pe.wait_ge(rms_sems["nb"]["rn"], 1)
            with pe.Fori(0, HP // 2) as i:
                for r in range(2):
                    pe.wait_ge(lo_done, 2 * i + (B_WQ + r + 1))
                    pe.wait_ge(free_w, 2 * i + (r + 1))
                    products(pe, 1 - r, 1 - r, XH, XL, ready=(xl_done, KD) if r == 0 else None).then_inc(unit_done, 1)

            def sel_scores(n):
                pe.wait_ge(qst_in, 16 * n + 16)
                for h in range(HP):
                    mm = pe.matmul(PS[:, h // 2, (h % 2) * 256:(h % 2) * 256 + 256], qst[:, h, :],
                                   KEYS[:, h, :], start=True, stop=True)
                mm.then_inc(sel_mm, 1)

            STEPS = [(0, p, t) for t in range(3) for p in range(3)] + [
                (k, p, t) for k in range(1, KD) for p in range(3) for t in range(3)]

            def e_block(n, slot, first=0, last=len(STEPS)):
                for at_step in range(first, last):
                    k, p, t = STEPS[at_step]
                    if at_step == 0:
                        pe.wait_ge(e_lo, n + 1)
                    if k == 0 and p == 0 and t > 0:
                        pe.wait_ge(e_gelu, 3 * n + t)
                    w, x = ((WH, XH), (WH, XL), (WL, XH))[p]
                    mm = pe.matmul(e_bank(slot, t), w[:, slot, k * P:k * P + P], x[:, k, t * TH:t * TH + TH],
                                   start=(k == 0 and p == 0), stop=(k == KD - 1 and p == 2))
                if last == len(STEPS):
                    mm.then_inc(e_mm, 1)

            def sel_pe(i, last):
                for r in range(SEL_E):
                    e_block(SEL_E * i + (PRE + r), r % 2)
                    if r == 0 and not last:
                        pe.wait_ge(sel_sc, i + 1)
                        pe.wait_ge(sel_done, i + 1)
                        sel_scores(i + 1)
                if not last:
                    pe.wait_ge(sel_sc, i + 2)
                pe.wait_ge(sel_g, i + 1)
                for k, x in enumerate((e1, e2, gate)):
                    mm = pe.matmul(PS[:, 0, k * P:k * P + P], x[:, :], const("ident"), start=True, stop=True)
                mm.then_inc(sel_t, 1)

            pe.wait_ge(free_w, HP + 2)
            pe.drain().then_inc(e_mm, 2)
            e_block(0, 0)
            pe.wait_ge(keys_in, 16)
            sel_scores(0)
            e_block(1, 1)
            with pe.Fori(0, NT) as i:
                sel_pe(i, False)
            sel_pe(NT, True)

            pe.wait_ge(sel_done, NT + 2)
            pe.drain().then_inc(w_mm, 2)
            parts = 2 * WT // WS
            each = len(STEPS) * WM_E // parts
            with pe.Fori(0, NWB // 2) as i:
                for s in range(parts):
                    pe.wait_ge(w_hot, 12 * i + (s + 1))
                    pe.wait_ge(w_evac, 12 * i + (s + 1))
                    for t in range(WS):
                        for k in range(2):
                            mm = pe.matmul(PS[:, 2 * (s % 2) + t // 4, (t % 4) * P:(t % 4) * P + P],
                                           HOT1[:, s % 2, :, t], HOTG[:, s % 2, k, :, t], start=k == 0, stop=k == 1)
                    mm.then_inc(w_mm, 1)
                    e, v = divmod(s, parts // WM_E)
                    e_block(WM_E * i + (E0 + e), e, each * v, each * (v + 1))
            for n in range(E0 + WM_E * (NWB // 2), NE):
                e_block(n, n % 2)

            pe.wait_ge(e_gelu, 3 * NE + 3)
            pe.drain().then_inc(v_mm, 2)

            def group_pe(g):
                for c in range(LATE):
                    pe.wait_ge(u_lo, 2 * g + (c + 1))
                    pe.wait_ge(acc_done, 8 * g + (c + 1))
                    products(pe, c, c, XH, XL).then_inc(u_mm, 1)
                order = [(d, c) for cs in (range(GE - 1), (GE - 1,)) for d in range(2) for c in cs]
                order += [(d, c) for d in range(2, 8) for c in range(GE)]
                for d, c in order:
                    if c == 0:
                        pe.wait_ge(v_lo, 8 * g + (d + 1))
                        if d < 2:
                            pe.wait_ge(a_gelu, 2 * g + (d + 1))
                        else:
                            pe.wait_ge(acc_done, 8 * g + (d + 1))
                    if d == 0 and c == 0:
                        pe.wait_ge(s_lo, 2 * g + EARLY)
                    if d == 0 and c >= EARLY:
                        pe.wait_ge(a_lo, 2 * g + (c - EARLY + 1))
                    for n, (w, x) in enumerate(((VH, AH), (VH, AL), (VL, AH))):
                        for t in range(3):
                            mm = pe.matmul(PS[:, 3 * (d % 2) + t, 0:TH], w[:, d % 2, c * P:c * P + P],
                                           x[:, c, t * TH:t * TH + TH],
                                           start=(c == 0 and n == 0), stop=(c == GE - 1 and n == 2))
                    if c == GE - 1:
                        mm.then_inc(v_mm, 1)

            with pe.Fori(0, NG) as g:
                group_pe(g)
            pe.wait_ge(acc_done, 8 * NG + 1)
            rms_pe(pe, rms_sems["nc"], totc)

        @block.vector
        def _(dve):
            def norm(src, r, col, base):
                dve.wait_ge(r["rn"], 1)

                def low(k):
                    dve.wait_ge(xh_done, base + k + 1)
                    dve.tensor_tensor(XL[:, k, :], xt[:, k % 2, :], XH[:, k, :].bitcast(F32),
                                      ALU.subtract).then_inc(xl_done, 1)

                for k in range(KD):
                    if k >= 2:
                        dve.drain()
                    dve.scalar_tensor_tensor(out=xt[:, k % 2, :], in0=src[:, k, :],
                                             scalar=SW[:, col + k:col + k + 1], in1=rn[:, :],
                                             op0=ALU.mult, op1=ALU.mult).then_inc(xt_done, 1)
                    if k >= 1:
                        low(k - 1)
                low(KD - 1)

            rms_zero(dve, rms_sems["na"], rn)
            for k in range(KD):
                rms_add(dve, k, k % 2, rms_sems["na"], sq, rn)
            split_lo(dve, 1, 0)
            dve.wait_ge(in_w, 16)
            norm(HID, rms_sems["na"], S_MIX, 0)
            dve.drain().then_inc(conv_q, 2)
            dve.wait_ge(zeroed, 1)
            LQ = PADQ - HQ
            with dve.Fori(0, NQ // 2) as i:
                for r in range(2):
                    split_lo(dve, 2 * i + (r + 2), 1 - r)
                    dve.wait_ge(hist_set, 2 * i + (r + 1))
                    dve.wait_ge(silu_q, 2 * i + (r + 1))
                    dve.wait_ge(evac_q, 2 * i + (r + 1))
                    for t in range(HQ + 1):
                        weight = SW[:, ds(8 * i + (S_CQ + 4 * r + t), 1)]
                        if t == 0:
                            dve.tensor_scalar(cy[:, r, 0:LQ], pad[:, r, 0:LQ], weight, None, ALU.mult)
                        else:
                            dve.drain()
                            ins = dve.scalar_tensor_tensor(out=cy[:, r, 0:LQ], in0=pad[:, r, t:t + LQ], scalar=weight,
                                                           in1=cy[:, r, 0:LQ], op0=ALU.mult, op1=ALU.add)
                    ins.then_inc(conv_q, 1)
            split_lo(dve, B_AB + 2, 1)
            def norms(g, weight):
                for c in range(H * g, H * g + H):
                    row = thirds(QKV[:, c % (2 * H), :])
                    dve.wait_ge(l2_bc, c + 1)
                    dve.scalar_tensor_tensor(out=row, in0=pset((c + 1) % 2), scalar=weight, in1=row,
                                             op0=ALU.mult, op1=ALU.mult).then_inc(l2_done, 1)

            norms(0, float(P) ** -0.5)
            norms(1, 1.0)
            dve.wait_ge(ab_a, 1)
            dve.tensor_tensor(ab[:, 3, :], ab[:, 1, :], ab[:, 2, :], ALU.add)
            dve.drain()
            dve.tensor_scalar(ab[:, 3, :], ab[:, 3, :], gsc[0:H, 0, 0:1], -1.0, ALU.mult, ALU.mult).then_inc(ab_v, 1)
            dve.wait_ge(ab_p, 1)
            dve.tensor_copy(gb_tok[:, 0:NT, :].rearrange("p t c -> p (t c)"), PS[:, 6, 0:8 * NT])
            dve.tensor_copy(gb_tok[0:TS, NT, :], PS[0:TS, 6, 8 * NT:8 * NT + 8]).then_inc(ab_t, 1)

            dve.drain()

            def dn_inputs(u, w, cols, tile):
                dve.tensor_copy(dnh(u, KST, w), QKV[:, H:2 * H, cols])
                dve.tensor_copy(dnh(u, VST, w), QKV[:, 2 * H:3 * H, cols])
                dve.tensor_copy(gbt[0:w, u, :], tile)
                dve.tensor_copy(dnh(u, GBC, P, w), tile[:, 0:H].unsqueeze(2).broadcast_to([w, H, P])).then_inc(dn_in, 1)

            def dn_diff(u, n, w, sfx):
                dve.wait_ge(dn_bc, n)
                dve.tensor_copy(gsc[0:w, u, :], PS[0:w, 3 * u + 2, 0:H])
                dve.tensor_tensor(dnh(u, KB, w), dnh(u, KST, w), bank(3 * u + 1, w), ALU.mult)
                dve.drain()
                for h in range(H):
                    ins = dve.scalar_tensor_tensor(
                        out=dnh(u, DIFF, w, w)[:, h, :], in0=bank(3 * u, w, w)[:, h, :], scalar=gsc[0:w, u, h:h + 1],
                        in1=const("neg" + sfx, w)[:, 0:w], op0=ALU.subtract, op1=ALU.add)
                ins.then_inc(dn_dt, 1)

            def dn_decay(u, n, w, cols):
                dve.wait_ge(dn_eg, n)
                dve.tensor_tensor(dnh(u, KBG, w), dnh(u, KB, w), dnh(u, EXPG, w), ALU.mult)
                dve.tensor_tensor(dnh(u, QD, w), QKV[:, 0:H, cols], dnh(u, EXPG, w), ALU.mult).then_inc(dn_d, 1)

            def mask(l, w, sfx):
                return const(f"mask{l}{sfx}", w)[:, 0:w].unsqueeze(1).broadcast_to([w, H, w])

            def dn_start(u, n, w, sfx):
                dve.wait_ge(dn_e, n)
                dve.tensor_tensor(dnh(u, MT, w, w), bank(3 * u + 1, w, w), dnh(u, DT, w, w), ALU.mult)
                dve.tensor_tensor(dnh(u, QKT, w, w), bank(3 * u + 2, w, w), dnh(u, DT, w, w), ALU.mult)
                dve.drain()
                unit = const("ident", w)[:, 0:w].unsqueeze(1).broadcast_to([w, H, w])
                dve.tensor_copy(dnh(u, TM, w, w), unit)
                dve.tensor_copy(dnh(u, TTR, w, w), unit)
                dve.tensor_tensor(dnh(u, BT, w, w), dnh(u, MT, w, w), mask(0, w, sfx), ALU.mult).then_inc(dn_t, 1)

            def dn_update(u, n, w, l, last, sfx):
                dve.wait_ge(dn_tt, n)
                if not last:
                    dve.tensor_tensor(dnh(u, TM, w, w), dnh(u, TM, w, w), bank(3 * u + 1, w, w), ALU.subtract)
                    dve.tensor_tensor(dnh(u, BT, w, w), dnh(u, MT, w, w), mask(l + 1, w, sfx), ALU.mult)
                dve.tensor_tensor(dnh(u, TTR, w, w), dnh(u, TTR, w, w), bank(3 * u + 2, w, w), ALU.subtract
                                  ).then_inc(dn_t, 1)

            def dn_residual(u, n, w, g):
                dve.wait_ge(dn_g, g)
                dve.wait_ge(dn_ks, n)
                dve.tensor_tensor(dnh(u, RES, P, w), dnh(u, VB, P, w), bank(6, P, w), ALU.subtract).then_inc(dn_r, 1)

            dve.wait_ge(out_q, 16)
            dve.memset(S[:, :, :], 0.0).then_inc(dn_st, 1)
            with dve.Fori(0, NPAIR) as i:
                dve.drain()
                for u in range(2):
                    dn_inputs(u, P, ds(2 * P * i + P * u, P), gb_tok[:, ds(2 * i + u, 1), :].rearrange("p n c -> p (n c)"))
                for u in range(2):
                    dn_diff(u, 2 * i + (u + 1), P, "")
                for u in range(2):
                    dn_decay(u, 2 * i + (u + 1), P, ds(2 * P * i + P * u, P))
                for u in range(2):
                    dn_start(u, 2 * i + (u + 1), P, "")

                def g_low(b):
                    split_lo(dve, 4 * i + (B_G + b + 2), (B_G + b + 1) % 2)

                g_low(0)
                for l in range(LEVELS):
                    for u in range(2):
                        dn_update(u, 2 * LEVELS * i + (2 * l + u + 1), P, l, l == LEVELS - 1, "")
                    if l in (2, 4, 6):
                        g_low(l // 2)
                for u in range(2):
                    dn_residual(u, 2 * i + (u + 1), P, 2 * i + 2)
                    dve.wait_ge(dn_ds, 2 * i + (u + 1))
                    for h in range(H):
                        ins = dve.scalar_tensor_tensor(out=S[:, h, :], in0=S[:, h, :], scalar=dnh(u, EXPG)[:, h, P - 1:P],
                                                       in1=bank(6)[:, h, :], op0=ALU.mult, op1=ALU.add)
                    ins.then_inc(dn_st, 1)
            dve.drain()
            dn_inputs(0, TS, slice(SEQ, T), gb_tok[0:TS, NT, :])
            dn_diff(0, NT + 1, TS, "_s")
            dn_decay(0, NT + 1, TS, slice(SEQ, T))
            dve.drain()
            seqcol = const("seqcol").rearrange("p (s c) -> p s c", s=NSEQ)
            for src, dst in ((KBG, kbgm), (QD, qdm)):
                for h in range(H):
                    ins = dve.tensor_tensor(dst[:, h, :, :], dnh(0, src, TS)[:, h, :].unsqueeze(1).broadcast_to([P, NSEQ, TS]),
                                            seqcol, ALU.mult)
            ins.then_inc(dn_m, 1)
            dn_start(0, NT + 1, TS, "_s")
            for l in range(LEVELS_S):
                dn_update(0, NT * LEVELS + l + 1, TS, l, l == LEVELS_S - 1, "_s")
            dn_residual(0, NT + 1, TS, NT + 1)
            dve.wait_ge(dn_vs, NT + 1)
            for s in range(NSEQ + 1):
                if s < NSEQ:
                    if s >= 2:
                        dve.wait_ge(dn_ds, NT + s - 1)
                    dve.tensor_scalar(dnh(0, (TM, TTR)[s % 2], P, TS), dnh(0, VN, P, TS), const("seqrow", TS)[:, s:s + 1],
                                      None, ALU.mult).then_inc(dn_vm, 1)
                if s >= 1:
                    dve.wait_ge(dn_ds, NT + s)
                    for h in range(H):
                        last = SLEN * s - 1
                        ins = dve.scalar_tensor_tensor(
                            out=SS[:, s - 1, h, :], in0=SS[:, s - 1, h, :], scalar=dnh(0, EXPG, TS)[:, h, last:last + 1],
                            in1=bank(6 + (s - 1) % 2)[:, h, :], op0=ALU.mult, op1=ALU.add)
                    ins.then_inc(dn_st, 1)
            norms(2, SW[:, S_DN:S_DN + 1])
            dve.wait_ge(out_s, 32)
            dve.drain().then_inc(free_c, 2)
            for h in range(H):
                n = B_Z + h
                split_lo(dve, n + 2, (n + 1) % 2)
                dve.wait_ge(silu_z, h + 1)
                dve.tensor_tensor(on[:, h % 2, :], QKV[:, h, :], zs[:, h % 2, :], ALU.mult).then_inc(on_done, 1)
                dve.drain().then_inc(free_c, 1)
                dve.wait_ge(oh_h, h + 1)
                dve.tensor_tensor(OL[:, h, :], on[:, h % 2, :], OH[:, h, :].bitcast(F32), ALU.subtract).then_inc(ol_done, 1)
            LA = PADA - HA
            for i in range(H):
                n = B_CONV + 3 * i
                st = n % 2
                split_lo(dve, n + 2, (n + 1) % 2)
                dve.wait_ge(unit_done, filled(n))
                dve.tensor_copy(thirds(cbuf[:, :]), pset(st)).then_inc(free_c, 1)
                split_lo(dve, n + 3, n % 2)
                dve.wait_ge(unit_done, filled(n + 1))
                if i:
                    dve.wait_ge(newa_set, i)
                dve.drain()
                dve.tensor_tensor(pada[:, HA:HA + 2 * TH].rearrange("p (a b) -> p a b", a=2),
                                  PS[:, 3 * (1 - st):3 * (1 - st) + 2, 0:TH],
                                  cbuf[:, 0:2 * TH].rearrange("p (a b) -> p a b", a=2), ALU.mult)
                dve.tensor_tensor(pada[:, HA + 2 * TH:HA + SEQ], PS[:, 3 * (1 - st) + 2, 0:SEQ - 2 * TH],
                                  cbuf[:, 2 * TH:SEQ], ALU.mult)
                dve.tensor_tensor(seqs(pada, HA + SEQ, HA, HA, SLEN),
                                  PS[:, 3 * (1 - st) + 2, SEQ - 2 * TH:TH].rearrange("p (s c) -> p s c", s=NSEQ),
                                  cbuf[:, SEQ:T].rearrange("p (s c) -> p s c", s=NSEQ), ALU.mult).then_inc(free_c, 1)
                split_lo(dve, n + 4, (n + 1) % 2)
                dve.wait_ge(c_hist, i + 1)
                for t in range(HA + 1):
                    weight = SW[:, S_CA + 3 * i + t:S_CA + 3 * i + t + 1]
                    dve.drain()
                    if t == 0:
                        dve.tensor_scalar(ya[:, 0:LA], pada[:, 0:LA], weight, None, ALU.mult)
                    else:
                        ins = dve.scalar_tensor_tensor(out=ya[:, 0:LA], in0=pada[:, t:t + LA], scalar=weight,
                                                       in1=ya[:, 0:LA], op0=ALU.mult, op1=ALU.add)
                ins.then_inc(ya_done, 1)
                dve.wait_ge(unit_done, filled(n + 2))
                dve.drain()
                dve.tensor_tensor(bc[:, 0:2 * TH].rearrange("p (a b) -> p a b", a=2), PS[:, 3 * st:3 * st + 2, 0:TH],
                                  ya[:, 0:2 * TH].rearrange("p (a b) -> p a b", a=2), ALU.mult)
                dve.tensor_tensor(bc[:, 2 * TH:SEQ], PS[:, 3 * st + 2, 0:SEQ - 2 * TH], ya[:, 2 * TH:SEQ], ALU.mult)
                dve.tensor_tensor(bc[:, SEQ:T].rearrange("p (s c) -> p s c", s=NSEQ),
                                  PS[:, 3 * st + 2, SEQ - 2 * TH:TH].rearrange("p (s c) -> p s c", s=NSEQ),
                                  seqs(ya, HA + SEQ, HA, 0, SLEN), ALU.mult).then_inc(bc_done, 1)
                dve.drain().then_inc(free_c, 1)
                dve.wait_ge(bh_done, i + 1)
                dve.tensor_tensor(BL[:, i, :], bc[:, :], BH[:, i, :].bitcast(F32), ALU.subtract).then_inc(bl_done, 1)
            dve.drain().then_inc(y_read, 2)
            with dve.Fori(0, KD // 2) as i:
                for q in range(2):
                    row = thirds(HID[:, ds(2 * i + q, 1), :].rearrange("p n t -> p (n t)"))
                    split_lo(dve, 2 * i + (B_Y + q + 2), (B_Y + q + 1) % 2)
                    dve.wait_ge(unit_done, 4 * i + filled(B_Y + 2 * q))
                    dve.wait_ge(sig_done, 4 * i + (2 * q + 1))
                    dve.tensor_tensor(row, pset(1), row, ALU.mult).then_inc(y_read, 1)
                    dve.wait_ge(unit_done, 4 * i + filled(B_Y + 2 * q + 1))
                    dve.wait_ge(sig_done, 4 * i + (2 * q + 2))
                    dve.tensor_tensor(thirds(sig[:, q, :]), pset(0), thirds(sig[:, q, :]), ALU.mult).then_inc(y_read, 1)
                    dve.drain()
                    dve.tensor_tensor(row, row, thirds(sig[:, q, :]), ALU.add).then_inc(m_done, 1)
            dve.drain().then_inc(free_h, 2)
            for k in range(KD):
                dve.wait_ge(mh_done, k + 1)
                dve.tensor_tensor(XL[:, k, :], HID[:, k, :], XH[:, k, :].bitcast(F32), ALU.subtract).then_inc(ml_done, 1)
            rms_zero(dve, rms_sems["nb"], rn)
            with dve.Fori(0, KD // 2) as i:
                for r in range(2):
                    split_lo(dve, 2 * i + (B_O + r + 2), (B_O + r + 1) % 2)
                    dve.wait_ge(xr_in[r], 16 * i + 16)
                    dve.wait_ge(unit_done, 2 * i + filled(unit_of(B_O) + r))
                    dve.tensor_tensor(thirds(HID[:, ds(2 * i + r, 1), :].rearrange("p n t -> p (n t)")), pset(1 - r),
                                      thirds(xr[:, r, :]), ALU.add).then_inc(free_h, 1)
                    rms_add(dve, 2 * i + r, r, rms_sems["nb"], sqb, rn)
            dve.drain()
            norm(HID, rms_sems["nb"], S_FFN, KD)
            for j in range(HP - 1):
                split_lo(dve, B_WQ + j + 2, (B_WQ + j + 1) % 2)

            def e_low(n, slot):
                dve.wait_ge(e_hi, n + 1)
                dve.tensor_tensor(WL[:, slot, :], RAW[:, slot, :], WH[:, slot, :].bitcast(F32), ALU.subtract).then_inc(e_lo, 1)

            def sel_dve(i, cols):
                w, n = P, i + 1

                def r(x):
                    return x[0:w]
                dve.wait_ge(sel_sc, n)
                dve.tensor_copy(r(tick), r(sc)[:, 0, 0:1])
                for j in range(2 * HP):
                    dve.max(r(best)[:, j, 0:8], r(sc)[:, j, :])
                dve.drain()
                for j in range(2 * HP):
                    dve.match_replace(r(sc2)[:, j, :], r(best)[:, j, 0:8], r(sc)[:, j, :], -3.4e38)
                    dve.max_index(r(besti)[:, j, 0:8], r(best)[:, j, 0:8], r(sc)[:, j, :])
                dve.drain().then_inc(sel_read, 1)
                e_low(SEL_E * i + (PRE + 1), 1)
                for j in range(2 * HP):
                    dve.max(r(best)[:, j, 8:16], r(sc2)[:, j, :])
                dve.drain()
                for j in range(2 * HP):
                    dve.max_index(r(besti)[:, j, 8:16], r(best)[:, j, 8:16], r(sc2)[:, j, :])
                e_low(SEL_E * i + (PRE + 2), 0)
                b2 = r(best).rearrange("p (h s) k -> p h s k", s=2)
                for i0, rows, n_cols in CAND:
                    a = ROW_START[i0]
                    dve.tensor_tensor(
                        r(cand)[:, :, a:a + rows * n_cols].rearrange("p h (i j) -> p h i j", i=rows),
                        b2[:, :, 0, i0:i0 + rows].unsqueeze(3).broadcast_to([w, HP, rows, n_cols]),
                        b2[:, :, 1, 0:n_cols].unsqueeze(2).broadcast_to([w, HP, rows, n_cols]), ALU.add)
                dve.drain()
                dve.tensor_copy(r(bestf), r(besti))
                for h in range(HP):
                    dve.max(r(top)[:, h, 0:8], r(cand)[:, h, :])
                dve.drain()
                for h in range(HP):
                    dve.match_replace(r(cand2)[:, h, :], r(top)[:, h, 0:8], r(cand)[:, h, :], -3.4e38)
                    dve.max_index(r(topi)[:, h, 0:8], r(top)[:, h, 0:8], r(cand)[:, h, :])
                dve.drain()
                for h in range(HP):
                    dve.max(r(top)[:, h, 8:16], r(cand2)[:, h, :])
                dve.drain()
                for h in range(HP):
                    dve.max_index(r(topi)[:, h, 8:16], r(top)[:, h, 8:16], r(cand2)[:, h, :])
                e_low(SEL_E * i + (PRE + 3), 1)
                g3 = r(gate).rearrange("p (h k) -> p h k", h=HP)
                dve.tensor_tensor(g3, r(top), r(top)[:, :, 0:1].broadcast_to([w, HP, TOPK]), ALU.subtract).then_inc(sel_b, 1)
                f2 = r(bestf).rearrange("p (h s) k -> p h s k", s=2)
                dve.tensor_copy(r(delta)[:, :, 0:1], f2[:, :, 0, 0:1])
                dve.tensor_tensor(r(delta)[:, :, 1:TOPK], f2[:, :, 0, 1:TOPK], f2[:, :, 0, 0:TOPK - 1], ALU.subtract)
                dve.drain()
                dve.tensor_copy(r(topf), r(topi))
                dve.drain()

                def over(x):
                    return x.unsqueeze(2).broadcast_to([w, HP, TOPK, TOPK])

                def each(x):
                    return x.unsqueeze(3).broadcast_to([w, HP, TOPK, TOPK])

                def row(x):
                    return x.unsqueeze(1).unsqueeze(1).broadcast_to([w, HP, TOPK, TOPK])

                e1v, e2v = (r(x).rearrange("p (h k) -> p h k", h=HP) for x in (e1, e2))
                dve.tensor_tensor(r(hot), each(r(topf)), row(const("start16", w)), ALU.is_ge)
                dve.drain()
                dve.tensor_tensor(r(pick), r(hot), over(r(delta)), ALU.mult)
                dve.drain()
                dve.tensor_reduce(e1v, r(pick), AX.X, ALU.add)
                dve.drain()
                dve.tensor_tensor(r(pick), r(hot), row(r(dstart)), ALU.mult)
                dve.drain()
                dve.tensor_reduce(e2v, r(pick), AX.X, ALU.add)
                dve.drain()
                dve.tensor_tensor(r(topf), r(topf), e2v, ALU.subtract)
                dve.drain()
                dve.tensor_tensor(r(hot), each(r(topf)), row(const("iota16", w)), ALU.is_equal)
                dve.drain()
                dve.tensor_tensor(r(pick), r(hot), over(f2[:, :, 1, :]), ALU.mult)
                dve.drain()
                dve.tensor_reduce(e2v, r(pick), AX.X, ALU.add)
                dve.wait_ge(sel_e, n)
                dve.tensor_reduce(r(gsum), g3, AX.X, ALU.add)
                dve.drain()
                dve.reciprocal(r(gsum), r(gsum))
                dve.drain()
                dve.tensor_tensor(g3, g3, r(gsum).unsqueeze(2).broadcast_to([w, HP, TOPK]), ALU.mult).then_inc(sel_g, 1)
                e_low(SEL_E * i + (PRE + 4), 0)
                dve.wait_ge(sel_t, n)
                dve.tensor_copy(EG[:, 0, cols], PS[:, 0, 0:w])
                dve.tensor_copy(EG[:, 1, cols], PS[:, 0, P:P + w])
                dve.tensor_scalar(EG[:, 2, cols], PS[:, 0, 2 * P:2 * P + w], GSCALE, None, ALU.mult)
                dve.drain()
                dve.scalar_tensor_tensor(out=EG[:, 3, cols], in0=PS[:, 0, 2 * P:2 * P + w], scalar=GSCALE,
                                         in1=EG[:, 2, cols], op0=ALU.mult, op1=ALU.subtract).then_inc(sel_done, 1)

            dve.wait_ge(iota_set, 1)
            dve.tensor_tensor(dstart[:, 1:TOPK], const("start16")[:, 1:TOPK], const("start16")[:, 0:TOPK - 1], ALU.subtract)
            dve.tensor_copy(dstart[:, 0:1], const("start16")[:, 0:1])
            for n in range(PRE + 1):
                e_low(n, n % 2)
            dve.drain().then_inc(sel_done, 1)
            with dve.Fori(0, NT) as i:
                dve.drain()
                sel_dve(i, ds(P * i, P))
            dve.drain()
            sel_dve(NT, slice(T - P, T))

            dve.drain()
            dve.wait_ge(iota_set, 2)
            with dve.Fori(0, NWB // 2) as i:
                for s in range(2 * WT // WS):
                    cols = ds(2 * WT * i + WS * s, WS)

                    def row(k):
                        return EG[:, k, cols].unsqueeze(1).broadcast_to([P, NKEYS, WS])
                    dve.wait_ge(w_mm, 12 * i + (s + 1))
                    dve.tensor_tensor(HOT2[:, s % 2], IOTA[:, :, :], row(1), ALU.is_equal).then_inc(w_second, 1)
                    dve.tensor_tensor(HOT1[:, s % 2], IOTA[:, :, :], row(0), ALU.is_equal)
                    dve.wait_ge(w_second, 12 * i + (s + 1))
                    for k in range(2):
                        ins = dve.tensor_tensor(HOTG[:, s % 2, k], HOT2[:, s % 2], row(2 + k), ALU.mult)
                    ins.then_inc(w_hot, 1)
                    if s % 6 == 3:
                        e = s // 6
                        e_low(WM_E * i + (E0 + 1 + e), 1 - e)
            for n in range(E0 + WM_E * (NWB // 2) + 1, NE):
                e_low(n, n % 2)

            def u_low(m, slot):
                dve.wait_ge(u_hi, m)
                dve.tensor_tensor(WL[:, slot, :], RAW[:, slot, :], WH[:, slot, :].bitcast(F32), ALU.subtract).then_inc(u_lo, 1)

            def s_gated(g, e):
                if e == 0:
                    dve.wait_ge(gw_in, 16 * g + 16)
                dve.wait_ge(as_in[e], 16 * g + 16)
                dve.tensor_tensor(AS[:, e, :], AS[:, e, :], GW[:, :, e], ALU.mult).then_inc(s_mul, 1)

            def v_low(d, s):
                dve.wait_ge(v_hi, s)
                dve.tensor_tensor(VL[:, d % 2, :], VRAW[:, d % 4, :], VH[:, d % 2, :].bitcast(F32), ALU.subtract).then_inc(v_lo, 1)

            dve.drain().then_inc(acc_done, 2)
            u_low(1, 0)
            u_low(2, 1)
            for e in range(EARLY):
                s_gated(0, e)

            def group_dve(g, last):
                dve.drain()
                for e in range(EARLY):
                    dve.wait_ge(s_hi, 2 * g + (e + 1))
                    dve.tensor_tensor(AL[:, e, :], AS[:, e, :], AH[:, e, :].bitcast(F32), ALU.subtract).then_inc(s_lo, 1)
                for d in range(2):
                    v_low(d, 8 * g + (d + 1))
                for c in range(LATE):
                    k = EARLY + c
                    dve.wait_ge(a_gelu, 2 * g + (c + 1))
                    dve.tensor_tensor(AF[:, k, :], AF[:, k, :], GW[:, :, k], ALU.mult).then_inc(a_mul, 1)
                    dve.wait_ge(a_hi, 2 * g + (c + 1))
                    dve.tensor_tensor(AL[:, k, :], AF[:, k, :], AH[:, k, :].bitcast(F32), ALU.subtract).then_inc(a_lo, 1)
                    if c == 0 and not last:
                        u_low(2 * g + 3, 0)
                if not last:
                    u_low(2 * g + 4, 1)
                for d in range(8):
                    dve.wait_ge(v_mm, 8 * g + (d + 3))
                    dve.tensor_tensor(thirds(HID[:, d, :]), thirds(HID[:, d, :]), pset(d % 2), ALU.add).then_inc(acc_done, 1)
                    if d < 6:
                        v_low(d + 2, 8 * g + (d + 3))
                    if last and d == 0:
                        rms_zero(dve, rms_sems["nc"], totc)
                    if last and d > 0:
                        rms_add(dve, d - 1, (d - 1) % 2, rms_sems["nc"], sqc, totc)
                    if d in (5, 6) and not last:
                        s_gated(g + 1, d - 5)

            with dve.Fori(0, NG - 1) as g:
                group_dve(g, False)
            group_dve(NG - 1, True)
            dve.drain()
            rms_add(dve, 7, 1, rms_sems["nc"], sqc, totc)
            dve.wait_ge(rms_sems["nc"]["rn"], 1)
            for k in range(KD):
                if k >= 2:
                    dve.wait_ge(out_y[k % 2], 16 * (k // 2))
                dve.scalar_tensor_tensor(out=xt[:, k % 2, :], in0=HID[:, k, :], scalar=SW[:, S_FIN + k:S_FIN + k + 1],
                                         in1=rn[:, :], op0=ALU.mult, op1=ALU.mult).then_inc(y_row, 1)


def packed(w):
    k, n = w.shape[0] // P, w.shape[1] // P
    return w.reshape(k, P, n, P).transpose(2, 1, 0, 3)


def kernel(x_prompt, x_sample, state_conv_a, state_conv_qkv, state_delta, g_norm_mix, w_in, w_conv_a,
           w_conv_qkv, a_log, dt_bias, g_dn_norm, w_out_a, w_out_dn, w_o, g_norm_ffn, w_query, sub_keys,
           expert_u, expert_v, g_norm_final):
    import concourse.bacc as bacc
    from concourse.bass_utils import run_bass_kernel_spmd

    def chunks(w, *tail):
        return w.reshape(-1, w.shape[-1] // P, P).transpose(2, 1, 0)

    x = np.concatenate([np.asarray(x_prompt).reshape(SEQ, D), np.asarray(x_sample).reshape(TS, D)])
    w = np.asarray(w_in)[0]
    half, wide = D // 2, H * P
    at = {}
    o = 0
    for name, n in (("b", half), ("c", half), ("h", half), ("qkv", 3 * wide), ("z", wide), ("a", H), ("beta", H),
                    ("ga", D), ("gb", D)):
        at[name] = w[:, o:o + n]
        o += n
    ab = np.zeros((D, P), w.dtype)
    ab[:, 0:H], ab[:, 32:32 + H] = at["a"], at["beta"]
    pk = {n: packed(v) for n, v in at.items() if n not in ("a", "beta")}
    wa, wd = packed(np.asarray(w_out_a)[0]), packed(np.asarray(w_out_dn)[0])
    blocks = [pk["qkv"], packed(ab)]
    for j in range(KD):
        blocks += [pk["ga"][j:j + 1], pk["gb"][j:j + 1]]
    blocks += [pk["z"]]
    for i in range(H):
        blocks += [pk[n][i:i + 1] for n in ("c", "h", "b")]
    blocks += [np.concatenate([wa, wd], axis=2), packed(np.asarray(w_o)[0]), packed(np.asarray(w_query)[0])]
    wall = np.ascontiguousarray(np.concatenate(blocks)).reshape(NBLK, P, D)

    small = np.zeros((P, NSMALL), w.dtype)
    for col, g in ((S_MIX, g_norm_mix), (S_FFN, g_norm_ffn), (S_FIN, g_norm_final)):
        small[:, col:col + KD] = np.asarray(g).reshape(KD, P).T
    small[:, S_CQ:S_CQ + 4 * NQ] = chunks(np.asarray(w_conv_qkv)[0]).reshape(P, 4 * NQ)
    small[:, S_CA:S_CA + 3 * H] = chunks(np.asarray(w_conv_a)[0]).reshape(P, 3 * H)
    small[:, S_DN] = np.asarray(g_dn_norm)[0]
    small[0:H, S_ALOG] = np.asarray(a_log)[0]
    small[0:H, S_DT] = np.asarray(dt_bias)[0]

    sk = np.asarray(sub_keys)[0]
    keys = np.zeros((P, HP, 2 * NKEYS), sk.dtype)
    for p in range(2):
        keys[64 * p:64 * p + 64, :, NKEYS * p:NKEYS * p + NKEYS] = sk[p].transpose(2, 0, 1)

    def history(s):
        n, k, c = s.shape
        return np.ascontiguousarray(s.reshape(n, k, c // P, P).transpose(3, 2, 0, 1))

    second = np.arange(NKEYS).reshape(NG, GE)
    order = np.concatenate([second[:, :EARLY].ravel(), second[:, EARLY:].ravel()])
    arrays = {
        "x_t": np.ascontiguousarray(x.reshape(T, KD, P).transpose(2, 1, 0)),
        "weights": wall,
        "small": small,
        "keys": keys,
        "constants": CONSTANTS,
        "hist_qkv": history(np.asarray(state_conv_qkv)[0]),
        "hist_a": history(np.asarray(state_conv_a)[0]),
        "state": np.ascontiguousarray(np.asarray(state_delta)[0].transpose(2, 0, 1, 3)),
        "experts_u": np.ascontiguousarray(
            np.asarray(expert_u)[0].reshape(NKEYS, NKEYS, KD, P).transpose(1, 3, 2, 0)[order]).reshape(NKEYS, P, D),
        "experts_v": np.ascontiguousarray(
            np.asarray(expert_v)[0].reshape(NKEYS, NG, GE, KD, P).transpose(1, 3, 0, 2, 4)).reshape(NG * KD, P, GE * P),
    }
    outs = {"y_t": (P, KD, T), "new_qkv": (P, NQ, NSEQ + 1, HQ), "new_a": (P, H, NSEQ + 1, HA),
            "state_p": (P, H, P), "state_s": (P, NSEQ, H, P)}
    nc = bacc.Bacc("TRN2", target_bir_lowering=False, num_devices=1)
    ins = [nc.dram_tensor(n, a.shape, F32, kind="ExternalInput").ap() for n, a in arrays.items()]
    got = [nc.dram_tensor(n, s, F32, kind="ExternalOutput").ap() for n, s in outs.items()]
    kept = [nc.dram_tensor(n, s, F32, kind="Internal").ap() for n, s in {
        "gate_matrices": (NG, P, T, GE), "queries": (P, HP, T), "activations": (NE, P, T),
        "merge_gates": (2 * KD, P, T)}.items()]
    program(nc, *ins, *got, *kept)
    res = run_bass_kernel_spmd(nc, [arrays], core_ids=[0]).results[0]

    y = res["y_t"].transpose(2, 1, 0).reshape(T, D)
    new_q = res["new_qkv"].transpose(2, 3, 1, 0).reshape(NSEQ + 1, HQ, NQ * P)
    new_a = res["new_a"].transpose(2, 3, 1, 0).reshape(NSEQ + 1, HA, H * P)
    return (y[:SEQ].reshape(1, SEQ, D), y[SEQ:].reshape(NSEQ, SLEN, D),
            new_a[None, 0:1], new_q[None, 0:1], res["state_p"].transpose(1, 0, 2)[None, None],
            new_a[None, 1:], new_q[None, 1:], res["state_s"].transpose(1, 2, 0, 3)[None])
```
